# Optimizing a Trainium2 kernel written in Bass

```python
import math
import jax, jax.numpy as jnp
from jax import lax
import numpy as np

D_MODEL = 1024
BATCH = 1
SEQ = 256
DEPTH = 2

HEAD_DIM = 64
ROPE_THETA = 10000.0
A_Q_HEADS = 8
A_KV_HEADS = 2
A_WINDOW = 128
A_BLOCK = 128
B_Q_HEADS = 8
B_Q_RANK = 256
B_IDX_HEADS = 8
B_IDX_DIM = HEAD_DIM
B_TOPK_MAX = 256
B_QBLOCK = 128
C_HEADS = 16
C_BLOCK = 256
C_TOPK = 3
C_QCHUNK = 16
D_FF = 4 * D_MODEL
N_EVEN = (DEPTH + 1) // 2
N_ODD = DEPTH // 2
DN_ALPHA = (2 * DEPTH) ** 0.25
DN_BETA = (8 * DEPTH) ** -0.25
LN_EPS = 1e-5
RMS_EPS = 1e-6

AB_WIDTHS = (A_Q_HEADS * HEAD_DIM, A_KV_HEADS * HEAD_DIM, A_KV_HEADS * HEAD_DIM,
             B_Q_RANK, HEAD_DIM, HEAD_DIM, B_IDX_DIM, B_IDX_HEADS)
AB_IN_WIDTH = sum(AB_WIDTHS)
AB_MIX_WIDTH = (A_Q_HEADS + B_Q_HEADS) * HEAD_DIM
C_WIDTH = C_HEADS * HEAD_DIM


def _split_widths(t, widths):
    return jnp.split(t, np.cumsum(widths)[:-1].tolist(), axis=-1)

def layer_norm(x, g, b):
    xf = x.astype(jnp.float32)
    mu = jnp.mean(xf, axis=-1, keepdims=True)
    var = jnp.mean(jnp.square(xf - mu), axis=-1, keepdims=True)
    return ((xf - mu) * lax.rsqrt(var + LN_EPS) * g.astype(jnp.float32) + b.astype(jnp.float32)).astype(x.dtype)

def rms_norm(x, g):
    xf = x.astype(jnp.float32)
    ms = jnp.mean(jnp.square(xf), axis=-1, keepdims=True)
    return (xf * lax.rsqrt(ms + RMS_EPS) * g.astype(jnp.float32)).astype(x.dtype)

def rope_tables(positions):
    inv = ROPE_THETA ** (-jnp.arange(0, HEAD_DIM, 2, dtype=jnp.float32) / HEAD_DIM)
    ang = positions.astype(jnp.float32)[..., None] * inv
    ang = jnp.concatenate([ang, ang], axis=-1)
    return jnp.cos(ang)[:, :, None, :], jnp.sin(ang)[:, :, None, :]

def apply_rope(t, cos, sin):
    t1, t2 = jnp.split(t, 2, axis=-1)
    rot = jnp.concatenate([-t2, t1], axis=-1)
    return (t * cos + rot * sin).astype(t.dtype)

def ada_modulation(c, w, b):
    m = jax.nn.silu(c) @ w + b
    shift, scale, gate = jnp.split(m[:, None, :], 3, axis=-1)
    return shift, scale, 1.0 + gate

def swa_sink_attention(q, k, v, sinks):
    Bn, S, HQ, hd = q.shape
    HKV = k.shape[2]
    G = HQ // HKV
    nb = S // A_BLOCK
    qb = q.reshape(Bn, nb, A_BLOCK, HKV, G, hd)

    def band(t):
        tb = t.reshape(Bn, nb, A_BLOCK, HKV, hd)
        prev = jnp.pad(tb[:, :-1], ((0, 0), (1, 0), (0, 0), (0, 0), (0, 0)))
        return jnp.concatenate([prev, tb], axis=2)

    kb, vb = band(k), band(v)
    s = jnp.einsum('bnqkgd,bnskd->bnkgqs', qb, kb, preferred_element_type=jnp.float32) * (hd ** -0.5)
    qpos = jnp.arange(nb)[:, None, None] * A_BLOCK + jnp.arange(A_BLOCK)[None, :, None]
    kpos = jnp.arange(nb)[:, None, None] * A_BLOCK - A_BLOCK + jnp.arange(2 * A_BLOCK)[None, None, :]
    diff = qpos - kpos
    mask = (diff >= 0) & (diff < A_WINDOW) & (kpos >= 0)
    s = jnp.where(mask[None, :, None, None], s, -jnp.inf)
    sink = jnp.broadcast_to(sinks.astype(jnp.float32).reshape(HKV, G)[None, None, :, :, None, None],
                            s.shape[:-1] + (1,))
    p = jax.nn.softmax(jnp.concatenate([s, sink], axis=-1), axis=-1)[..., :-1]
    o = jnp.einsum('bnkgqs,bnskd->bnqkgd', p.astype(vb.dtype), vb)
    return o.reshape(Bn, S, HQ * hd)

def dsa_attention(q, k, v, iq, ik, iw):
    Bn, S, H, hd = q.shape
    n_top = min(B_TOPK_MAX, S // 4)
    nqb = S // B_QBLOCK

    def to_blocks(t):
        return jnp.moveaxis(t.reshape((Bn, nqb, B_QBLOCK) + t.shape[2:]), 1, 0)

    kpos = jnp.arange(S)
    bidx = jnp.arange(Bn)[:, None, None]
    scale = hd ** -0.5

    def one_block(args):
        i, qb, iqb, iwb = args
        tpos = i * B_QBLOCK + jnp.arange(B_QBLOCK)
        raw = jnp.einsum('bqhd,bsd->bhqs', iqb, ik, preferred_element_type=jnp.float32)
        score = jnp.einsum('bhqs,bqh->bqs', jax.nn.relu(raw), iwb.astype(jnp.float32))
        causal = kpos[None, :] <= tpos[:, None]
        score = jnp.where(causal[None], score, -jnp.inf)
        _, idx = lax.top_k(score, n_top)
        valid = idx <= tpos[None, :, None]
        kg = k[bidx, idx]
        vg = v[bidx, idx]
        s = jnp.einsum('bqhd,bqkd->bhqk', qb, kg, preferred_element_type=jnp.float32) * scale
        s = jnp.where(valid[:, None], s, -jnp.inf)
        p = jax.nn.softmax(s, axis=-1)
        o = jnp.einsum('bhqk,bqkd->bqhd', p.astype(vg.dtype), vg)
        return o.reshape(Bn, B_QBLOCK, H * hd)

    out = lax.map(one_block, (jnp.arange(nqb), to_blocks(q), to_blocks(iq), to_blocks(iw)))
    return jnp.moveaxis(out, 0, 1).reshape(Bn, S, H * hd)

def moba_attention(q, k, v):
    Bn, S, H, hd = q.shape
    nb = -(-S // C_BLOCK)
    Sp = nb * C_BLOCK
    pad = ((0, 0), (0, Sp - S), (0, 0), (0, 0))
    kb = jnp.pad(k, pad).reshape(Bn, nb, C_BLOCK, H, hd).transpose(0, 3, 1, 2, 4)
    vb = jnp.pad(v, pad).reshape(Bn, nb, C_BLOCK, H, hd).transpose(0, 3, 1, 2, 4)
    kmean = jnp.mean(kb.astype(jnp.float32), axis=3)
    n_sel = min(C_TOPK, nb - 1)
    nqc = S // C_QCHUNK
    qc = q.reshape(Bn, nqc, C_QCHUNK, H, hd).transpose(1, 0, 3, 2, 4)
    bi = jnp.arange(Bn)[:, None, None, None]
    hi = jnp.arange(H)[None, :, None, None]
    scale = hd ** -0.5

    def one_chunk(args):
        i, qblk = args
        tpos = i * C_QCHUNK + jnp.arange(C_QCHUNK)
        own = tpos // C_BLOCK
        own_idx = jnp.broadcast_to(own[None, None, :, None], (Bn, H, C_QCHUNK, 1))
        own_ok = jnp.ones((Bn, H, C_QCHUNK, 1), dtype=bool)
        if n_sel > 0:
            gate = jnp.einsum('bhqd,bhnd->bhqn', qblk, kmean, preferred_element_type=jnp.float32)
            past = jnp.arange(nb)[None, :] < own[:, None]
            gate = jnp.where(past[None, None], gate, -jnp.inf)
            _, sel = lax.top_k(gate, n_sel)
            sel_ok = sel < own[None, None, :, None]
            blk = jnp.concatenate([sel, own_idx], axis=-1)
            blk_ok = jnp.concatenate([sel_ok, own_ok], axis=-1)
        else:
            blk, blk_ok = own_idx, own_ok
        kg = kb[bi, hi, blk]
        vg = vb[bi, hi, blk]
        s = jnp.einsum('bhqd,bhqnjd->bhqnj', qblk, kg, preferred_element_type=jnp.float32) * scale
        kpos = blk[..., None] * C_BLOCK + jnp.arange(C_BLOCK)
        ok = blk_ok[..., None] & (kpos <= tpos[None, None, :, None, None])
        s = jnp.where(ok, s, -jnp.inf)
        p = jax.nn.softmax(s.reshape(s.shape[:3] + (-1,)), axis=-1).reshape(s.shape)
        o = jnp.einsum('bhqnj,bhqnjd->bqhd', p.astype(vg.dtype), vg)
        return o.reshape(Bn, C_QCHUNK, H * hd)

    out = lax.map(one_chunk, (jnp.arange(nqc), qc))
    return jnp.moveaxis(out, 0, 1).reshape(Bn, S, H * hd)

def mixer_ab(h, cos, sin, w_in, q_norm, w_uq, w_uiq, sinks, w_out):
    Bn, S, _ = h.shape
    aq, ak, av, cq, bk, bv, bik, biw = _split_widths(h @ w_in, AB_WIDTHS)
    aq = apply_rope(aq.reshape(Bn, S, A_Q_HEADS, HEAD_DIM), cos, sin)
    ak = apply_rope(ak.reshape(Bn, S, A_KV_HEADS, HEAD_DIM), cos, sin)
    av = av.reshape(Bn, S, A_KV_HEADS, HEAD_DIM)
    ya = swa_sink_attention(aq, ak, av, sinks)
    cq = rms_norm(cq, q_norm)
    bq = apply_rope((cq @ w_uq).reshape(Bn, S, B_Q_HEADS, HEAD_DIM), cos, sin)
    biq = apply_rope((cq @ w_uiq).reshape(Bn, S, B_IDX_HEADS, B_IDX_DIM), cos, sin)
    bk = apply_rope(bk[:, :, None, :], cos, sin)[:, :, 0]
    bik = apply_rope(bik[:, :, None, :], cos, sin)[:, :, 0]
    iw = biw * (B_IDX_HEADS ** -0.5 * B_IDX_DIM ** -0.5)
    yb = dsa_attention(bq, bk, bv, biq, bik, iw)
    return jnp.concatenate([ya, yb], axis=-1) @ w_out

def mixer_c(h, cos, sin, w_in, w_out):
    Bn, S, _ = h.shape
    q, k, v = jnp.split(h @ w_in, 3, axis=-1)
    q = apply_rope(q.reshape(Bn, S, C_HEADS, HEAD_DIM), cos, sin)
    k = apply_rope(k.reshape(Bn, S, C_HEADS, HEAD_DIM), cos, sin)
    v = v.reshape(Bn, S, C_HEADS, HEAD_DIM)
    return moba_attention(q, k, v) @ w_out

def squared_relu_mlp(h, w1, w2):
    return jnp.square(jax.nn.relu(h @ w1)) @ w2

def first_inputs(seed: int = 0) -> dict:
    key = jax.random.key(seed)
    ks = jax.random.split(key, 20)
    f32 = jnp.float32
    n = lambda k, shp, s: jax.random.normal(k, shp, f32) * s
    D = D_MODEL
    return {
        "x": n(ks[0], (BATCH, SEQ, D), 1.0),
        "c": n(ks[1], (BATCH, D), 1.0),
        "positions": jnp.broadcast_to(jnp.arange(SEQ, dtype=jnp.int32)[None, :], (BATCH, SEQ)),
        "ab_w_in": n(ks[2], (N_EVEN, D, AB_IN_WIDTH), D ** -0.5),
        "ab_q_norm": 1.0 + n(ks[3], (N_EVEN, B_Q_RANK), 0.02),
        "ab_w_uq": n(ks[4], (N_EVEN, B_Q_RANK, B_Q_HEADS * HEAD_DIM), B_Q_RANK ** -0.5),
        "ab_w_uiq": n(ks[5], (N_EVEN, B_Q_RANK, B_IDX_HEADS * B_IDX_DIM), B_Q_RANK ** -0.5),
        "ab_sinks": n(ks[6], (N_EVEN, A_Q_HEADS), 1.0),
        "ab_w_out": n(ks[7], (N_EVEN, AB_MIX_WIDTH, D), AB_MIX_WIDTH ** -0.5 * DN_BETA),
        "c_w_in": n(ks[8], (N_ODD, D, 3 * C_WIDTH), D ** -0.5),
        "c_w_out": n(ks[9], (N_ODD, C_WIDTH, D), C_WIDTH ** -0.5 * DN_BETA),
        "ada_w": n(ks[10], (DEPTH, 2, D, 3 * D), 0.1 * D ** -0.5),
        "ada_b": n(ks[11], (DEPTH, 2, 3 * D), 0.02),
        "ln_g": 1.0 + n(ks[12], (DEPTH, 2, D), 0.02),
        "ln_b": n(ks[13], (DEPTH, 2, D), 0.02),
        "mlp_w1": n(ks[14], (DEPTH, D, D_FF), D ** -0.5),
        "mlp_w2": n(ks[15], (DEPTH, D_FF, D), D_FF ** -0.5 * DN_BETA),
    }

def first_block(x, c, positions, ab_w_in, ab_q_norm, ab_w_uq, ab_w_uiq, ab_sinks, ab_w_out,
              c_w_in, c_w_out, ada_w, ada_b, ln_g, ln_b, mlp_w1, mlp_w2):
    cos, sin = rope_tables(positions)
    for layer in range(DEPTH):
        shift, scale, gate = ada_modulation(c, ada_w[layer, 0], ada_b[layer, 0])
        h = x * (1.0 + scale) + shift
        if layer % 2 == 0:
            e = layer // 2
            y = mixer_ab(h, cos, sin, ab_w_in[e], ab_q_norm[e], ab_w_uq[e], ab_w_uiq[e],
                         ab_sinks[e], ab_w_out[e])
        else:
            o = layer // 2
            y = mixer_c(h, cos, sin, c_w_in[o], c_w_out[o])
        x = layer_norm(DN_ALPHA * x + gate * y, ln_g[layer, 0], ln_b[layer, 0])
        shift, scale, gate = ada_modulation(c, ada_w[layer, 1], ada_b[layer, 1])
        h = x * (1.0 + scale) + shift
        y = squared_relu_mlp(h, mlp_w1[layer], mlp_w2[layer])
        x = layer_norm(DN_ALPHA * x + gate * y, ln_g[layer, 1], ln_b[layer, 1])
    return x


GRID_W = 64
NUM_MIXERS = 2
MIX_WIDTH = D_MODEL
A_HEADS = MIX_WIDTH // HEAD_DIM
A_WIN_ROWS = 8
A_WIN_COLS = 16
B_Q_HEADS_2 = MIX_WIDTH // HEAD_DIM
B_KV_HEADS = 4
B_QBLK = 128
ROPE_SECTION = HEAD_DIM // 2
PLE_DIM = 256
NORM_EPS = 1e-6


def rms_norm_2(x, g):
    xf = x.astype(jnp.float32)
    y = xf * lax.rsqrt(jnp.mean(xf * xf, axis=-1, keepdims=True) + NORM_EPS)
    return (y * g.astype(jnp.float32)).astype(x.dtype)

def _na_indices(rows):
    win_r = min(A_WIN_ROWS, rows)
    win_c = A_WIN_COLS
    r = np.arange(rows)
    c = np.arange(GRID_W)
    rs = np.clip(r - win_r // 2, 0, rows - win_r)
    cs = np.clip(c - win_c // 2, 0, GRID_W - win_c)
    key_r = rs[:, None] + np.arange(win_r)[None, :]
    key_c = cs[:, None] + np.arange(win_c)[None, :]
    idx = key_r[:, None, :, None] * GRID_W + key_c[None, :, None, :]
    idx = idx.reshape(rows, GRID_W, win_r * win_c).astype(np.int32)
    dr = (key_r - r[:, None] + (A_WIN_ROWS - 1)).astype(np.int32)
    dc = (key_c - c[:, None] + (A_WIN_COLS - 1)).astype(np.int32)
    return idx, dr, dc

def mixer_a(h, w_in, rpb, w_out):
    b, s, _ = h.shape
    rows = s // GRID_W
    idx_np, dr, dc = _na_indices(rows)
    nk = idx_np.shape[-1]
    proj = h @ w_in
    q, k, v, gate = jnp.split(proj, 4, axis=-1)
    to_heads = lambda t: t.reshape(b, s, A_HEADS, HEAD_DIM).transpose(0, 2, 1, 3)
    q, k, v = to_heads(q), to_heads(k), to_heads(v)
    bias = rpb[:, dr[:, None, :, None], dc[None, :, None, :]]
    bias = bias.reshape(A_HEADS, rows, GRID_W, nk).transpose(1, 0, 2, 3)
    q_blk = q.reshape(b, A_HEADS, rows, GRID_W, HEAD_DIM).transpose(2, 0, 1, 3, 4)
    idx = jnp.asarray(idx_np)
    scale = 1.0 / math.sqrt(HEAD_DIM)

    def row_block(args):
        qb, ib, bb = args
        flat = ib.reshape(-1)
        kg = jnp.take(k, flat, axis=2).reshape(b, A_HEADS, GRID_W, nk, HEAD_DIM)
        vg = jnp.take(v, flat, axis=2).reshape(b, A_HEADS, GRID_W, nk, HEAD_DIM)
        sc = jnp.einsum('bhqd,bhqnd->bhqn', qb, kg).astype(jnp.float32) * scale
        sc = sc + bb.astype(jnp.float32)[None]
        pr = jax.nn.softmax(sc, axis=-1).astype(vg.dtype)
        return jnp.einsum('bhqn,bhqnd->bhqd', pr, vg)

    o = lax.map(row_block, (q_blk, idx, bias))
    o = o.transpose(1, 0, 3, 2, 4).reshape(b, s, MIX_WIDTH)
    return (o * jax.nn.silu(gate)) @ w_out

def _axial_rope(seq):
    t = jnp.arange(seq)
    row = (t // GRID_W).astype(jnp.float32)
    col = (t % GRID_W).astype(jnp.float32)
    n_freq = ROPE_SECTION // 2
    inv = jnp.power(ROPE_THETA, -jnp.arange(n_freq, dtype=jnp.float32) * 2.0 / ROPE_SECTION)
    ang_r = row[:, None] * inv[None, :]
    ang_c = col[:, None] * inv[None, :]
    return jnp.cos(ang_r), jnp.sin(ang_r), jnp.cos(ang_c), jnp.sin(ang_c)

def _rotate(x, cos, sin):
    x1, x2 = jnp.split(x, 2, axis=-1)
    return jnp.concatenate([x1 * cos - x2 * sin, x2 * cos + x1 * sin], axis=-1)

def _apply_axial_rope(x, tabs):
    cos_r, sin_r, cos_c, sin_c = tabs
    xf = x.astype(jnp.float32)
    xr = _rotate(xf[..., :ROPE_SECTION], cos_r, sin_r)
    xc = _rotate(xf[..., ROPE_SECTION:], cos_c, sin_c)
    return jnp.concatenate([xr, xc], axis=-1).astype(x.dtype)

def mixer_b(h, w_in, q_norm_g, k_norm_g, w_out):
    b, s, _ = h.shape
    group = B_Q_HEADS_2 // B_KV_HEADS
    kv_w = B_KV_HEADS * HEAD_DIM
    proj = h @ w_in
    q, k, v, gate = jnp.split(proj, [MIX_WIDTH, MIX_WIDTH + kv_w, MIX_WIDTH + 2 * kv_w], axis=-1)
    q = rms_norm_2(q.reshape(b, s, B_Q_HEADS_2, HEAD_DIM), q_norm_g).transpose(0, 2, 1, 3)
    k = rms_norm_2(k.reshape(b, s, B_KV_HEADS, HEAD_DIM), k_norm_g).transpose(0, 2, 1, 3)
    v = v.reshape(b, s, B_KV_HEADS, HEAD_DIM).transpose(0, 2, 1, 3)
    tabs = _axial_rope(s)
    q = _apply_axial_rope(q, tabs)
    k = _apply_axial_rope(k, tabs)
    nb = s // B_QBLK
    q_blk = q.reshape(b, B_KV_HEADS, group, nb, B_QBLK, HEAD_DIM).transpose(3, 0, 1, 2, 4, 5)
    scale = 1.0 / math.sqrt(HEAD_DIM)

    def q_block(qb):
        sc = jnp.einsum('bkgqd,bksd->bkgqs', qb, k).astype(jnp.float32) * scale
        pr = jax.nn.softmax(sc, axis=-1).astype(v.dtype)
        return jnp.einsum('bkgqs,bksd->bkgqd', pr, v)

    o = lax.map(q_block, q_blk)
    o = o.transpose(1, 0, 4, 2, 3, 5).reshape(b, s, MIX_WIDTH)
    return (o * jax.nn.silu(gate)) @ w_out

def second_inputs(seed: int = 0) -> dict:
    key = jax.random.key(seed)
    ks = jax.random.split(key, 16)
    n_a = (DEPTH + NUM_MIXERS - 1) // NUM_MIXERS
    n_b = DEPTH // NUM_MIXERS
    kv_w = B_KV_HEADS * HEAD_DIM
    b_in_w = 2 * MIX_WIDTH + 2 * kv_w
    nrm = lambda k, shape, fan: jax.random.normal(k, shape, jnp.float32) * (fan ** -0.5)
    gain = lambda k, shape: 1.0 + 0.05 * jax.random.normal(k, shape, jnp.float32)
    return {
        "x": jax.random.normal(ks[0], (BATCH, SEQ, D_MODEL), jnp.float32),
        "p": jax.random.normal(ks[1], (DEPTH, BATCH, SEQ, PLE_DIM), jnp.float32),
        "norm_g": gain(ks[2], (DEPTH, D_MODEL)),
        "a_w_in": nrm(ks[3], (n_a, D_MODEL, 4 * MIX_WIDTH), D_MODEL),
        "a_rpb": 0.1 * jax.random.normal(ks[4], (n_a, A_HEADS, 2 * A_WIN_ROWS - 1, 2 * A_WIN_COLS - 1), jnp.float32),
        "a_w_out": nrm(ks[5], (n_a, MIX_WIDTH, D_MODEL), MIX_WIDTH),
        "b_w_in": nrm(ks[6], (n_b, D_MODEL, b_in_w), D_MODEL),
        "b_q_norm": gain(ks[7], (n_b, HEAD_DIM)),
        "b_k_norm": gain(ks[8], (n_b, HEAD_DIM)),
        "b_w_out": nrm(ks[9], (n_b, MIX_WIDTH, D_MODEL), MIX_WIDTH),
        "ple_norm_g": gain(ks[10], (DEPTH, D_MODEL)),
        "ple_w_gate": nrm(ks[11], (DEPTH, D_MODEL, D_MODEL), D_MODEL),
        "ple_w_proj": nrm(ks[12], (DEPTH, PLE_DIM, D_MODEL), PLE_DIM),
        "final_norm_g": gain(ks[13], (D_MODEL,)),
    }

def second_block(x, p, norm_g, a_w_in, a_rpb, a_w_out, b_w_in, b_q_norm, b_k_norm,
              b_w_out, ple_norm_g, ple_w_gate, ple_w_proj, final_norm_g):
    for i in range(DEPTH):
        h = rms_norm_2(x, norm_g[i])
        j = i // NUM_MIXERS
        if i % NUM_MIXERS == 0:
            y = mixer_a(h, a_w_in[j], a_rpb[j], a_w_out[j])
        else:
            y = mixer_b(h, b_w_in[j], b_q_norm[j], b_k_norm[j], b_w_out[j])
        x = x + y
        g = jax.nn.sigmoid(rms_norm_2(x, ple_norm_g[i]) @ ple_w_gate[i])
        x = x + g * (p[i] @ ple_w_proj[i])
    return rms_norm_2(x, final_norm_g)


def setup_inputs(seed=0):
    out = dict(first_inputs(seed))
    for name, value in second_inputs(seed + 1).items():
        if name != "x":
            out[name + "_2"] = value
    return out


def reference(
    x, c, positions, ab_w_in, ab_q_norm, ab_w_uq, ab_w_uiq, ab_sinks, ab_w_out, c_w_in, c_w_out,
    ada_w, ada_b, ln_g, ln_b, mlp_w1, mlp_w2, p_2, norm_g_2, a_w_in_2, a_rpb_2, a_w_out_2,
    b_w_in_2, b_q_norm_2, b_k_norm_2, b_w_out_2, ple_norm_g_2, ple_w_gate_2, ple_w_proj_2,
    final_norm_g_2,
):
    x = first_block(
        x, c, positions, ab_w_in, ab_q_norm, ab_w_uq, ab_w_uiq, ab_sinks, ab_w_out, c_w_in,
        c_w_out, ada_w, ada_b, ln_g, ln_b, mlp_w1, mlp_w2,
    )
    return second_block(
        x, p_2, norm_g_2, a_w_in_2, a_rpb_2, a_w_out_2, b_w_in_2, b_q_norm_2, b_k_norm_2,
        b_w_out_2, ple_norm_g_2, ple_w_gate_2, ple_w_proj_2, final_norm_g_2,
    )


_drawn_inputs = setup_inputs


def setup_inputs(seed=0):
    import zlib

    import numpy as np

    out = dict(_drawn_inputs(seed))
    spreads = {}
    factors = {'ab_q_norm': 8.0,
     'ab_sinks': 8.0,
     'norm_g_2': 3.835,
     'a_rpb_2': 6.535,
     'b_q_norm_2': 8.0,
     'b_k_norm_2': 8.0,
     'ple_norm_g_2': 4.694}
    for name, (base, spread) in spreads.items():
        noise = np.random.default_rng([zlib.crc32(name.encode()), seed]).standard_normal(out[name].shape)
        drawn = base * np.exp(spread * noise) if base else spread * noise
        out[name] = __import__('jax').numpy.asarray(drawn.astype(out[name].dtype))
    for name, factor in factors.items():
        out[name] = (out[name] * factor).astype(out[name].dtype)
    return out
```

```python
from contextlib import ExitStack

import numpy as np

import concourse.bass as bass
from concourse import mybir

F32 = mybir.dt.float32
F32R = mybir.dt.float32r
BF16 = mybir.dt.bfloat16
I32 = mybir.dt.int32
U32 = mybir.dt.uint32
ALU = mybir.AluOpType
ACT = mybir.ActivationFunctionType
AX = mybir.AxisListType.X

P = 128
S = 256
T = S // P
D = 1024
KD = D // P
HD = 64
FF = 4 * D
N_SUB = 4
ALPHA = 4 ** 0.25
LN_EPS = 1e-5
RMS_EPS = 1e-6
SCALE = HD ** -0.5
MASKED = -1e30
PICKED = -3e38
TOPK = 64
GRID = 64
IW_SCALE = 8 ** -0.5 * HD ** -0.5
TWO_PI = 2 * np.pi
C1 = 6.28125
C2 = float(np.float32(np.round((TWO_PI - C1) * 2 ** 20) / 2 ** 20))
C3 = float(np.float32(TWO_PI - C1 - C2))
ROUND = 1.5 * 2 ** 23
RSQRT_MAGIC = float(0x5F3759DF)

TILE = 2048
RAW_SLOTS = 4

CONST = {}
_at = 0
for _name, _n in (("ident", P), ("ones", P), ("causal", P), ("window", P), ("invf", HD), ("sign", HD),
                  ("axcos", T * HD), ("axsin", T * HD), ("near", GRID)):
    CONST[_name] = (_at, _at + _n)
    _at += _n
N_CONST = _at

VEC_A = {"ada_b": 0, "c": 96}
N_VEC_A = 104
VEC_B = {"ln_g": 0, "ln_b": 32, "norm_g": 64, "ple_g": 80, "q_norm": 96}
N_VEC_B = 98


def constants():
    out = np.zeros((P, N_CONST), np.float32)

    def put(name, value):
        a, b = CONST[name]
        out[:, a:b] = value

    row = np.arange(P)[:, None]
    col = np.arange(P)[None, :]
    put("ident", np.eye(P))
    put("ones", 1.0)
    put("causal", np.where(col <= row, 0.0, MASKED))
    put("window", np.where(col > row, 0.0, MASKED))
    inv = 10000.0 ** (-np.arange(0, HD, 2) / HD)
    put("invf", np.concatenate([inv, inv])[None, :])
    put("sign", np.concatenate([-np.ones(HD // 2), np.ones(HD // 2)])[None, :])
    quarter = HD // 4
    inv = 10000.0 ** (-np.arange(quarter) * 2.0 / (HD // 2))
    token = np.arange(S).reshape(T, P).T
    ang = np.stack([(token // GRID)[:, :, None] * inv, (token % GRID)[:, :, None] * inv], 2)
    put("axcos", np.stack([np.cos(ang), np.cos(ang)], 3).reshape(P, T * HD))
    put("axsin", np.stack([-np.sin(ang), np.sin(ang)], 3).reshape(P, T * HD))
    c = np.arange(P)[:, None] % GRID
    start = np.clip(c - 8, 0, GRID - 16)
    key = np.arange(GRID)[None, :]
    put("near", np.where((key >= start) & (key < start + 16), 0.0, MASKED))
    return out


def make_plan(R):
    plan, tiles = [], []
    count = {"split": 0, "ada": 0, "job": 0, "rows": 0, "cut": 0, "head": 0, "score": 0, "ssq": 0, "high": 0}
    uses = [0] * 8
    cut_of = {}
    pair = [0]
    gate_jobs = []

    def tick(name, n=1):
        count[name] += n
        return count[name]

    def rows():
        return tick("rows")

    def add(kind, **k):
        plan.append({"kind": kind, **k})
        return plan[-1]

    def banks(pairs=None):
        if pairs is None:
            b = 2 * (pair[0] % 2)
            pair[0] += 1
            pairs = (b, b + 1)
        got = [(b, uses[b]) for b in pairs]
        for b in pairs:
            uses[b] += 1
        return got

    ride = [0, 1, 0]

    def tile(view, kc, cols, kind):
        if kind == "split" and ride[0]:
            ride[2] += 1
            if ride[2] % ride[1] == 0:
                ride[0] -= 1
                ada_tiles(1)
        tiles.append({"view": view, "kc": kc, "cols": cols, "kind": kind, "n": tick(kind) - 1})
        return tiles[-1]["n"]

    def job(kind, **k):
        return add(kind, banks=banks(), job=tick("job"), **k)

    def linear(w, c0, width, kc, lhs, end, k0=0, cut=None):
        bk = banks()
        step = min(4, kc)
        v = w.rearrange("(k p) n -> p k n", p=P)
        for h in range(kc // step):
            n = tile(v[:, k0 + h * step:k0 + (h + 1) * step, c0:c0 + width], step, width, "split")
            last = h == kc // step - 1
            it = add("tokens", tile=n, kc=step, width=width, lhs=lhs, off=h * step, banks=bk,
                     first=h == 0, last=last, cut=cut or count["cut"], enter=h == 0)
            if last:
                it["end"] = end
        return it

    def split_rows(src, chunks, dst, wait, affine=None, dst0=0):
        for a in range(0, chunks, 4):
            n = min(4, chunks - a)
            nb = (n + 1) // 2
            it = job("turn_split", src=src, a=a, n=n, dst=dst, dst0=dst0, wait=wait, affine=affine)
            it["banks"] = it["banks"][:nb]
            if nb == 1:
                uses[it["banks"][0][0] + 1] -= 1
            it["heads"] = count["head"]
            it["high"] = tick("high")
            it["emptied"] = cut_of.get(it["banks"][0][0], 0)
            tick("cut", nb)
            cut_of[it["banks"][0][0]] = count["cut"]

    def gate(s):
        gate_jobs.append(count["job"] + 1)
        return job("gate_row", s=s)

    def turn(src_cols, dst, wait):
        before = list(uses)
        for a in range(0, len(src_cols), 4):
            job("turn", cols=src_cols[a:a + 4], dst=dst + a, wait=wait, before=before)

    def heads(kind, spec):
        it = add("heads", mode=kind, spec=spec, s0=count["score"], h0=count["head"], uses=list(uses))
        tick("score", len(spec))
        if kind != "index":
            tick("head", len(spec))
        return it

    def ada_tiles(n):
        for i in range(count["ada"], count["ada"] + n):
            s, part, k = i // 12, i // 4 % 3, i % 4
            w = R["ada_w"][s // 2, s % 2].rearrange("(k p) n -> p k n", p=P)
            tile(w[:, 2 * k:2 * k + 2, part * D:(part + 1) * D], 2, D, "ada")
            tiles[-1].update(s=s, part=part, k=2 * k)

    def spread(n, every):
        ride[:] = [n, every, 0]

    def ada(s):
        it = job("ada_columns", s=s)
        it["banks"] = it["banks"][:1]
        uses[it["banks"][0][0] + 1] -= 1
        it["ada"] = 12 * s + 8

    def mlp(layer, end):
        w1 = R["mlp_w1"][layer].rearrange("(k p) n -> p k n", p=P)
        w2 = R["mlp_w2"][layer].rearrange("(k p) n -> p k n", p=P)
        yb = {n: banks((4 + 2 * n, 5 + 2 * n)) for n in range(2)}
        hid_cut = {}
        enter = {0: True, 1: True}
        need = count["cut"]

        def up(g):
            for j in range(2):
                bk = banks()
                for h in range(2):
                    c0 = g * 1024 + j * 512 + h * 256
                    n = tile(w1[:, :, c0:c0 + 256], KD, 256, "split")
                    it = add("hidden", tile=n, half=h, banks=bk, cut=need, buf=g % 2, c0=4 * j)
                it["end"] = "hidden"
                it["high"] = tick("high")
                it["emptied"] = cut_of.get(bk[0][0], 0)
                tick("cut", 2)
                cut_of[bk[0][0]] = count["cut"]
            hid_cut[g] = count["cut"]

        def down(g):
            for n in range(2):
                for h in range(2):
                    k0 = g * 8 + h * 4
                    t = tile(w2[:, k0:k0 + 4, n * 512:(n + 1) * 512], 4, 512, "split")
                    it = add("tokens", tile=t, kc=4, width=512, lhs=("hid", g % 2), off=h * 4, banks=yb[n],
                             first=g == 0 and h == 0, last=g == 3 and h == 1, cut=hid_cut[g], enter=g == 0 and h == 0)
                if g == 3:
                    it["end"] = ("y_ln", n)

        up(0)
        gate(2 * layer + 1)
        if layer == 0:
            spread(12, 2)
        up(1), down(0), up(2), down(1), up(3), down(2), down(3)

    def norm_ln(s):
        it = add("ln", s=s)
        it["rows"] = tick("rows", 2)
        return it["rows"]

    def norm_rms():
        it = add("rms")
        it["rows"] = tick("rows", 2)
        it["ssq"] = count["ssq"]
        return it["rows"]

    def y_rms(w):
        for n in range(2):
            linear(w, n * 512, 512, KD, "ht", ("y_rms", n))
            tick("ssq", 2)

    job("turn_vectors")
    uses[1] -= 1
    ada_tiles(8)
    ada(0)
    add("rope_tables")
    spread(4, 2)
    split_rows("x", KD, "ht", 0, ("affine", 0))
    w = R["ab_w_in"][0]
    linear(w, 512, 512, KD, "ht", ("tok", 512, 1.0, 512))
    add("low_rank", rows=rows(), uses=list(uses))
    cq_rows = count["rows"]
    linear(w, 1024, 200, KD, "ht", ("tok", 1024, 1.0, 200))
    add("rope", what=[(512, 2, 2304), (1024, 1, 2560), (1152, 1, 2688)], table="text", rows=rows(), uses=list(uses))
    linear(w, 0, 512, KD, "ht", ("tok", 0, 1.0, 512))
    add("rope", what=[(0, 8, None)], table="text", rows=rows(), uses=list(uses))
    aq_rows = count["rows"]
    split_rows("cq", 2, "ht", cq_rows, ("vec", VEC_B["q_norm"]))
    linear(R["ab_w_uiq"][0], 0, 512, 2, "ht", ("tok", 1792, 1.0, 512))
    add("rope", what=[(1792, 8, None)], table="text", rows=rows(), uses=list(uses))
    biq_rows = count["rows"]
    linear(R["ab_w_uq"][0], 0, 512, 2, "ht", ("tok", 1280, 1.0, 512))
    add("rope", what=[(1280, 8, None)], table="text", rows=rows(), uses=list(uses))
    gate(0)
    ada_tiles(12)
    turn([0, 128, 256, 384, 2304, 2432, 2560, 2688], 0, aq_rows)
    turn([1792, 1920, 2048, 2176], 12, biq_rows)
    turn([1280, 1408, 1536, 1664], 8, count["rows"])
    heads("index", [(12 + h // 2, h % 2, 7, None, h) for h in range(8)])
    heads("window", [(h // 2, h % 2, 4 + h // 4, 640 + HD * (h // 4), h) for h in range(8)])
    heads("sparse", [(8 + h // 2, h % 2, 6, 1088, 8 + h) for h in range(8)])
    split_rows("o", KD, "ht", 0)
    for n in range(2):
        linear(R["ab_w_out"][0], n * 512, 512, KD, "ht", ("y_ln", n))
    r = norm_ln(0)
    ada(1)
    split_rows("xhat", KD, "ht", r, ("affine", 1))
    add("resid", s=0)
    mlp(0, None)
    r = norm_ln(1)
    ada(2)
    split_rows("xhat", KD, "ht", r, ("affine", 2))
    add("resid", s=1)
    w = R["c_w_in"][0]
    for j in range(4):
        linear(w, j * 512, 512, KD, "ht", ("tok", j * 512, 1.0, 512))
        add("rope", what=[(j * 512, 8, None)], table="text", rows=rows(), uses=list(uses))
        if j == 0:
            gate(2)
    spread(4, 1)
    for j in range(4, 6):
        linear(w, j * 512, 512, KD, "ht", ("tok", j * 512, 1.0, 512))
    ada_tiles(8)
    turn([P * i for i in range(16)], 0, count["rows"])
    heads("causal", [(h // 2, h % 2, 8 + h // 2, 2048 + HD * h, h) for h in range(16)])
    split_rows("o", KD, "ht", 0)
    for n in range(2):
        linear(R["c_w_out"][0], n * 512, 512, KD, "ht", ("y_ln", n))
    r = norm_ln(2)
    ada(3)
    split_rows("xhat", KD, "ht", r, ("affine", 3))
    add("resid", s=2)
    mlp(1, None)
    norm_ln(3)
    add("resid", s=3)
    tick("ssq", 4)
    for i in range(2):
        r = norm_rms()
        split_rows("xhat", KD, "ht", r, ("vec", VEC_B["norm_g"] + KD * i))
        if i == 0:
            w = R["a_w_in_2"][0]
            first_tile = len(tiles)
            for j in range(6):
                linear(w, j * 512, 512, KD, "ht", ("tok", j * 512, 1.0, 512))
            tiles[first_tile]["near"] = True
            for j in range(6, 8):
                linear(w, j * 512, 512, KD, "ht", ("silu", j * 512, 0.5, 512))
            add("bias_table", rows=rows())
            add("gates", c0=3072, uses=list(uses))
            turn([P * j for j in range(16)], 0, count["rows"])
            heads("near", [(h // 2, h % 2, 8 + h // 2, 2048 + HD * h, h) for h in range(16)])["gate"] = 3072
        else:
            w = R["b_w_in_2"][0]
            add("axial_tables")
            linear(w, 1024, 512, KD, "ht", ("tok", 1024, 1.0, 512))
            add("qk_rope", what=[(1024, 4, 2560)], gain="k", rows=rows(), uses=list(uses))
            for j in range(2):
                linear(w, j * 512, 512, KD, "ht", ("tok", j * 512, 1.0, 512))
                add("qk_rope", what=[(j * 512, 8, None)], gain="q", rows=rows(), uses=list(uses))
            for j in range(3, 5):
                linear(w, j * 512, 512, KD, "ht", ("silu", j * 512, 0.5, 512))
            add("gates", c0=1536, uses=list(uses))
            turn([P * j for j in range(8)] + [2560 + P * j for j in range(4)], 0, count["rows"])
            heads("full", [(h // 2, h % 2, 8 + h // 4, 1280 + HD * (h // 4), h) for h in range(16)])["gate"] = 1536
        split_rows("o", KD, "ht", 0)
        y_rms(R[("a" if i == 0 else "b") + "_w_out_2"][0])
        r = norm_rms()
        split_rows(("p", i), 2, "plt", 0)
        for n in range(2):
            linear(R["ple_w_proj_2"][i], n * 512, 512, 2, "plt", ("tok", n * 512, 0.5, 512))
        split_rows("xhat", KD, "ht", r, ("vec", VEC_B["ple_g"] + KD * i))
        for n in range(2):
            linear(R["ple_w_gate_2"][i], n * 512, 512, KD, "ht", ("ple", n))
            tick("ssq", 2)
    add("final", ssq=count["ssq"], rows=tick("rows", 2))
    assert ride[0] == 0 and count["ada"] == 12 * N_SUB
    split = [t for t in tiles if t["kind"] == "split"]
    order = tiles[:8] + split[:2]
    for t in tiles[8:]:
        if t["kind"] == "ada":
            order.append(t)
        elif t["n"] + 2 < len(split):
            order.append(split[t["n"] + 2])
    near_first = next(r for r, t in enumerate(order) if t.get("near"))
    for r, t in enumerate(order):
        t["slot"], t["full"] = r % RAW_SLOTS, 16 * (r // RAW_SLOTS + 1)
    adas = [t for t in tiles if t["kind"] == "ada"]
    for t in adas:
        t["gate_job"] = gate_jobs[t["s"] - 1] if t["s"] else 0
    return plan, order, split, adas, near_first + 2 + RAW_SLOTS


def block_kernel(nc, R, out, toeplitz):
    plan, order, split, adas, bias_from = make_plan(R)
    p_after = [i["h0"] + len(i["spec"]) for i in plan if i["kind"] == "heads" and i["mode"] in ("near", "full")]

    with ExitStack() as ctx:
        def sb(name, shape, dt=F32):
            return ctx.enter_context(nc.sbuf_tensor(name, shape, dt))

        def sem(name):
            return ctx.enter_context(nc.semaphore(name))

        x = sb("x", [P, T, D])
        u = sb("u", [P, T, D])
        ht_hi = sb("ht_hi", [P, KD, S], F32R)
        ht_lo = sb("ht_lo", [P, KD, S], F32R)
        plt_hi = sb("plt_hi", [P, 2, S], F32R)
        plt_lo = sb("plt_lo", [P, 2, S], F32R)
        tok = sb("tok", [P, T, 4 * D])
        qkt = sb("qkt", [P, 16, S])
        near_bias = sb("near_bias", [P, 16, 6 * GRID])
        raw = sb("raw", [P, RAW_SLOTS, TILE])
        w_hi = sb("w_hi", [P, 2, TILE], F32R)
        w_lo = sb("w_lo", [P, 2, TILE], F32R)
        full = sb("full", [P, 4, 512])
        probs = sb("probs", [P, 3, T, S])
        probs_t = sb("probs_t", [P, 2, T, S])
        biased = sb("biased", [P, 2, T, S])
        tmp_a = sb("tmp_a", [P, 512])
        tmp_b = sb("tmp_b", [P, 512])
        consts = sb("consts", [P, N_CONST])
        vec = sb("vec", [P, N_VEC_A + N_VEC_B])
        cs = sb("cs", [P, 3, KD])
        mod = sb("mod", [P, 2 * KD])
        aff = sb("aff", [P, 2, KD])
        pos_i = sb("pos_i", [P, T], I32)
        pos_f = sb("pos_f", [P, T])
        cosr = sb("cosr", [P, T, HD])
        sinr = sb("sinr", [P, T, HD])
        gain = sb("gain", [P, 2, HD])
        stats = sb("stats", [P, T, 2, 6])
        meanvar = sb("meanvar", [P, T, 2])
        ssq = sb("ssq", [P, T, 2])
        small = sb("small", [P, 3, 16])
        bits = sb("bits", [P, 16], U32)
        rstd = sb("rstd", [P, 16])
        sinks = sb("sinks", [P, 2, 8])
        mx = sb("mx", [P, 4, T])
        nmx = sb("nmx", [P, 4, T])
        sums = sb("sums", [P, 4, T])
        rs = sb("rs", [P, 4, T])
        sink_exp = sb("sink_exp", [P, 4, T])
        iw = sb("iw", [P, T, 8])
        top8 = sb("top8", [P, 8])
        maskb = sb("maskb", [P, 3, P], BF16)
        smask = sb("smask", [P, T, S], BF16)

        def over(owner, offset, name, shape, dt=F32):
            return nc.alloc_sbuf_tensor_at(name, shape, dt, offset=nc.lookup_mloc(owner).addr + offset)

        hid_hi = over(tok, 0, "hid_hi", [P, 2, KD, S], F32R)
        hid_lo = over(tok, 2 * KD * S * 4, "hid_lo", [P, 2, KD, S], F32R)
        g_row = over(near_bias, 0, "g_row", [P, D])
        b_row = over(near_bias, 4 * D, "b_row", [P, D])
        gate_row = over(near_bias, 8 * D, "gate_row", [P, D])
        ada_sum = over(near_bias, 12 * D, "ada_sum", [P, 3, D])
        score = over(plt_hi, 0, "score", [P, T, S])
        rpb_rows = over(qkt, 0, "rpb_rows", [16, 7, 128])
        vec_rows = over(qkt, 4 * D, "vec_rows", [P, 2, P])
        ax = over(near_bias, 8 * D, "ax", [P, 2, 2, T, HD])
        angle = over(biased, 0, "angle", [P, 3, T, HD])
        junk = over(probs, 4 * D, "junk", [P, 512])
        g_final = over(near_bias, 0, "g_final", [P, D])
        p_rows = over(probs, 0, "p_rows", [P, T, S])
        assert nc.lookup_mloc(near_bias).dims[1] >= 24 * D

        bank = [ctx.enter_context(nc.psum_tensor(f"bank{b}", [P, 512], F32)) for b in range(8)]

        raw_in = [sem(f"raw_in{i}") for i in range(RAW_SLOTS)]
        const_in = sem("const_in")
        vec_in = sem("vec_in")
        gate_in = sem("gate_in")
        row_in = sem("row_in")
        p_in = [sem(f"p_in{i}") for i in range(2)]
        misc_in = sem("misc_in")
        pad_ready = sem("pad_ready")
        rpb_in = sem("rpb_in")
        pad_out = sem("pad_out")
        bias_in = sem("bias_in")
        final_in = sem("final_in")
        out_done = sem("out_done")
        high_done = sem("high_done")
        low_done = sem("low_done")
        tile_done = sem("tile_done")
        ada_done = sem("ada_done")
        job_done = sem("job_done")
        bank_free = [sem(f"bank_free{b}") for b in range(8)]
        high_copied = sem("high_copied")
        split_done = sem("split_done")
        rows_ready = sem("rows_ready")
        silu_ready = sem("silu_ready")
        affine_ready = sem("affine_ready")
        resid_done = sem("resid_done")
        x_ready = sem("x_ready")
        ssq_ready = sem("ssq_ready")
        tanh_ready = sem("tanh_ready")
        angle_ready = sem("angle_ready")
        sin_ready = sem("sin_ready")
        scores_ready = sem("scores_ready")
        negmax_ready = sem("negmax_ready")
        scores_used = sem("scores_used")
        probs_turned = sem("probs_turned")
        turned_copied = [sem("turned_copied_act"), sem("turned_copied_dve")]
        head_out = sem("head_out")
        head_copied = sem("head_copied")
        index_used = sem("index_used")
        mask_ready = sem("mask_ready")
        act_step = sem("act_step")
        dve_step = sem("dve_step")
        pool_step = sem("pool_step")

        def const(name):
            a, b = CONST[name]
            return consts[:, a:b]

        ident = const("ident")
        sources = {"x": x, "xhat": u, "o": u}

        def raw_tile(t):
            return raw[:, t["slot"], 0:t["kc"] * t["cols"]]

        def view(buf, n):
            t = split[n]
            return buf[:, n % 2, 0:t["kc"] * t["cols"]].rearrange("p (k n) -> p k n", k=t["kc"])

        def source(it, t, c):
            if it["src"] == "cq":
                return tok[:, t, 768 + c * P:768 + (c + 1) * P]
            if it["src"][0] == "p":
                return p_rows[:, t, c * P:(c + 1) * P]
            return sources[it["src"]][:, t, c * P:(c + 1) * P]

        pool_steps = [0]

        def ada_products(engine, ops, n):
            t = adas[n]
            if n in (0, 8):
                engine.wait_ge(silu_ready, 1)
            if t["part"] == t["k"] == 0 and t["s"]:
                engine.wait_ge(job_done, t["gate_job"])
            engine.wait_ge(raw_in[t["slot"]], t["full"])
            w = raw_tile(t).rearrange("p (k n) -> p k n", k=2)
            dst = ada_sum[:, t["part"], :]
            for i in range(2):
                c = cs[:, 0, t["k"] + i:t["k"] + i + 1]
                if t["k"] + i == 0:
                    ins = ops.tensor_scalar(dst, w[:, i, :], c, None, ALU.mult)
                elif n < 8:
                    ins = ops.scalar_tensor_tensor(dst, w[:, i, :], c, dst, ALU.mult, ALU.add)
                else:
                    ops.tensor_tensor(w[:, i, :], w[:, i, :], c.broadcast_to([P, D]), ALU.mult).then_inc(pool_step, 1)
                    pool_steps[0] += 1
                    engine.wait_ge(pool_step, pool_steps[0])
                    ins = ops.tensor_tensor(dst, w[:, i, :], dst, ALU.add)
                ins.then_inc(ada_done, 1)
                engine.wait_ge(ada_done, 2 * n + i + 1)

        def parts(it):
            return (plt_hi, plt_lo) if it["dst"] == "plt" else (ht_hi, ht_lo)

        def head_cols(mode, t):
            return P * (t + 1) if mode in ("causal", "window", "sparse", "index") else S

        def turned_halves(mode, h):
            dst, src = probs_t[:, h % 2, :, :], bank[4 + h % 2][:, :].rearrange("p (k q) -> p k q", k=T)
            if mode in ("near", "full"):
                return [(dst, src)]
            return [(dst[:, 0, :], src[:, 0, :]), (dst[:, 1, P:S], src[:, 1, P:S])]

        block = ctx.enter_context(nc.Block())

        @block.sync
        def _(sp):
            sp.dma_start(consts[:, :], R["consts"]).then_inc(const_in, 16)
            ada_rows = R["ada_b"].rearrange("l s (j p) -> (l s j) p", p=P)
            ln_rows = [R[n].rearrange("l s (j p) -> (l s j) p", p=P) for n in ("ln_g", "ln_b")]
            sp.dma_start(vec_rows[0:96, 0, :], ada_rows).then_inc(vec_in, 16)
            sp.dma_start(vec_rows[96:104, 0, :], R["c"].rearrange("b (j p) -> (b j) p", p=P)).then_inc(vec_in, 16)
            sp.dma_start(vec_rows[0:32, 1, :], ln_rows[0]).then_inc(vec_in, 16)
            sp.dma_start(vec_rows[32:64, 1, :], ln_rows[1]).then_inc(vec_in, 16)
            for name, a, n in (("norm_g_2", 64, 16), ("ple_norm_g_2", 80, 16), ("ab_q_norm", 96, 2)):
                sp.dma_start(vec_rows[a:a + n, 1, :], R[name].rearrange("l (j p) -> (l j) p", p=P)).then_inc(vec_in, 16)
            sp.dma_start(x[:, :, :], R["x"][0].rearrange("(t p) d -> p t d", p=P)).then_inc(const_in, 16)
            with nc.allow_non_contiguous_dma("256 positions"):
                sp.dma_start(pos_i[:, :], R["positions"][0].rearrange("(t p) -> p t", p=P)).then_inc(const_in, 16)
            for r, t in enumerate(order):
                if r >= bias_from and bias_from + 16 > r:
                    if r == bias_from:
                        sp.wait_ge(pad_out, 16)
                        sp.wait_ge(resid_done, T * N_SUB)
                    for row in range(8 * (r - bias_from), 8 * (r - bias_from + 1)):
                        half, c = row // GRID, row % GRID
                        sp.dma_start(
                            near_bias[row:row + 1, :, :],
                            bass.AP(toeplitz, (1 - half) * 128 + GRID - 1 - c, [[0, 1], [7 * 128, 16], [128, 6], [1, GRID]]),
                        ).then_inc(bias_in, 16)
                if r >= RAW_SLOTS:
                    old = order[r - RAW_SLOTS]
                    if old["kind"] == "split":
                        sp.wait_ge(low_done, old["n"] + 1)
                    else:
                        sp.wait_ge(ada_done, 2 * (old["n"] + 1))
                dst = raw_tile(t).rearrange("p (k n) -> p k n", k=t["kc"])
                sp.dma_start(dst, t["view"]).then_inc(raw_in[t["slot"]], 16)
            for t in range(T):
                sp.wait_ge(rows_ready, plan[-1]["rows"] - T + t + 1)
                sp.dma_start(out[0, t * P:(t + 1) * P, :], u[:, t, :]).then_inc(out_done, 16)
            sp.wait_ge(out_done, 16 * T)

        @block.gpsimd
        def _(pool):
            pool.dma_start(sinks[:, 0, :], R["ab_sinks"][0].partition_broadcast(P)).then_inc(misc_in, 16)
            pool.dma_start(gain[:, 0, :], R["b_q_norm_2"][0].partition_broadcast(P)).then_inc(misc_in, 16)
            pool.dma_start(gain[:, 1, :], R["b_k_norm_2"][0].partition_broadcast(P)).then_inc(misc_in, 16)
            for s in range(N_SUB):
                if s:
                    pool.wait_ge(resid_done, T * s)
                gate_bias = R["ada_b"][s // 2, s % 2, 2 * D:3 * D]
                pool.dma_start(gate_row[:, :], gate_bias.partition_broadcast(P)).then_inc(gate_in, 16)
                pool.dma_start(g_row[:, :], R["ln_g"][s // 2, s % 2].partition_broadcast(P)).then_inc(row_in, 16)
                pool.dma_start(b_row[:, :], R["ln_b"][s // 2, s % 2].partition_broadcast(P)).then_inc(row_in, 16)
                for n, t in enumerate(adas):
                    if n >= 8 and (t["s"] == s + 1 or n < 12 and s == 0):
                        ada_products(pool, nc.gpsimd, n)
                if s == 3:
                    nc.gpsimd.memset(rpb_rows[:, :, :], 0.0).then_inc(pool_step, 1)
                    pool.wait_ge(pool_step, pool_steps[0] + 1)
                    pool.dma_start(rpb_rows[:, :, 48:79], R["a_rpb_2"][0, :, 4:11, :]).then_inc(rpb_in, 16)
                    pool.wait_ge(rpb_in, 16)
                    pool.dma_start(toeplitz[:, :, :], rpb_rows[:, :, :]).then_inc(pad_out, 16)
            for i in range(2):
                pool.wait_ge(probs_turned, p_after[i])
                pool.dma_start(p_rows[:, :, :], R["p_2"][i, 0].rearrange("(t p) d -> p t d", p=P)).then_inc(p_in[i], 16)
                if i == 0:
                    pool.dma_start(g_final[:, :], R["final_norm_g_2"].partition_broadcast(P)).then_inc(final_in, 16)

        @block.scalar
        def _(act):
            steps = [0]

            def link(ins):
                steps[0] += 1
                ins.then_inc(act_step, 1)
                act.wait_ge(act_step, steps[0])

            def split_high(n):
                if n >= len(split):
                    return
                t = split[n]
                act.wait_ge(raw_in[t["slot"]], t["full"])
                if n >= 2:
                    act.wait_ge(tile_done, n - 1)
                size = t["kc"] * t["cols"]
                nc.scalar.activation(w_hi[:, n % 2, 0:size], raw_tile(t), ACT.Copy).then_inc(high_done, 1)

            def squares(t, n):
                nc.scalar.activation(junk[:, :], x[:, t, n * 512:(n + 1) * 512], ACT.Square,
                                     accum_out=ssq[:, t, n:n + 1]).then_inc(ssq_ready, 1)
                squared[0] += 1
                act.wait_ge(ssq_ready, squared[0])

            squared = [0]
            x_seen = 0
            tanhs = 0
            act.wait_ge(bank_free[0], 1)
            nc.scalar.activation(cs[:, 1, :], vec[:, VEC_A["c"]:VEC_A["c"] + KD], ACT.Tanh, scale=0.5).then_inc(tanh_ready, 1)
            tanhs += 1
            split_high(0)
            split_high(1)
            act.wait_ge(angle_ready, 1)
            nc.scalar.activation(sinr[:, :, :], angle[:, 1, :, :], ACT.Sin).then_inc(sin_ready, 1)
            nc.scalar.activation(cosr[:, :, :], angle[:, 2, :, :], ACT.Sin).then_inc(sin_ready, 1)

            for it in plan:
                kind = it["kind"]
                if kind == "turn_split":
                    b, used = it["banks"][0]
                    act.wait_ge(job_done, it["job"])
                    if it["emptied"]:
                        act.wait_ge(split_done, it["emptied"])
                    m = min(2, it["n"])
                    hi = parts(it)[0][:, it["dst0"] + it["a"]:it["dst0"] + it["a"] + m, :]
                    if it["affine"] and it["affine"][0] == "affine":
                        act.wait_ge(affine_ready, it["affine"][1] + 1)
                    for c in range(m):
                        dst, ps = full[:, b, c * S:(c + 1) * S], bank[b][:, c * S:(c + 1) * S]
                        k = it["a"] + c
                        if it["affine"] is None:
                            ins = nc.scalar.activation(dst, ps, ACT.Copy)
                        elif it["affine"][0] == "affine":
                            ins = nc.scalar.activation(dst, ps, ACT.Identity, scale=aff[:, 0, k:k + 1], bias=aff[:, 1, k:k + 1])
                        else:
                            v = N_VEC_A + it["affine"][1] + k
                            ins = nc.scalar.activation(dst, ps, ACT.Copy, scale=vec[:, v:v + 1])
                    ins.then_inc(bank_free[b], 1)
                    act.wait_ge(bank_free[b], used + 1)
                    nc.scalar.activation(hi, full[:, b, 0:m * S].rearrange("p (c s) -> p c s", c=m), ACT.Copy)\
                        .then_inc(high_copied, 1)

                elif kind == "turn":
                    b, used = it["banks"][0]
                    act.wait_ge(job_done, it["job"])
                    nc.scalar.activation(qkt[:, it["dst"]:it["dst"] + 2, :],
                                         bank[b][:, :].rearrange("p (c s) -> p c s", c=2), ACT.Copy).then_inc(bank_free[b], 1)

                elif kind in ("tokens", "hidden"):
                    n = it["tile"]
                    split_high(n + 2)
                    end = it.get("end")
                    if end is None:
                        continue
                    if end == "hidden":
                        b, used = it["banks"][0]
                        act.wait_ge(tile_done, n + 1)
                        if it["emptied"]:
                            act.wait_ge(split_done, it["emptied"])
                        link(nc.scalar.activation(full[:, b, :], bank[b][:, :], ACT.Relu))
                        nc.scalar.activation(full[:, b, :], full[:, b, :], ACT.Square).then_inc(bank_free[b], 1)
                        act.wait_ge(bank_free[b], used + 1)
                        nc.scalar.activation(hid_hi[:, it["buf"], it["c0"]:it["c0"] + 2, :],
                                             full[:, b, :].rearrange("p (c s) -> p c s", c=2), ACT.Copy).then_inc(high_copied, 1)
                    elif end[0] in ("tok", "silu"):
                        _, c0, scale, width = end
                        act.wait_ge(tile_done, n + 1)
                        for t, (b, used) in enumerate(it["banks"]):
                            nc.scalar.activation(tok[:, t, c0:c0 + width], bank[b][:, 0:width], ACT.Copy, scale=scale)\
                                .then_inc(bank_free[b], 1)
                    elif end[0] == "y_rms":
                        for t, (b, used) in enumerate(it["banks"]):
                            act.wait_ge(bank_free[b], used + 1)
                            squares(t, end[1])
                    elif end[0] == "ple":
                        act.wait_ge(tile_done, n + 1)
                        for t, (b, used) in enumerate(it["banks"]):
                            nc.scalar.activation(full[:, 2 * end[1] + t, :], bank[b][:, :], ACT.Tanh, scale=0.5)\
                                .then_inc(bank_free[b], 1)
                        for t in range(T):
                            x_seen += 1
                            act.wait_ge(x_ready, x_seen)
                            squares(t, end[1])

                elif kind == "resid" and it["s"] == 3:
                    for t in range(T):
                        act.wait_ge(resid_done, T * 3 + t + 1)
                        for n in range(2):
                            squares(t, n)

                elif kind == "gates":
                    for b in range(4):
                        act.wait_ge(bank_free[b], it["uses"][b])
                    for t in range(T):
                        nc.scalar.activation(full[:, 2 * t:2 * t + 2, :],
                                             tok[:, t, it["c0"]:it["c0"] + D].rearrange("p (a n) -> p a n", a=2),
                                             ACT.Tanh).then_inc(tanh_ready, 1)
                        tanhs += 1

                elif kind == "heads":
                    mode, spec, s0, h0 = it["mode"], it["spec"], it["s0"], it["h0"]
                    if mode == "index":
                        for i in range(len(spec)):
                            s = s0 + i
                            act.wait_ge(scores_ready, s + 1)
                            if i >= 2:
                                act.wait_ge(index_used, i - 1)
                            for t in range(T):
                                m = head_cols(mode, t)
                                ins = nc.scalar.activation(biased[:, i % 2, t, 0:m], bank[s % 4][:, t * S:t * S + m], ACT.Relu)
                            ins.then_inc(scores_used, 1)
                        continue
                    for i in range(len(spec) + 2):
                        if i < len(spec):
                            s, h = s0 + i, h0 + i
                            act.wait_ge(negmax_ready, h + 1)
                            if h >= 3:
                                act.wait_ge(probs_turned, h - 2)
                            if mode == "window":
                                hh = spec[i][4]
                                nc.scalar.activation(sink_exp[:, h % 4, :], nmx[:, h % 4, :], ACT.Exp, bias=sinks[:, 0, hh:hh + 1])
                            for t in range(T):
                                m = head_cols(mode, t)
                                src = biased[:, h % 2, t, :] if mode == "near" else bank[s % 4][:, t * S:t * S + m]
                                ins = nc.scalar.activation(probs[:, h % 3, t, 0:m], src, ACT.Exp, bias=nmx[:, h % 4, t:t + 1],
                                                           scale=1.0 if mode == "near" else SCALE,
                                                           accum_out=sums[:, h % 4, t:t + 1])
                            ins.then_inc(scores_used, 1)
                        h = h0 + i - 2
                        if i >= 2 and h % 2 == 0:
                            act.wait_ge(probs_turned, h + 1)
                            if h >= 2:
                                act.wait_ge(head_out, h - 1)
                            for dst, src in turned_halves(mode, h):
                                ins = nc.scalar.activation(dst, src, ACT.Copy)
                            ins.then_inc(turned_copied[0], 1)

        @block.tensor
        def _(pe):
            def enter(banks):
                for b, used in banks:
                    if used:
                        pe.wait_ge(bank_free[b], used)

            for it in plan:
                kind = it["kind"]
                if kind == "turn_vectors":
                    pe.wait_ge(const_in, 48)
                    pe.wait_ge(vec_in, 16 * 7)
                    b, _ = it["banks"][0]
                    nc.tensor.transpose(bank[b][:, 0:N_VEC_A], vec_rows[0:N_VEC_A, 0, :], ident[0:N_VEC_A, 0:N_VEC_A])
                    nc.tensor.transpose(bank[b][:, N_VEC_A:N_VEC_A + N_VEC_B], vec_rows[0:N_VEC_B, 1, :],
                                        ident[0:N_VEC_B, 0:N_VEC_B]).then_inc(job_done, 1)

                elif kind == "ada_columns":
                    enter(it["banks"])
                    pe.wait_ge(ada_done, 2 * it["ada"])
                    b = it["banks"][0][0]
                    for i in range(2 * KD):
                        mm = nc.tensor.matmul(bank[b][:, i:i + 1], ada_sum[:, i // KD, (i % KD) * P:(i % KD + 1) * P],
                                              const("ones")[:, 0:1], start=True, stop=True)
                    mm.then_inc(job_done, 1)

                elif kind == "gate_row":
                    enter(it["banks"])
                    pe.wait_ge(ada_done, 24 * (it["s"] + 1))
                    for n, (b, _) in enumerate(it["banks"]):
                        mm = nc.tensor.matmul(bank[b][:, :], const("ones"), ada_sum[:, 2, n * 512:(n + 1) * 512], start=True, stop=True)
                    mm.then_inc(job_done, 1)

                elif kind == "turn_split":
                    enter(it["banks"])
                    if it["wait"]:
                        pe.wait_ge(rows_ready, it["wait"])
                    if it["src"] == "o":
                        pe.wait_ge(head_copied, it["heads"])
                    if it["src"][0] == "p":
                        pe.wait_ge(p_in[it["src"][1]], 16)
                    for c in range(it["n"]):
                        b = it["banks"][c // 2][0]
                        for t in range(T):
                            o = (c % 2) * S + t * P
                            mm = nc.tensor.transpose(bank[b][:, o:o + P], source(it, t, it["a"] + c), ident)
                    mm.then_inc(job_done, 1)

                elif kind == "turn":
                    enter(it["banks"])
                    if it["wait"]:
                        pe.wait_ge(rows_ready, it["wait"])
                    for b in range(4):
                        pe.wait_ge(bank_free[b], it["before"][b])
                    for c, col in enumerate(it["cols"]):
                        b = it["banks"][c // 2][0]
                        for t in range(T):
                            o = (c % 2) * S + t * P
                            mm = nc.tensor.transpose(bank[b][:, o:o + P], tok[:, t, col:col + P], ident)
                    mm.then_inc(job_done, 1)

                elif kind == "tokens":
                    n = it["tile"]
                    if it["enter"]:
                        enter(it["banks"])
                    pe.wait_ge(split_done, it["cut"])
                    pe.wait_ge(low_done, n + 1)
                    hi, lo = view(w_hi, n), view(w_lo, n)
                    if it["lhs"] == "ht":
                        a_hi, a_lo = ht_hi[:, :, :], ht_lo[:, :, :]
                    elif it["lhs"] == "plt":
                        a_hi, a_lo = plt_hi[:, :, :], plt_lo[:, :, :]
                    else:
                        a_hi, a_lo = hid_hi[:, it["lhs"][1], :, :], hid_lo[:, it["lhs"][1], :, :]
                    for t, (b, _) in enumerate(it["banks"]):
                        dst = bank[b][:, 0:it["width"]]
                        for k in range(it["kc"]):
                            rows = slice(t * P, (t + 1) * P)
                            c = it["off"] + k
                            nc.tensor.matmul(dst, a_hi[:, c, rows], lo[:, k, :], start=it["first"] and k == 0, stop=False)
                            nc.tensor.matmul(dst, a_hi[:, c, rows], hi[:, k, :], start=False, stop=False)
                            mm = nc.tensor.matmul(dst, a_lo[:, c, rows], hi[:, k, :], start=False,
                                                  stop=it["last"] and k == it["kc"] - 1)
                    mm.then_inc(tile_done, 1)

                elif kind == "hidden":
                    n = it["tile"]
                    b, used = it["banks"][it["half"]]
                    enter([(b, used)])
                    pe.wait_ge(split_done, it["cut"])
                    pe.wait_ge(low_done, n + 1)
                    hi, lo = view(w_hi, n), view(w_lo, n)
                    for c in range(2):
                        dst = bank[b][:, c * S:(c + 1) * S]
                        for k in range(KD):
                            cols = slice(c * P, (c + 1) * P)
                            nc.tensor.matmul(dst, lo[:, k, cols], ht_hi[:, k, :], start=k == 0, stop=False)
                            nc.tensor.matmul(dst, hi[:, k, cols], ht_lo[:, k, :], start=False, stop=False)
                            mm = nc.tensor.matmul(dst, hi[:, k, cols], ht_hi[:, k, :], start=False, stop=k == KD - 1)
                    mm.then_inc(tile_done, 1)

                elif kind == "heads":
                    mode, spec, s0, h0 = it["mode"], it["spec"], it["s0"], it["h0"]
                    for b in range(8):
                        if it["uses"][b]:
                            pe.wait_ge(bank_free[b], it["uses"][b])
                    if mode == "sparse":
                        pe.wait_ge(mask_ready, 1)
                    last_lag = 0 if mode == "index" else 3
                    for i in range(len(spec) + last_lag):
                        if i < len(spec):
                            s = s0 + i
                            qc, half, kc, _, _ = spec[i]
                            part = slice(half * HD, (half + 1) * HD)
                            if s >= 4:
                                pe.wait_ge(scores_used, s - 3)
                            for t in range(T):
                                m = head_cols(mode, t)
                                masks = {"causal": [(t * P, maskb[:, 2, :])],
                                         "window": [(0, maskb[:, 2 - t:3, :].rearrange("p a n -> p (a n)"))],
                                         "sparse": [(0, smask[:, t, 0:m])]}.get(mode, [])
                                mm = nc.tensor.matmul(bank[s % 4][:, t * S:t * S + m], qkt[part, qc, t * P:(t + 1) * P],
                                                      qkt[part, kc, 0:m], start=True, stop=not masks)
                                for o, mask in masks:
                                    mm = nc.tensor.matmul(bank[s % 4][:, t * S + o:t * S + m], maskb[:, 0, :], mask,
                                                          start=False, stop=True)
                            mm.then_inc(scores_ready, 1)
                        if mode == "index":
                            continue
                        if 2 <= i < len(spec) + 2:
                            h = h0 + i - 2
                            pe.wait_ge(scores_used, s0 + i - 1)
                            if h >= 2:
                                pe.wait_ge(turned_copied[h % 2], h // 2)
                            for t in range(T):
                                for k in range(head_cols(mode, t) // P):
                                    mm = nc.tensor.transpose(bank[4 + h % 2][:, k * S + t * P:k * S + (t + 1) * P],
                                                             probs[:, h % 3, t, k * P:(k + 1) * P], ident)
                            mm.then_inc(probs_turned, 1)
                        if i >= 3:
                            h = h0 + i - 3
                            v = spec[i - 3][3]
                            pe.wait_ge(turned_copied[h % 2], h // 2 + 1)
                            if h >= 2:
                                pe.wait_ge(head_copied, h - 1)
                            for t in range(T):
                                o = t * HD
                                nk = head_cols(mode, t) // P
                                for k in range(nk):
                                    mm = nc.tensor.matmul(bank[6 + h % 2][:, o:o + HD], probs_t[:, h % 2, k, t * P:(t + 1) * P],
                                                          tok[:, k, v:v + HD], start=k == 0, stop=k == nk - 1)
                            mm.then_inc(head_out, 1)

        @block.vector
        def _(dve):
            steps = [0]

            def link(ins):
                steps[0] += 1
                ins.then_inc(dve_step, 1)
                dve.wait_ge(dve_step, steps[0])

            def split_low(n):
                if n >= len(split):
                    return
                t = split[n]
                size = t["kc"] * t["cols"]
                dve.wait_ge(high_done, n + 1)
                nc.vector.tensor_tensor(w_lo[:, n % 2, 0:size], raw_tile(t), w_hi[:, n % 2, 0:size].bitcast(F32),
                                        ALU.subtract).then_inc(low_done, 1)

            cuts = [0]

            def low_part(lo, v, hi):
                nc.vector.tensor_tensor(lo, v, hi.bitcast(F32), ALU.subtract).then_inc(split_done, 1)
                cuts[0] += 1

            def rsqrt(v, n):
                y, a, b = rstd[:, 0:n], small[:, 1, 0:n], small[:, 2, 0:n]
                link(nc.vector.tensor_scalar(bits[:, 0:n], v.bitcast(U32), 1, None, ALU.logical_shift_right))
                link(nc.vector.tensor_scalar(y.bitcast(U32), bits[:, 0:n], -1.0, RSQRT_MAGIC, ALU.mult, ALU.add))
                for _ in range(4):
                    link(nc.vector.tensor_tensor(a, y, y, ALU.mult))
                    link(nc.vector.scalar_tensor_tensor(b, a, -0.5, v, ALU.mult, ALU.mult))
                    link(nc.vector.scalar_tensor_tensor(y, b, 1.5, y, ALU.add, ALU.mult))

            def rope(it, cos, sin, groups, half):
                for n, (col, nh, dup) in enumerate(it["what"]):
                    for t in range(T):
                        w = nh * HD
                        q = tok[:, t, col:col + w]
                        ta, tb = tmp_a[:, 0:w], tmp_b[:, 0:w]
                        c = cos(t).unsqueeze(1).broadcast_to([P, nh, HD])
                        nc.vector.tensor_tensor(ta.rearrange("p (h d) -> p h d", h=nh), q.rearrange("p (h d) -> p h d", h=nh), c, ALU.mult)
                        for a in range(2):
                            qv = q.rearrange("p (h g a d) -> p h g a d", h=nh, g=groups, a=2)[:, :, :, 1 - a, :]
                            tv = tb.rearrange("p (h g a d) -> p h g a d", h=nh, g=groups, a=2)[:, :, :, a, :]
                            sv = sin(t).rearrange("p (g a d) -> p g a d", g=groups, a=2)[:, :, a, :]\
                                .unsqueeze(1).broadcast_to([P, nh, groups, half])
                            if groups == 1:
                                qv, tv, sv = qv[:, :, 0, :], tv[:, :, 0, :], sv[:, :, 0, :]
                            ins = nc.vector.tensor_tensor(tv, qv, sv, ALU.mult)
                        link(ins)
                        if dup is None:
                            ins = nc.vector.tensor_tensor(q, ta, tb, ALU.add)
                        else:
                            for r in range(2):
                                o = tok[:, t, dup:dup + 2 * w].rearrange("p (h r d) -> p h r d", h=nh, r=2)[:, :, r, :]
                                ins = nc.vector.tensor_tensor(o, ta.rearrange("p (h d) -> p h d", h=nh),
                                                              tb.rearrange("p (h d) -> p h d", h=nh), ALU.add)
                        if n == len(it["what"]) - 1 and t == T - 1:
                            ins.then_inc(rows_ready, 1)
                            dve.wait_ge(rows_ready, it["rows"])
                        else:
                            link(ins)

            def projected(it):
                for b in range(4):
                    dve.wait_ge(bank_free[b], it["uses"][b])

            turned = next(i for i in plan if i["kind"] == "turn_vectors")
            dve.wait_ge(job_done, turned["job"])
            nv = N_VEC_A + N_VEC_B
            b0 = turned["banks"][0][0]
            nc.vector.tensor_copy(vec[:, :], bank[b0][:, 0:nv]).then_inc(bank_free[b0], 1)
            dve.wait_ge(bank_free[b0], 1)
            cvec = vec[:, VEC_A["c"]:VEC_A["c"] + KD]
            link(nc.vector.tensor_scalar(cs[:, 2, :], cvec, 0.5, None, ALU.mult))
            dve.wait_ge(tanh_ready, 1)
            tanhs = 1
            nc.vector.scalar_tensor_tensor(cs[:, 0, :], cs[:, 1, :], 1.0, cs[:, 2, :], ALU.add, ALU.mult).then_inc(silu_ready, 1)
            for n in range(8):
                ada_products(dve, nc.vector, n)
            for m, name in enumerate(("ident", "window", "causal")):
                link(nc.vector.tensor_copy(maskb[:, m, :], const(name)))
            link(nc.vector.tensor_copy(pos_f[:, :], pos_i[:, :]))
            for t in range(T):
                link(nc.vector.tensor_scalar(angle[:, 0, t, :], const("invf"), pos_f[:, t:t + 1], None, ALU.mult))
            for j, turn in ((1, 0.0), (2, 0.25)):
                k = tmp_a[:, 0:T * HD]
                a0 = angle[:, 0, :, :].rearrange("p t d -> p (t d)")
                r = angle[:, j, :, :].rearrange("p t d -> p (t d)")
                link(nc.vector.tensor_scalar(k, a0, float(1 / TWO_PI), turn, ALU.mult, ALU.add))
                link(nc.vector.tensor_scalar(k, k, ROUND, -ROUND, ALU.add, ALU.add))
                link(nc.vector.scalar_tensor_tensor(r, k, -C1, a0, ALU.mult, ALU.add))
                link(nc.vector.scalar_tensor_tensor(r, k, -C2, r, ALU.mult, ALU.add))
                link(nc.vector.scalar_tensor_tensor(r, k, -C3, r, ALU.mult, ALU.add))
                link(nc.vector.tensor_scalar(r, r, float(turn * TWO_PI), 3.1415925, ALU.add, ALU.min))
                ins = nc.vector.tensor_scalar(r, r, -3.1415925, None, ALU.max)
                if j == 2:
                    ins.then_inc(angle_ready, 1)
                else:
                    link(ins)
            split_low(0)
            split_low(1)
            dve.wait_ge(sin_ready, 2)
            for t in range(T):
                link(nc.vector.tensor_tensor(sinr[:, t, :], sinr[:, t, :], const("sign"), ALU.mult))
            dve.wait_ge(misc_in, 48)
            link(nc.vector.tensor_scalar(sinks[:, 1, :], sinks[:, 0, :], -1.0, None, ALU.mult))

            resid_count = 0
            x_count = [0]
            for it in plan:
                kind = it["kind"]
                if kind == "ada_columns":
                    s = it["s"]
                    b, used = it["banks"][0]
                    dve.wait_ge(job_done, it["job"])
                    bias = vec[:, 3 * KD * s:3 * KD * s + 2 * KD]
                    nc.vector.tensor_tensor(mod[:, :], bank[b][:, 0:2 * KD], bias, ALU.add).then_inc(bank_free[b], 1)
                    dve.wait_ge(bank_free[b], used + 1)
                    shift, scale = mod[:, 0:KD], mod[:, KD:2 * KD]
                    if s == 0:
                        link(nc.vector.tensor_scalar(aff[:, 0, :], scale, 1.0, None, ALU.add))
                        nc.vector.tensor_copy(aff[:, 1, :], shift).then_inc(affine_ready, 1)
                    else:
                        g = vec[:, N_VEC_A + KD * (s - 1):N_VEC_A + KD * s]
                        lb = vec[:, N_VEC_A + 32 + KD * (s - 1):N_VEC_A + 32 + KD * s]
                        link(nc.vector.scalar_tensor_tensor(aff[:, 0, :], scale, 1.0, g, ALU.add, ALU.mult))
                        link(nc.vector.scalar_tensor_tensor(aff[:, 1, :], scale, 1.0, lb, ALU.add, ALU.mult))
                        nc.vector.tensor_tensor(aff[:, 1, :], aff[:, 1, :], shift, ALU.add).then_inc(affine_ready, 1)
                    dve.wait_ge(affine_ready, s + 1)

                elif kind == "gate_row":
                    dve.wait_ge(gate_in, 16 * (it["s"] + 1))
                    dve.wait_ge(job_done, it["job"])
                    for n, (b, used) in enumerate(it["banks"]):
                        row = gate_row[:, n * 512:(n + 1) * 512]
                        nc.vector.scalar_tensor_tensor(row, bank[b][:, :], 1.0, row, ALU.add, ALU.add).then_inc(bank_free[b], 1)
                        dve.wait_ge(bank_free[b], used + 1)

                elif kind == "turn_split":
                    dve.wait_ge(job_done, it["job"])
                    hi_all, lo_all = parts(it)
                    if len(it["banks"]) > 1:
                        b, used = it["banks"][1]
                        c0 = it["dst0"] + it["a"] + 2
                        hi, lo = hi_all[:, c0:c0 + 2, :], lo_all[:, c0:c0 + 2, :]
                        for c in range(2):
                            k = it["a"] + 2 + c
                            dst, ps = full[:, b, c * S:(c + 1) * S], bank[b][:, c * S:(c + 1) * S]
                            if it["affine"] is None:
                                ins = nc.vector.tensor_copy(dst, ps)
                            elif it["affine"][0] == "affine":
                                ins = nc.vector.tensor_scalar(dst, ps, aff[:, 0, k:k + 1], aff[:, 1, k:k + 1], ALU.mult, ALU.add)
                            else:
                                v = N_VEC_A + it["affine"][1] + k
                                ins = nc.vector.tensor_scalar(dst, ps, vec[:, v:v + 1], None, ALU.mult)
                        ins.then_inc(bank_free[b], 1)
                        dve.wait_ge(bank_free[b], used + 1)
                        v2 = full[:, b, :].rearrange("p (c s) -> p c s", c=2)
                        link(nc.vector.tensor_copy(hi, v2))
                        low_part(lo, v2, hi)
                    b, _ = it["banks"][0]
                    m = min(2, it["n"])
                    c0 = it["dst0"] + it["a"]
                    dve.wait_ge(high_copied, it["high"])
                    low_part(lo_all[:, c0:c0 + m, :], full[:, b, 0:m * S].rearrange("p (c s) -> p c s", c=m), hi_all[:, c0:c0 + m, :])

                elif kind == "turn":
                    b, _ = it["banks"][1]
                    dve.wait_ge(job_done, it["job"])
                    nc.vector.tensor_copy(qkt[:, it["dst"] + 2:it["dst"] + 4, :],
                                          bank[b][:, :].rearrange("p (c s) -> p c s", c=2)).then_inc(bank_free[b], 1)

                elif kind in ("tokens", "hidden"):
                    n = it["tile"]
                    split_low(n + 2)
                    end = it.get("end")
                    if end is None:
                        continue
                    if end == "hidden":
                        b, used = it["banks"][1]
                        dve.wait_ge(tile_done, n + 1)
                        v2 = full[:, b, :].rearrange("p (c s) -> p c s", c=2)
                        link(nc.vector.tensor_scalar(full[:, b, :], bank[b][:, :], 0.0, None, ALU.max))
                        nc.vector.tensor_tensor(full[:, b, :], full[:, b, :], full[:, b, :], ALU.mult).then_inc(bank_free[b], 1)
                        dve.wait_ge(bank_free[b], used + 1)
                        hi = hid_hi[:, it["buf"], it["c0"] + 2:it["c0"] + 4, :]
                        link(nc.vector.tensor_copy(hi, v2))
                        low_part(hid_lo[:, it["buf"], it["c0"] + 2:it["c0"] + 4, :], v2, hi)
                        b, _ = it["banks"][0]
                        dve.wait_ge(high_copied, it["high"])
                        low_part(hid_lo[:, it["buf"], it["c0"]:it["c0"] + 2, :],
                                 full[:, b, :].rearrange("p (c s) -> p c s", c=2),
                                 hid_hi[:, it["buf"], it["c0"]:it["c0"] + 2, :])
                    elif end[0] == "y_ln":
                        dve.wait_ge(tile_done, n + 1)
                        cols = slice(end[1] * 512, (end[1] + 1) * 512)
                        for t, (b, used) in enumerate(it["banks"]):
                            nc.vector.tensor_tensor(tmp_a[:, :], bank[b][:, :], gate_row[:, cols], ALU.mult).then_inc(bank_free[b], 1)
                            dve.wait_ge(bank_free[b], used + 1)
                            link(nc.vector.scalar_tensor_tensor(u[:, t, cols], x[:, t, cols], ALPHA, tmp_a[:, :], ALU.mult, ALU.add))
                            link(nc.vector.bn_stats(stats[:, t, end[1], :], u[:, t, cols]))
                    elif end[0] == "y_rms":
                        dve.wait_ge(tile_done, n + 1)
                        cols = slice(end[1] * 512, (end[1] + 1) * 512)
                        for t, (b, used) in enumerate(it["banks"]):
                            nc.vector.tensor_tensor(x[:, t, cols], bank[b][:, :], x[:, t, cols], ALU.add).then_inc(bank_free[b], 1)
                            dve.wait_ge(bank_free[b], used + 1)
                    elif end[0] == "ple":
                        cols = slice(end[1] * 512, (end[1] + 1) * 512)
                        for t, (b, used) in enumerate(it["banks"]):
                            dve.wait_ge(bank_free[b], used + 1)
                            link(nc.vector.scalar_tensor_tensor(tmp_a[:, :], full[:, 2 * end[1] + t, :], 1.0, tok[:, t, cols], ALU.add, ALU.mult))
                            nc.vector.tensor_tensor(x[:, t, cols], x[:, t, cols], tmp_a[:, :], ALU.add).then_inc(x_ready, 1)
                            x_count[0] += 1
                            dve.wait_ge(x_ready, x_count[0])

                elif kind == "ln":
                    for t in range(T):
                        link(nc.vector.bn_aggr(meanvar[:, t, :], stats[:, t, :, :]))
                    link(nc.vector.tensor_scalar(small[:, 0, 0:T], meanvar[:, :, 1], LN_EPS, None, ALU.add))
                    rsqrt(small[:, 0, 0:T], T)
                    for t in range(T):
                        nc.vector.tensor_scalar(u[:, t, :], u[:, t, :], meanvar[:, t, 0:1], rstd[:, t:t + 1],
                                                ALU.subtract, ALU.mult).then_inc(rows_ready, 1)
                        dve.wait_ge(rows_ready, it["rows"] - T + t + 1)

                elif kind == "resid":
                    dve.wait_ge(row_in, 32 * (it["s"] + 1))
                    for t in range(T):
                        link(nc.vector.tensor_tensor(x[:, t, :], u[:, t, :], g_row[:, :], ALU.mult))
                        nc.vector.tensor_tensor(x[:, t, :], x[:, t, :], b_row[:, :], ALU.add).then_inc(resid_done, 1)
                        resid_count += 1
                        dve.wait_ge(resid_done, resid_count)

                elif kind in ("rms", "final"):
                    dve.wait_ge(ssq_ready, it["ssq"])
                    v = small[:, 0, 0:T]
                    link(nc.vector.tensor_tensor(v, ssq[:, :, 0], ssq[:, :, 1], ALU.add))
                    link(nc.vector.tensor_scalar(v, v, 1.0 / D, RMS_EPS, ALU.mult, ALU.add))
                    rsqrt(v, T)
                    if kind == "final":
                        dve.wait_ge(final_in, 16)
                    for t in range(T):
                        if kind == "rms":
                            ins = nc.vector.tensor_scalar(u[:, t, :], x[:, t, :], rstd[:, t:t + 1], None, ALU.mult)
                        else:
                            ins = nc.vector.scalar_tensor_tensor(u[:, t, :], x[:, t, :], rstd[:, t:t + 1], g_final[:, :], ALU.mult, ALU.mult)
                        ins.then_inc(rows_ready, 1)
                        dve.wait_ge(rows_ready, it["rows"] - T + t + 1)

                elif kind == "low_rank":
                    projected(it)
                    for t in range(T):
                        cq = tok[:, t, 768:1024]
                        link(nc.vector.tensor_tensor(tmp_a[:, 0:256], cq, cq, ALU.mult))
                        link(nc.vector.tensor_reduce(small[:, 0, t:t + 1], tmp_a[:, 0:256], AX, ALU.add))
                    v = small[:, 0, 0:T]
                    link(nc.vector.tensor_scalar(v, v, 1.0 / 256, RMS_EPS, ALU.mult, ALU.add))
                    rsqrt(v, T)
                    for t in range(T):
                        ins = nc.vector.tensor_scalar(tok[:, t, 768:1024], tok[:, t, 768:1024], rstd[:, t:t + 1], None, ALU.mult)
                        if t == T - 1:
                            ins.then_inc(rows_ready, 1)
                            dve.wait_ge(rows_ready, it["rows"])

                elif kind == "rope":
                    projected(it)
                    rope(it, lambda t: cosr[:, t, :], lambda t: sinr[:, t, :], 1, HD // 2)

                elif kind == "qk_rope":
                    projected(it)
                    g = 0 if it["gain"] == "q" else 1
                    col, nh, _ = it["what"][0]
                    w = nh * HD
                    for t in range(T):
                        q = tok[:, t, col:col + w]
                        link(nc.vector.tensor_tensor(tmp_a[:, 0:w], q, q, ALU.mult))
                        link(nc.vector.tensor_reduce(small[:, 0, t * nh:(t + 1) * nh], tmp_a[:, 0:w].rearrange("p (h d) -> p h d", h=nh), AX, ALU.add))
                    v = small[:, 0, 0:T * nh]
                    link(nc.vector.tensor_scalar(v, v, 1.0 / HD, RMS_EPS, ALU.mult, ALU.add))
                    rsqrt(v, T * nh)
                    for t in range(T):
                        q = tok[:, t, col:col + w].rearrange("p (h d) -> p h d", h=nh)
                        link(nc.vector.tensor_tensor(q, q, rstd[:, t * nh:(t + 1) * nh].unsqueeze(2).broadcast_to([P, nh, HD]), ALU.mult))
                    rope(it, lambda t: ax[:, g, 0, t, :], lambda t: ax[:, g, 1, t, :], 2, HD // 4)

                elif kind == "axial_tables":
                    for g in range(2):
                        for t in range(T):
                            cs_t = const("axcos")[:, t * HD:(t + 1) * HD]
                            sn_t = const("axsin")[:, t * HD:(t + 1) * HD].rearrange("p (g a d) -> p g a d", g=2, a=2)
                            gv = gain[:, g, :].rearrange("p (g a d) -> p g a d", g=2, a=2)
                            dst = ax[:, g, 1, t, :].rearrange("p (g a d) -> p g a d", g=2, a=2)
                            link(nc.vector.tensor_tensor(ax[:, g, 0, t, :], cs_t, gain[:, g, :], ALU.mult))
                            for a in range(2):
                                link(nc.vector.tensor_tensor(dst[:, :, a, :], sn_t[:, :, a, :], gv[:, :, 1 - a, :], ALU.mult))

                elif kind == "bias_table":
                    dve.wait_ge(bias_in, 16 * P)
                    for h in range(16):
                        nb = near_bias[:, h, :].rearrange("p (r k) -> p r k", r=6)
                        ins = nc.vector.tensor_tensor(nb, nb, const("near").unsqueeze(1).broadcast_to([P, 6, GRID]), ALU.add)
                    ins.then_inc(rows_ready, 1)
                    dve.wait_ge(rows_ready, it["rows"])

                elif kind == "gates":
                    for t in range(T):
                        tanhs += 1
                        dve.wait_ge(tanh_ready, tanhs)
                        gv = tok[:, t, it["c0"]:it["c0"] + D].rearrange("p (a n) -> p a n", a=2)
                        link(nc.vector.scalar_tensor_tensor(gv, full[:, 2 * t:2 * t + 2, :], 1.0, gv, ALU.add, ALU.mult))

                elif kind == "heads":
                    mode, spec, s0, h0 = it["mode"], it["spec"], it["s0"], it["h0"]
                    if mode == "index":
                        link(nc.vector.tensor_scalar(iw[:, :, :], tok[:, :, 1216:1224], IW_SCALE, None, ALU.mult))
                        for i in range(len(spec)):
                            dve.wait_ge(scores_used, s0 + i + 1)
                            for t in range(T):
                                m = head_cols(mode, t)
                                src, w = biased[:, i % 2, t, 0:m], iw[:, t, i:i + 1]
                                if i == 0:
                                    ins = nc.vector.tensor_scalar(score[:, t, 0:m], src, w, None, ALU.mult)
                                else:
                                    ins = nc.vector.scalar_tensor_tensor(score[:, t, 0:m], src, w, score[:, t, 0:m], ALU.mult, ALU.add)
                            ins.then_inc(index_used, 1)
                            dve.wait_ge(index_used, i + 1)
                        for t in range(T):
                            own = score[:, t, t * P:(t + 1) * P]
                            link(nc.vector.tensor_tensor(own, own, const("causal"), ALU.add))
                        continue
                    for i in range(len(spec) + 3):
                        if i < len(spec):
                            s, h = s0 + i, h0 + i
                            dve.wait_ge(scores_ready, s + 1)
                            if mode == "near":
                                if i >= 2:
                                    dve.wait_ge(scores_used, s - 1)
                                for t in range(T):
                                    o = (2 - 2 * t) * GRID
                                    ins = nc.vector.scalar_tensor_tensor(biased[:, h % 2, t, :], bank[s % 4][:, t * S:(t + 1) * S], SCALE,
                                                                         near_bias[:, spec[i][4], o:o + S], ALU.mult, ALU.add)
                                link(ins)
                                link(nc.vector.tensor_reduce(mx[:, h % 4, :], biased[:, h % 2, :, :], AX, ALU.max))
                            elif mode == "full":
                                link(nc.vector.tensor_reduce(mx[:, h % 4, :], bank[s % 4][:, :].rearrange("p (t k) -> p t k", t=T), AX, ALU.max))
                            else:
                                for t in range(T):
                                    ins = nc.vector.tensor_reduce(mx[:, h % 4, t:t + 1], bank[s % 4][:, t * S:t * S + head_cols(mode, t)], AX, ALU.max)
                                link(ins)
                            if mode == "window":
                                hh = spec[i][4]
                                nc.vector.tensor_scalar(nmx[:, h % 4, :], mx[:, h % 4, :], -SCALE, sinks[:, 1, hh:hh + 1],
                                                        ALU.mult, ALU.min).then_inc(negmax_ready, 1)
                            else:
                                nc.vector.tensor_scalar(nmx[:, h % 4, :], mx[:, h % 4, :], -1.0 if mode == "near" else -SCALE, None,
                                                        ALU.mult).then_inc(negmax_ready, 1)
                        h = h0 + i - 2
                        if 2 <= i < len(spec) + 2 and h % 2:
                            dve.wait_ge(probs_turned, h + 1)
                            if h >= 2:
                                dve.wait_ge(head_out, h - 1)
                            for dst, src in turned_halves(mode, h):
                                ins = nc.vector.tensor_copy(dst, src)
                            ins.then_inc(turned_copied[1], 1)
                        if i >= 3:
                            h = h0 + i - 3
                            hh = spec[i - 3][4]
                            dve.wait_ge(scores_used, s0 + i - 2)
                            if mode == "window":
                                link(nc.vector.tensor_tensor(sums[:, h % 4, :], sums[:, h % 4, :], sink_exp[:, h % 4, :], ALU.add))
                            link(nc.vector.reciprocal(rs[:, h % 4, :], sums[:, h % 4, :]))
                            dve.wait_ge(head_out, h + 1)
                            ps = bank[6 + h % 2][:, 0:P].rearrange("p (t d) -> p t d", t=T)
                            if "gate" in it:
                                for t in range(T):
                                    gc = it["gate"] + hh * HD
                                    ins = nc.vector.scalar_tensor_tensor(u[:, t, hh * HD:(hh + 1) * HD], ps[:, t, :], rs[:, h % 4, t:t + 1],
                                                                         tok[:, t, gc:gc + HD], ALU.mult, ALU.mult)
                            else:
                                ins = nc.vector.tensor_tensor(u[:, :, hh * HD:(hh + 1) * HD], ps,
                                                              rs[:, h % 4, :].unsqueeze(2).broadcast_to([P, T, HD]), ALU.mult)
                            ins.then_inc(head_copied, 1)
                        if mode == "window" and i < 8:
                            for r in (2 * i, 2 * i + 1):
                                t = r // 8
                                sc = score[:, t, 0:P * (t + 1)]
                                link(nc.vector.max(top8[:, :], sc))
                                link(nc.vector.match_replace(sc, top8[:, :], sc, PICKED))
                            if i == 7:
                                for t in range(T):
                                    m = P * (t + 1)
                                    link(nc.vector.tensor_scalar(smask[:, t, 0:m], score[:, t, 0:m], PICKED / 2, MASKED, ALU.is_gt, ALU.mult))
                                    own = smask[:, t, t * P:m]
                                    ins = nc.vector.tensor_tensor(own, own, maskb[:, 2, :], ALU.min)
                                    if t == 0:
                                        link(ins)
                                ins.then_inc(mask_ready, 1)


_INS = ["x", "c", "positions", "ab_w_in", "ab_q_norm", "ab_w_uq", "ab_w_uiq", "ab_sinks", "ab_w_out", "c_w_in", "c_w_out",
        "ada_w", "ada_b", "ln_g", "ln_b", "mlp_w1", "mlp_w2", "p_2", "norm_g_2", "a_w_in_2", "a_rpb_2", "a_w_out_2",
        "b_w_in_2", "b_q_norm_2", "b_k_norm_2", "b_w_out_2", "ple_norm_g_2", "ple_w_gate_2", "ple_w_proj_2", "final_norm_g_2"]


def kernel(**inputs):
    import concourse.bacc as bacc
    from concourse.bass_utils import run_bass_kernel_spmd

    nc = bacc.Bacc("TRN2", target_bir_lowering=False, num_devices=1)
    arrays, rows = {}, {}
    for name in _INS:
        a = np.ascontiguousarray(inputs[name])
        arrays[f"in_{name}"] = a
        rows[name] = nc.dram_tensor(f"in_{name}", a.shape, mybir.dt.from_np(a.dtype), kind="ExternalInput").ap()
    arrays["in_consts"] = constants()
    rows["consts"] = nc.dram_tensor("in_consts", (P, N_CONST), F32, kind="ExternalInput").ap()
    out = nc.dram_tensor("out_0", (1, S, D), F32, kind="ExternalOutput").ap()
    toeplitz = nc.dram_tensor("toeplitz", (16, 7, 128), F32, kind="Internal")
    block_kernel(nc, rows, out, toeplitz)
    r = run_bass_kernel_spmd(nc, [arrays], core_ids=[0])
    return r.results[0]["out_0"]
```

```python
from contextlib import ExitStack

import numpy as np

import concourse.bass as bass
from concourse import mybir

F32 = mybir.dt.float32
F32R = mybir.dt.float32r
BF16 = mybir.dt.bfloat16
I32 = mybir.dt.int32
U32 = mybir.dt.uint32
ALU = mybir.AluOpType
ACT = mybir.ActivationFunctionType
AX = mybir.AxisListType.X

P = 128
S = 256
T = S // P
D = 1024
KD = D // P
HD = 64
FF = 4 * D
N_SUB = 4
ALPHA = 4 ** 0.25
LN_EPS = 1e-5
RMS_EPS = 1e-6
SCALE = HD ** -0.5
MASKED = -1e30
PICKED = -3e38
TOPK = 64
GRID = 64
IW_SCALE = 8 ** -0.5 * HD ** -0.5
TWO_PI = 2 * np.pi
C1 = 6.28125
C2 = float(np.float32(np.round((TWO_PI - C1) * 2 ** 20) / 2 ** 20))
C3 = float(np.float32(TWO_PI - C1 - C2))
ROUND = 1.5 * 2 ** 23
RSQRT_MAGIC = float(0x5F3759DF)

TILE = 2048
RAW_SLOTS = 5
HIGH_SLOTS = 3

CONST = {}
_at = 0
for _name, _n in (("ident", P), ("ones", P), ("causal", P), ("window", P), ("invf", HD), ("sign", HD),
                  ("axcos", T * HD), ("axsin", T * HD), ("near", GRID)):
    CONST[_name] = (_at, _at + _n)
    _at += _n
N_CONST = _at

VEC_A = {"ada_b": 0, "c": 96}
N_VEC_A = 104
VEC_B = {"ln_g": 0, "ln_b": 32, "norm_g": 64, "ple_g": 80, "q_norm": 96}
N_VEC_B = 98


def constants():
    out = np.zeros((P, N_CONST), np.float32)

    def put(name, value):
        a, b = CONST[name]
        out[:, a:b] = value

    row = np.arange(P)[:, None]
    col = np.arange(P)[None, :]
    put("ident", np.eye(P))
    put("ones", 1.0)
    put("causal", np.where(col <= row, 0.0, MASKED))
    put("window", np.where(col > row, 0.0, MASKED))
    inv = 10000.0 ** (-np.arange(0, HD, 2) / HD)
    put("invf", np.concatenate([inv, inv])[None, :])
    put("sign", np.concatenate([-np.ones(HD // 2), np.ones(HD // 2)])[None, :])
    quarter = HD // 4
    inv = 10000.0 ** (-np.arange(quarter) * 2.0 / (HD // 2))
    token = np.arange(S).reshape(T, P).T
    ang = np.stack([(token // GRID)[:, :, None] * inv, (token % GRID)[:, :, None] * inv], 2)
    put("axcos", np.stack([np.cos(ang), np.cos(ang)], 3).reshape(P, T * HD))
    put("axsin", np.stack([-np.sin(ang), np.sin(ang)], 3).reshape(P, T * HD))
    c = np.arange(P)[:, None] % GRID
    start = np.clip(c - 8, 0, GRID - 16)
    key = np.arange(GRID)[None, :]
    put("near", np.where((key >= start) & (key < start + 16), 0.0, MASKED))
    return out


def make_plan(R):
    plan, tiles = [], []
    count = {"split": 0, "ada": 0, "job": 0, "rows": 0, "cut": 0, "head": 0, "score": 0, "ssq": 0, "high": 0, "x": 0, "half": 0}
    cuts = {}
    uses = [0] * 8
    cut_of = {}
    pair = [0]
    updated = {}
    gate_jobs = []

    def tick(name, n=1):
        count[name] += n
        return count[name]

    def rows():
        return tick("rows")

    def add(kind, **k):
        plan.append({"kind": kind, **k})
        return plan[-1]

    def banks(pairs=None):
        if pairs is None:
            b = 2 * (pair[0] % 2)
            pair[0] += 1
            pairs = (b, b + 1)
        got = [(b, uses[b]) for b in pairs]
        for b in pairs:
            uses[b] += 1
        return got

    ride = [0, 1, 0]

    def tile(view, kc, cols, kind):
        if kind == "split" and ride[0]:
            ride[2] += 1
            if ride[2] % ride[1] == 0:
                ride[0] -= 1
                ada_tiles(1)
                tiles[-1]["riding"] = True
        tiles.append({"view": view, "kc": kc, "cols": cols, "kind": kind, "n": tick(kind) - 1})
        return tiles[-1]["n"]

    def job(kind, **k):
        return add(kind, banks=banks(), job=tick("job"), **k)

    def linear(w, c0, width, kc, lhs, end, between=None):
        bk = banks()
        step = min(4, kc)
        v = w.rearrange("(k p) n -> p k n", p=P)
        for h in range(kc // step):
            n = tile(v[:, h * step:(h + 1) * step, c0:c0 + width], step, width, "split")
            last = h == kc // step - 1
            it = add("tokens", tile=n, kc=step, width=width, lhs=lhs, off=h * step, banks=bk,
                     first=h == 0, last=last, cut=cuts[lhs][h], enter=h == 0, half=tick("half"))
            if h == 0 and between:
                between()
                pair[0] += 1
            if last:
                it["end"] = end
        return it

    def split_rows(src, chunks, dst, wait, affine=None, dst0=0, first=0):
        for a in range(first, chunks, 4):
            n = min(4, chunks - a)
            nb = (n + 1) // 2
            it = job("turn_split", src=src, a=a, n=n, dst=dst, dst0=dst0, wait=wait, affine=affine)
            if src == "x" and updated:
                it["updated"] = updated[a // 4]
            it["banks"] = it["banks"][:nb]
            if nb == 1:
                uses[it["banks"][0][0] + 1] -= 1
            it["heads"] = count["head"] - (8 if a == 0 else 0)
            it["high"] = tick("high")
            it["emptied"] = cut_of.get(it["banks"][0][0], 0)
            tick("cut", nb)
            cut_of[it["banks"][0][0]] = count["cut"]
            cuts[dst] = (count["cut"] if a == 0 else cuts[dst][0], count["cut"])

    def rows_linear(rows_of, of, norm=None):
        src, chunks, dst, wait, affine = rows_of

        def between():
            split_rows(src, chunks, dst, wait, affine, first=4)
            if src == "xhat":
                add("resid", s=3)
                tick("ssq", 4)
            if norm is not None:
                norm_rms(norm)

        split_rows(src, 4, dst, wait, affine)
        return linear(*of, between=between)

    def gate(s):
        gate_jobs.append(count["job"] + 1)
        return job("gate_row", s=s)

    def turn(src_cols, dst, wait):
        before = list(uses)
        for a in range(0, len(src_cols), 4):
            job("turn", cols=src_cols[a:a + 4], dst=dst + a, wait=wait, before=before)

    def heads(kind, spec):
        it = add("heads", mode=kind, spec=spec, s0=count["score"], h0=count["head"], uses=list(uses))
        tick("score", len(spec))
        if kind != "index":
            tick("head", len(spec))
        return it

    def ada_tiles(n):
        for i in range(count["ada"], count["ada"] + n):
            s, part, k = i // 12, i // 4 % 3, i % 4
            w = R["ada_w"][s // 2, s % 2].rearrange("(k p) n -> p k n", p=P)
            tile(w[:, 2 * k:2 * k + 2, part * D:(part + 1) * D], 2, D, "ada")
            tiles[-1].update(s=s, part=part, k=2 * k)

    def spread(n, every):
        ride[:] = [n, every, 0]

    def ada(s):
        it = add("ada_columns", s=s, banks=banks((4,)), job=tick("job"))
        it["ada"] = 12 * s + 8

    def mlp(layer, end):
        w1 = R["mlp_w1"][layer].rearrange("(k p) n -> p k n", p=P)
        w2 = R["mlp_w2"][layer].rearrange("(k p) n -> p k n", p=P)
        yb = {n: banks((4 + 2 * n, 5 + 2 * n)) for n in range(2)}
        hid_cut = {}
        enter = {0: True, 1: True}
        need = cuts["ht"]

        def up(g):
            for j in range(2):
                bk = banks()
                for h in range(2):
                    c0 = g * 1024 + j * 512 + h * 256
                    n = tile(w1[:, :, c0:c0 + 256], KD, 256, "split")
                    it = add("hidden", tile=n, half=h, banks=bk, cut=need, buf=g % 2, c0=4 * j)
                it["end"] = "hidden"
                it["high"] = tick("high")
                it["emptied"] = cut_of.get(bk[0][0], 0)
                tick("cut", 2)
                cut_of[bk[0][0]] = count["cut"]
            hid_cut[g] = count["cut"]

        def down(g):
            for n in range(2):
                for h in range(2):
                    k0 = g * 8 + h * 4
                    t = tile(w2[:, k0:k0 + 4, n * 512:(n + 1) * 512], 4, 512, "split")
                    it = add("tokens", tile=t, kc=4, width=512, lhs=("hid", g % 2), off=h * 4, banks=yb[n],
                             first=g == 0 and h == 0, last=g == 3 and h == 1, cut=hid_cut[g], enter=g == 0 and h == 0, half=tick("half"))
                if g == 3:
                    it["end"] = ("y_ln", n, 2 * layer + 1)

        up(0)
        gate(2 * layer + 1)
        if layer == 0:
            spread(12, 2)
        up(1), down(0), up(2), down(1), up(3), down(2), down(3)

    def norm_ln(s):
        it = add("ln", s=s)
        it["rows"] = tick("rows", 2)
        return it["rows"]

    def norm_rms(i):
        add("rms", ssq=count["ssq"], i=i)

    def y_rms(w):
        for n in range(2):
            of = (w, n * 512, 512, KD, "ht", ("y_rms", n))
            it = linear(*of) if n else rows_linear(("o", KD, "ht", 0, None), of)
            updated[n] = ("bank", [(b, used + 1) for b, used in it["banks"]])
            tick("ssq", 2)

    job("turn_vectors")
    uses[1] -= 1
    ada_tiles(8)
    spread(4, 2)
    w = R["ab_w_in"][0]
    split_rows("x", KD, "ht", 0, ("affine", 0))
    ada(0)
    linear(w, 512, 512, KD, "ht", ("tok", 512, 1.0, 512))
    add("rope_tables")
    add("low_rank", rows=rows(), uses=list(uses))
    cq_rows = count["rows"]
    linear(w, 1024, 200, KD, "ht", ("tok", 1024, 1.0, 200))
    add("rope", what=[(512, 2, 2304), (1024, 1, 2560), (1152, 1, 2688)], table="text", rows=rows(), uses=list(uses))
    linear(w, 0, 512, KD, "ht", ("tok", 0, 1.0, 512), between=lambda: split_rows("cq", 2, "plt", cq_rows, ("vec", VEC_B["q_norm"])))
    add("rope", what=[(0, 8, None)], table="text", rows=rows(), uses=list(uses))
    aq_rows = count["rows"]
    linear(R["ab_w_uiq"][0], 0, 512, 2, "plt", ("tok", 1792, 1.0, 512))
    add("rope", what=[(1792, 8, None)], table="text", rows=rows(), uses=list(uses))
    biq_rows = count["rows"]
    linear(R["ab_w_uq"][0], 0, 512, 2, "plt", ("tok", 1280, 1.0, 512))
    add("rope", what=[(1280, 8, None)], table="text", rows=rows(), uses=list(uses))
    ada_tiles(12)
    turn([0, 128, 256, 384, 2304, 2432, 2560, 2688], 0, aq_rows)
    turn([1792, 1920, 2048, 2176], 12, biq_rows)
    turn([1280, 1408, 1536, 1664], 8, count["rows"])
    gate(0)
    heads("index", [(12 + h // 2, h % 2, 7, None, h) for h in range(8)])
    heads("window", [(h // 2, h % 2, 4 + h // 4, 640 + HD * (h // 4), h) for h in range(8)])
    heads("sparse", [(8 + h // 2, h % 2, 6, 1088, 8 + h) for h in range(8)])
    rows_linear(("o", KD, "ht", 0, None), (R["ab_w_out"][0], 0, 512, KD, "ht", ("y_ln", 0, 0)))
    linear(R["ab_w_out"][0], 512, 512, KD, "ht", ("y_ln", 1, 0))
    r = norm_ln(0)
    ada(1)
    split_rows("xhat", KD, "ht", r, ("affine", 1))
    mlp(0, None)
    r = norm_ln(1)
    ada(2)
    split_rows("xhat", KD, "ht", r, ("affine", 2))
    w = R["c_w_in"][0]
    for j in range(4):
        linear(w, j * 512, 512, KD, "ht", ("tok", j * 512, 1.0, 512))
        add("rope", what=[(j * 512, 8, None)], table="text", rows=rows(), uses=list(uses))
        if j == 0:
            gate(2)
            spread(8, 2)
    for j in range(4, 6):
        linear(w, j * 512, 512, KD, "ht", ("tok", j * 512, 1.0, 512))
    ada_tiles(4)
    turn([P * i for i in range(16)], 0, count["rows"])
    heads("causal", [(h // 2, h % 2, 8 + h // 2, 2048 + HD * h, h) for h in range(16)])
    rows_linear(("o", KD, "ht", 0, None), (R["c_w_out"][0], 0, 512, KD, "ht", ("y_ln", 0, 2)))
    linear(R["c_w_out"][0], 512, 512, KD, "ht", ("y_ln", 1, 2))
    r = norm_ln(2)
    ada(3)
    split_rows("xhat", KD, "ht", r, ("affine", 3))
    mlp(1, None)
    last_rows = norm_ln(3)
    for i in range(2):
        r = 2 * i
        if i == 0:
            w = R["a_w_in_2"][0]
            for j in range(6):
                of = (w, j * 512, 512, KD, "ht", ("tok", j * 512, (r, 0), 512))
                linear(*of) if j else rows_linear(("xhat", KD, "ht", last_rows, ("affine", 4)), of, norm=r)
                if j == 2:
                    add("bias_table", rows=rows(), part=0)
            for j in range(6, 8):
                linear(w, j * 512, 512, KD, "ht", ("silu", j * 512, (r, 1), 512))
            add("bias_table", rows=rows(), part=1)
            add("gates", c0=3072, uses=list(uses))
            turn([P * j for j in range(16)], 0, count["rows"])
            heads("near", [(h // 2, h % 2, 8 + h // 2, 2048 + HD * h, h) for h in range(16)])["gate"] = 3072
        else:
            w = R["b_w_in_2"][0]
            rows_linear(("x", KD, "ht", 0, ("vec", VEC_B["norm_g"] + KD * i)),
                        (w, 1024, 512, KD, "ht", ("tok", 1024, (r, 0), 512)), norm=r)
            add("axial_tables")
            add("qk_rope", what=[(1024, 4, 2560)], gain="k", rows=rows(), uses=list(uses))
            for j in range(2):
                linear(w, j * 512, 512, KD, "ht", ("tok", j * 512, (r, 0), 512))
                add("qk_rope", what=[(j * 512, 8, None)], gain="q", rows=rows(), uses=list(uses))
            for j in range(3, 5):
                linear(w, j * 512, 512, KD, "ht", ("silu", j * 512, (r, 1), 512))
            add("gates", c0=1536, uses=list(uses))
            turn([P * j for j in range(8)] + [2560 + P * j for j in range(4)], 0, count["rows"])
            heads("full", [(h // 2, h % 2, 8 + h // 4, 1280 + HD * (h // 4), h) for h in range(16)])["gate"] = 1536
        y_rms(R[("a" if i == 0 else "b") + "_w_out_2"][0])
        split_rows(("p", i), 2, "plt", 0)
        for n in range(2):
            linear(R["ple_w_proj_2"][i], n * 512, 512, 2, "plt", ("tok", n * 512, 0.5, 512))
        r = 2 * i + 1
        for n in range(2):
            of = (R["ple_w_gate_2"][i], n * 512, 512, KD, "ht", ("ple", n, r))
            it = linear(*of) if n else rows_linear(("x", KD, "ht", 0, ("vec", VEC_B["ple_g"] + KD * i)), of, norm=r)
            it["x"] = tick("x", 2)
            updated[n] = ("x", it["x"])
            tick("ssq", 2)
    add("final", ssq=count["ssq"], rows=tick("rows", 2))
    for it, after in zip(plan, plan[1:]):
        if "tile" in it:
            late = after["kind"] in ("turn_split", "ln", "turn", "rms", "ada_columns", "heads")
            it["ahead"] = it["tile"] + (1 if late else 2)
    assert ride[0] == 0 and count["ada"] == 12 * N_SUB
    split = [t for t in tiles if t["kind"] == "split"]
    order = tiles[:8] + split[:2]
    for t in tiles[8:]:
        if t["kind"] == "ada":
            order.append(t)
        elif t["n"] + 2 < len(split):
            order.append(split[t["n"] + 2])
    for i, t in enumerate(tiles):
        t["turn"] = i + (2.5 if t.get("riding") else 0)
    held, filled = [None] * RAW_SLOTS, [0] * RAW_SLOTS
    for t in order:
        slot = min(range(RAW_SLOTS), key=lambda i: (held[i]["turn"] if held[i] else -1, i))
        filled[slot] += 1
        t["slot"], t["full"], t["old"] = slot, 16 * filled[slot], held[slot]
        held[slot] = t
    adas = [t for t in tiles if t["kind"] == "ada"]
    for t in adas:
        if t["s"]:
            t["gate_job"] = gate_jobs[t["s"] - 1]
            t["columns_job"] = next(i["job"] for i in plan if i["kind"] == "ada_columns" and i["s"] == t["s"] - 1)
    return plan, order, split, adas


def block_kernel(nc, R, out, toeplitz):
    plan, order, split, adas = make_plan(R)
    p_after = [i["h0"] + len(i["spec"]) for i in plan if i["kind"] == "heads" and i["mode"] in ("near", "full")]

    with ExitStack() as ctx:
        def sb(name, shape, dt=F32):
            return ctx.enter_context(nc.sbuf_tensor(name, shape, dt))

        def sem(name):
            return ctx.enter_context(nc.semaphore(name))

        x = sb("x", [P, T, D])
        u = sb("u", [P, T, D])
        ht_hi = sb("ht_hi", [P, KD, S], F32R)
        ht_lo = sb("ht_lo", [P, KD, S], F32R)
        plt_hi = sb("plt_hi", [P, 2, S], F32R)
        plt_lo = sb("plt_lo", [P, 2, S], F32R)
        tok = sb("tok", [P, T, 4 * D])
        qkt = sb("qkt", [P, 16, S])
        near_bias = sb("near_bias", [P, 16, 6 * GRID])
        raw = sb("raw", [P, RAW_SLOTS, TILE])
        w_hi = sb("w_hi", [P, HIGH_SLOTS, TILE], F32R)
        full = sb("full", [P, 4, 512])
        probs = sb("probs", [P, 3, T, S])
        probs_t = sb("probs_t", [P, 2, T, S])
        biased = sb("biased", [P, 2, T, S])
        tmp_a = sb("tmp_a", [P, 512])
        tmp_b = sb("tmp_b", [P, 512])
        consts = sb("consts", [P, N_CONST])
        vec = sb("vec", [P, N_VEC_A + N_VEC_B])
        cs = sb("cs", [P, 3, KD])
        mod = sb("mod", [P, 2 * KD])
        aff = sb("aff", [P, 2, KD])
        pos_i = sb("pos_i", [P, T], I32)
        pos_f = sb("pos_f", [P, T])
        cosr = sb("cosr", [P, T, HD])
        sinr = sb("sinr", [P, T, HD])
        gain = sb("gain", [P, 2, HD])
        stats = sb("stats", [P, T, 2, 6])
        meanvar = sb("meanvar", [P, T, 2])
        ssq = sb("ssq", [P, T, 2])
        rms = sb("rms", [P, 4, 2, T])
        small = sb("small", [P, 3, 16])
        bits = sb("bits", [P, 16], U32)
        rstd = sb("rstd", [P, 16])
        sinks = sb("sinks", [P, 2, 8])
        mx = sb("mx", [P, 4, T])
        nmx = sb("nmx", [P, 4, T])
        sums = sb("sums", [P, 4, T])
        rs = sb("rs", [P, 4, T])
        sink_exp = sb("sink_exp", [P, 4, T])
        iw = sb("iw", [P, T, 8])
        top8 = sb("top8", [P, 8])
        maskb = sb("maskb", [P, 3, P], BF16)
        smask = sb("smask", [P, T, S], BF16)

        def over(owner, offset, name, shape, dt=F32):
            return nc.alloc_sbuf_tensor_at(name, shape, dt, offset=nc.lookup_mloc(owner).addr + offset)

        w_lo = over(raw, 0, "w_lo", [P, RAW_SLOTS, TILE], F32R)
        hid_hi = over(tok, 0, "hid_hi", [P, 2, KD, S], F32R)
        hid_lo = over(tok, 2 * KD * S * 4, "hid_lo", [P, 2, KD, S], F32R)
        g_row = over(near_bias, 0, "g_row", [P, D])
        b_row = over(near_bias, 4 * D, "b_row", [P, D])
        gate_row = over(near_bias, 8 * D, "gate_row", [P, D])
        ada_sum = over(near_bias, 12 * D, "ada_sum", [P, 3, D])
        score = over(plt_hi, 0, "score", [P, T, S])
        near_rev = over(qkt, 0, "near_rev", [P, 48, GRID])
        rpb_rows = over(qkt, 12 * D, "rpb_rows", [16, 7, 128])
        rpb_in_rows = over(probs_t, 0, "rpb_in_rows", [16, 7, 31])
        vec_rows = over(qkt, 4 * D, "vec_rows", [P, 2, P])
        ax = over(near_bias, 8 * D, "ax", [P, 2, 2, T, HD])
        angle = over(biased, 0, "angle", [P, 3, T, HD])
        junk = over(probs, 4 * D, "junk", [P, 512])
        g_final = over(near_bias, 0, "g_final", [P, D])
        p_rows = over(probs, 0, "p_rows", [P, T, S])
        assert nc.lookup_mloc(near_bias).dims[1] >= 24 * D

        bank = [ctx.enter_context(nc.psum_tensor(f"bank{b}", [P, 512], F32)) for b in range(8)]

        raw_in = [sem(f"raw_in{i}") for i in range(RAW_SLOTS)]
        const_in = sem("const_in")
        vec_in = sem("vec_in")
        x_in = sem("x_in")
        gate_in = sem("gate_in")
        row_in = sem("row_in")
        p_in = [sem(f"p_in{i}") for i in range(2)]
        misc_in = sem("misc_in")
        pad_ready = sem("pad_ready")
        rpb_in = sem("rpb_in")
        pad_out = sem("pad_out")
        bias_in = [sem(f"bias_in{i}") for i in range(2)]
        final_in = sem("final_in")
        out_done = sem("out_done")
        high_done = sem("high_done")
        low_done = sem("low_done")
        tile_done = sem("tile_done")
        half_done = sem("half_done")
        ada_done = sem("ada_done")
        job_done = sem("job_done")
        bank_free = [sem(f"bank_free{b}") for b in range(8)]
        high_copied = sem("high_copied")
        split_done = sem("split_done")
        rows_ready = sem("rows_ready")
        silu_ready = sem("silu_ready")
        affine_ready = sem("affine_ready")
        resid_done = sem("resid_done")
        x_ready = sem("x_ready")
        rms_ready = sem("rms_ready")
        ssq_ready = sem("ssq_ready")
        tanh_ready = sem("tanh_ready")
        angle_ready = sem("angle_ready")
        sin_ready = sem("sin_ready")
        scores_ready = sem("scores_ready")
        negmax_ready = sem("negmax_ready")
        scores_used = sem("scores_used")
        probs_turned = sem("probs_turned")
        turned_copied = [sem("turned_copied_act"), sem("turned_copied_dve")]
        head_out = sem("head_out")
        head_copied = sem("head_copied")
        index_used = sem("index_used")
        mask_ready = sem("mask_ready")
        act_step = sem("act_step")
        dve_step = sem("dve_step")
        pool_step = sem("pool_step")

        def const(name):
            a, b = CONST[name]
            return consts[:, a:b]

        ident = const("ident")
        sources = {"x": x, "xhat": u, "o": u}

        def raw_tile(t):
            return raw[:, t["slot"], 0:t["kc"] * t["cols"]]

        def split_parts(n):
            t = split[n]
            size = t["kc"] * t["cols"]
            return w_hi[:, n % HIGH_SLOTS, 0:size], w_lo[:, t["slot"], 0:size]

        def views(n):
            return [v.rearrange("p (k n) -> p k n", k=split[n]["kc"]) for v in split_parts(n)]

        def source(it, t, c):
            if it["src"] == "cq":
                return tok[:, t, 768 + c * P:768 + (c + 1) * P]
            if it["src"][0] == "p":
                return p_rows[:, t, c * P:(c + 1) * P]
            return sources[it["src"]][:, t, c * P:(c + 1) * P]

        def came(engine, it, t):
            if t == 0:
                engine.wait_ge(half_done, it["half"])
            else:
                engine.wait_ge(tile_done, it["tile"] + 1)

        pool_steps = [0]

        def ada_products(engine, ops, n):
            t = adas[n]
            if n in (0, 8):
                engine.wait_ge(silu_ready, 1)
            if n == 8:
                engine.wait_ge(ada_done, 16)
            if t["s"] and t["k"] == 0 and t["part"] in (0, 2):
                engine.wait_ge(job_done, t["gate_job"] if t["part"] else t["columns_job"])
            engine.wait_ge(raw_in[t["slot"]], t["full"])
            w = raw_tile(t).rearrange("p (k n) -> p k n", k=2)
            dst = ada_sum[:, t["part"], :]
            for i in range(2):
                c = cs[:, 0, t["k"] + i:t["k"] + i + 1]
                if t["k"] + i == 0:
                    ins = ops.tensor_tensor(dst, w[:, i, :], c.broadcast_to([P, D]), ALU.mult)
                elif n < 8:
                    ins = ops.scalar_tensor_tensor(dst, w[:, i, :], c, dst, ALU.mult, ALU.add)
                else:
                    ops.tensor_tensor(w[:, i, :], w[:, i, :], c.broadcast_to([P, D]), ALU.mult).then_inc(pool_step, 1)
                    pool_steps[0] += 1
                    engine.wait_ge(pool_step, pool_steps[0])
                    ins = ops.tensor_tensor(dst, w[:, i, :], dst, ALU.add)
                ins.then_inc(ada_done, 1)
                engine.wait_ge(ada_done, 2 * n + i + 1)

        def parts(it):
            return (plt_hi, plt_lo) if it["dst"] == "plt" else (ht_hi, ht_lo)

        def head_cols(mode, t):
            return P * (t + 1) if mode in ("causal", "window", "sparse", "index") else S

        def turned_halves(mode, h):
            dst, src = probs_t[:, h % 2, :, :], bank[4 + h % 2][:, :].rearrange("p (k q) -> p k q", k=T)
            if mode in ("near", "full"):
                return [(dst, src)]
            return [(dst[:, 0, :], src[:, 0, :]), (dst[:, 1, P:S], src[:, 1, P:S])]

        block = ctx.enter_context(nc.Block())

        @block.sync
        def _(sp):
            sp.dma_start(consts[:, :], R["consts"]).then_inc(const_in, 16)
            ada_rows = R["ada_b"].rearrange("l s (j p) -> (l s j) p", p=P)
            ln_rows = [R[n].rearrange("l s (j p) -> (l s j) p", p=P) for n in ("ln_g", "ln_b")]
            sp.dma_start(vec_rows[0:96, 0, :], ada_rows).then_inc(vec_in, 16)
            sp.dma_start(vec_rows[96:104, 0, :], R["c"].rearrange("b (j p) -> (b j) p", p=P)).then_inc(vec_in, 16)
            sp.dma_start(vec_rows[0:32, 1, :], ln_rows[0]).then_inc(vec_in, 16)
            sp.dma_start(vec_rows[32:64, 1, :], ln_rows[1]).then_inc(vec_in, 16)
            for name, a, n in (("norm_g_2", 64, 16), ("ple_norm_g_2", 80, 16), ("ab_q_norm", 96, 2)):
                sp.dma_start(vec_rows[a:a + n, 1, :], R[name].rearrange("l (j p) -> (l j) p", p=P)).then_inc(vec_in, 16)
            with nc.allow_non_contiguous_dma("256 positions"):
                sp.dma_start(pos_i[:, :], R["positions"][0].rearrange("(t p) -> p t", p=P)).then_inc(const_in, 16)
            for r, t in enumerate(order):
                if r == 4:
                    sp.dma_start(x[:, :, :], R["x"][0].rearrange("(t p) d -> p t d", p=P)).then_inc(x_in, 16)
                old = t["old"]
                if old:
                    if old["kind"] == "split":
                        sp.wait_ge(tile_done, old["n"] + 1)
                    else:
                        sp.wait_ge(ada_done, 2 * (old["n"] + 1))
                dst = raw_tile(t).rearrange("p (k n) -> p k n", k=t["kc"])
                sp.dma_start(dst, t["view"]).then_inc(raw_in[t["slot"]], 16)
            for t in range(T):
                sp.wait_ge(rows_ready, plan[-1]["rows"] - T + t + 1)
                sp.dma_start(out[0, t * P:(t + 1) * P, :], u[:, t, :]).then_inc(out_done, 16)
            sp.wait_ge(out_done, 16 * T)

        @block.gpsimd
        def _(pool):
            norm_rows = [i["rows"] for i in plan if i["kind"] == "ln"]
            pool.dma_start(sinks[:, 0, :], R["ab_sinks"][0].partition_broadcast(P)).then_inc(misc_in, 16)
            pool.dma_start(gain[:, 0, :], R["b_q_norm_2"][0].partition_broadcast(P)).then_inc(misc_in, 16)
            pool.dma_start(gain[:, 1, :], R["b_k_norm_2"][0].partition_broadcast(P)).then_inc(misc_in, 16)
            for s in range(N_SUB):
                if s:
                    pool.wait_ge(resid_done, T * s)
                else:
                    pool.wait_ge(ada_done, 16)
                gate_bias = R["ada_b"][s // 2, s % 2, 2 * D:3 * D]
                pool.dma_start(gate_row[:, :], gate_bias.partition_broadcast(P)).then_inc(gate_in, 16)
                pool.dma_start(g_row[:, :], R["ln_g"][s // 2, s % 2].partition_broadcast(P)).then_inc(row_in, 16)
                pool.dma_start(b_row[:, :], R["ln_b"][s // 2, s % 2].partition_broadcast(P)).then_inc(row_in, 16)
                for n, t in enumerate(adas):
                    if n >= 8 and (t["s"] == s + 1 or n < 12 and s == 0):
                        ada_products(pool, nc.gpsimd, n)
                if s < 3:
                    pool.wait_ge(row_in, 32 * (s + 1))
                    for t in range(T):
                        pool.wait_ge(rows_ready, norm_rows[s] - T + t + 1)
                        nc.gpsimd.tensor_tensor(x[:, t, :], u[:, t, :], g_row[:, :], ALU.mult).then_inc(pool_step, 1)
                        pool_steps[0] += 1
                        pool.wait_ge(pool_step, pool_steps[0])
                        nc.gpsimd.tensor_tensor(x[:, t, :], x[:, t, :], b_row[:, :], ALU.add).then_inc(resid_done, 1)
            nc.gpsimd.memset(rpb_rows[:, :, :], 0.0).then_inc(pool_step, 1)
            pool.dma_start(rpb_in_rows[:, :, :], R["a_rpb_2"][0, :, 4:11, :]).then_inc(rpb_in, 16)
            pool.wait_ge(rpb_in, 16)
            pool.wait_ge(pool_step, pool_steps[0] + 1)
            nc.gpsimd.tensor_copy(rpb_rows[:, :, 49:80], rpb_in_rows[:, :, ::-1]).then_inc(pool_step, 1)
            pool.wait_ge(pool_step, pool_steps[0] + 2)
            for half in range(2):
                pool.dma_start(toeplitz[half, :, :, :], rpb_rows[:, 1 - half:7 - half, :]).then_inc(pad_out, 16)
            pool.wait_ge(pad_out, 32)
            for part in range(2):
                if part:
                    pool.wait_ge(rows_ready, next(i["rows"] for i in plan if i["kind"] == "bias_table"))
                for half in range(2):
                    pool.dma_start(
                        near_rev[half * GRID:(half + 1) * GRID, :, :],
                        bass.AP(toeplitz, ((half * 2 + part) * 48) * 128 + 1, [[1, GRID], [128, 48], [1, GRID]]),
                    ).then_inc(bias_in[part], 16)
            for i in range(2):
                pool.wait_ge(probs_turned, p_after[i])
                pool.dma_start(p_rows[:, :, :], R["p_2"][i, 0].rearrange("(t p) d -> p t d", p=P)).then_inc(p_in[i], 16)
                if i == 0:
                    pool.dma_start(g_final[:, :], R["final_norm_g_2"].partition_broadcast(P)).then_inc(final_in, 16)

        @block.scalar
        def _(act):
            steps = [0]

            def link(ins):
                steps[0] += 1
                ins.then_inc(act_step, 1)
                act.wait_ge(act_step, steps[0])

            highs = [0]

            def split_high(until):
                for n in range(highs[0], min(until + 1, len(split))):
                    high_part(n)
                highs[0] = max(highs[0], until + 1)

            def high_part(n):
                t = split[n]
                act.wait_ge(raw_in[t["slot"]], t["full"])
                if n >= HIGH_SLOTS:
                    act.wait_ge(tile_done, n - HIGH_SLOTS + 1)
                nc.scalar.activation(split_parts(n)[0], raw_tile(t), ACT.Copy).then_inc(high_done, 1)

            def squares(t, n):
                nc.scalar.activation(junk[:, :], x[:, t, n * 512:(n + 1) * 512], ACT.Square,
                                     accum_out=ssq[:, t, n:n + 1]).then_inc(ssq_ready, 1)
                squared[0] += 1
                act.wait_ge(ssq_ready, squared[0])

            squared = [0]
            tanhs = 0
            act.wait_ge(bank_free[0], 1)
            nc.scalar.activation(cs[:, 1, :], vec[:, VEC_A["c"]:VEC_A["c"] + KD], ACT.Tanh, scale=0.5).then_inc(tanh_ready, 1)
            tanhs += 1
            split_high(1)
            act.wait_ge(angle_ready, 1)
            nc.scalar.activation(sinr[:, :, :], angle[:, 1, :, :], ACT.Sin).then_inc(sin_ready, 1)
            nc.scalar.activation(cosr[:, :, :], angle[:, 2, :, :], ACT.Sin).then_inc(sin_ready, 1)

            for it in plan:
                kind = it["kind"]
                if kind == "turn_split":
                    b, used = it["banks"][0]
                    act.wait_ge(job_done, it["job"])
                    if it["emptied"]:
                        act.wait_ge(split_done, it["emptied"])
                    m = min(2, it["n"])
                    hi = parts(it)[0][:, it["dst0"] + it["a"]:it["dst0"] + it["a"] + m, :]
                    if it["affine"] and it["affine"][0] == "affine":
                        act.wait_ge(affine_ready, it["affine"][1] + 1)
                    for c in range(m):
                        dst, ps = full[:, b, c * S:(c + 1) * S], bank[b][:, c * S:(c + 1) * S]
                        k = it["a"] + c
                        if it["affine"] is None:
                            ins = nc.scalar.activation(dst, ps, ACT.Copy)
                        elif it["affine"][0] == "affine":
                            ins = nc.scalar.activation(dst, ps, ACT.Identity, scale=aff[:, 0, k:k + 1], bias=aff[:, 1, k:k + 1])
                        else:
                            v = N_VEC_A + it["affine"][1] + k
                            ins = nc.scalar.activation(dst, ps, ACT.Copy, scale=vec[:, v:v + 1])
                    ins.then_inc(bank_free[b], 1)
                    act.wait_ge(bank_free[b], used + 1)
                    nc.scalar.activation(hi, full[:, b, 0:m * S].rearrange("p (c s) -> p c s", c=m), ACT.Copy)\
                        .then_inc(high_copied, 1)

                elif kind == "turn":
                    b, used = it["banks"][0]
                    act.wait_ge(job_done, it["job"])
                    nc.scalar.activation(qkt[:, it["dst"]:it["dst"] + 2, :],
                                         bank[b][:, :].rearrange("p (c s) -> p c s", c=2), ACT.Copy).then_inc(bank_free[b], 1)

                elif kind in ("tokens", "hidden"):
                    n = it["tile"]
                    split_high(it["ahead"])
                    end = it.get("end")
                    if end is None:
                        continue
                    if end == "hidden":
                        b, used = it["banks"][0]
                        act.wait_ge(tile_done, n + 1)
                        if it["emptied"]:
                            act.wait_ge(split_done, it["emptied"])
                        link(nc.scalar.activation(full[:, b, :], bank[b][:, :], ACT.Relu))
                        nc.scalar.activation(full[:, b, :], full[:, b, :], ACT.Square).then_inc(bank_free[b], 1)
                        act.wait_ge(bank_free[b], used + 1)
                        nc.scalar.activation(hid_hi[:, it["buf"], it["c0"]:it["c0"] + 2, :],
                                             full[:, b, :].rearrange("p (c s) -> p c s", c=2), ACT.Copy).then_inc(high_copied, 1)
                    elif end[0] in ("tok", "silu"):
                        _, c0, scale, width = end
                        if isinstance(scale, tuple):
                            act.wait_ge(rms_ready, scale[0] + 1)
                        for t, (b, used) in enumerate(it["banks"]):
                            came(act, it, t)
                            nc.scalar.activation(tok[:, t, c0:c0 + width], bank[b][:, 0:width], ACT.Copy,
                                                 scale=rms[:, scale[0], scale[1], t:t + 1] if isinstance(scale, tuple) else scale)\
                                .then_inc(bank_free[b], 1)
                    elif end[0] == "y_rms":
                        for t, (b, used) in enumerate(it["banks"]):
                            act.wait_ge(bank_free[b], used + 1)
                            squares(t, end[1])
                    elif end[0] == "ple":
                        act.wait_ge(rms_ready, end[2] + 1)
                        for t, (b, used) in enumerate(it["banks"]):
                            came(act, it, t)
                            nc.scalar.activation(full[:, 2 * end[1] + t, :], bank[b][:, :], ACT.Tanh, scale=rms[:, end[2], 1, t:t + 1])\
                                .then_inc(bank_free[b], 1)
                        for t in range(T):
                            act.wait_ge(x_ready, it["x"] - T + t + 1)
                            squares(t, end[1])

                elif kind == "resid" and it["s"] == 3:
                    for t in range(T):
                        act.wait_ge(resid_done, T * 3 + t + 1)
                        for n in range(2):
                            squares(t, n)

                elif kind == "gates":
                    for b in range(4):
                        act.wait_ge(bank_free[b], it["uses"][b])
                    for t in range(T):
                        nc.scalar.activation(full[:, 2 * t:2 * t + 2, :],
                                             tok[:, t, it["c0"]:it["c0"] + D].rearrange("p (a n) -> p a n", a=2),
                                             ACT.Tanh).then_inc(tanh_ready, 1)
                        tanhs += 1

                elif kind == "heads":
                    mode, spec, s0, h0 = it["mode"], it["spec"], it["s0"], it["h0"]
                    if mode == "index":
                        for i in range(len(spec)):
                            s = s0 + i
                            act.wait_ge(scores_ready, s + 1)
                            if i >= 2:
                                act.wait_ge(index_used, i - 1)
                            for t in range(T):
                                m = head_cols(mode, t)
                                ins = nc.scalar.activation(biased[:, i % 2, t, 0:m], bank[s % 4][:, t * S:t * S + m], ACT.Relu)
                            ins.then_inc(scores_used, 1)
                        continue
                    for i in range(len(spec) + 2):
                        if i < len(spec):
                            s, h = s0 + i, h0 + i
                            act.wait_ge(negmax_ready, h + 1)
                            if h >= 3:
                                act.wait_ge(probs_turned, h - 2)
                            if mode == "window":
                                hh = spec[i][4]
                                nc.scalar.activation(sink_exp[:, h % 4, :], nmx[:, h % 4, :], ACT.Exp, bias=sinks[:, 0, hh:hh + 1])
                            for t in range(T):
                                m = head_cols(mode, t)
                                src = biased[:, h % 2, t, :] if mode == "near" else bank[s % 4][:, t * S:t * S + m]
                                ins = nc.scalar.activation(probs[:, h % 3, t, 0:m], src, ACT.Exp, bias=nmx[:, h % 4, t:t + 1],
                                                           scale=1.0 if mode == "near" else SCALE,
                                                           accum_out=sums[:, h % 4, t:t + 1])
                            ins.then_inc(scores_used, 1)
                        h = h0 + i - 2
                        if i >= 2 and h % 2 == 0:
                            act.wait_ge(probs_turned, h + 1)
                            if h >= 2:
                                act.wait_ge(head_out, h - 1)
                            for dst, src in turned_halves(mode, h):
                                ins = nc.scalar.activation(dst, src, ACT.Copy)
                            ins.then_inc(turned_copied[0], 1)

        @block.tensor
        def _(pe):
            def enter(banks):
                for b, used in banks:
                    if used:
                        pe.wait_ge(bank_free[b], used)

            for it in plan:
                kind = it["kind"]
                if kind == "turn_vectors":
                    pe.wait_ge(const_in, 32)
                    pe.wait_ge(vec_in, 16 * 7)
                    b, _ = it["banks"][0]
                    nc.tensor.transpose(bank[b][:, 0:N_VEC_A], vec_rows[0:N_VEC_A, 0, :], ident[0:N_VEC_A, 0:N_VEC_A])
                    nc.tensor.transpose(bank[b][:, N_VEC_A:N_VEC_A + N_VEC_B], vec_rows[0:N_VEC_B, 1, :],
                                        ident[0:N_VEC_B, 0:N_VEC_B]).then_inc(job_done, 1)

                elif kind == "ada_columns":
                    enter(it["banks"])
                    pe.wait_ge(ada_done, 2 * it["ada"])
                    b = it["banks"][0][0]
                    for i in range(2 * KD):
                        mm = nc.tensor.matmul(bank[b][:, i:i + 1], ada_sum[:, i // KD, (i % KD) * P:(i % KD + 1) * P],
                                              const("ones")[:, 0:1], start=True, stop=True)
                    mm.then_inc(job_done, 1)

                elif kind == "gate_row":
                    enter(it["banks"])
                    pe.wait_ge(ada_done, 24 * (it["s"] + 1))
                    for n, (b, _) in enumerate(it["banks"]):
                        mm = nc.tensor.matmul(bank[b][:, :], const("ones"), ada_sum[:, 2, n * 512:(n + 1) * 512], start=True, stop=True)
                    mm.then_inc(job_done, 1)

                elif kind == "turn_split":
                    enter(it["banks"])
                    if it["src"] == "x":
                        pe.wait_ge(x_in, 16)
                    if it["wait"] and it["src"] != "xhat":
                        pe.wait_ge(rows_ready, it["wait"])
                    if "updated" in it:
                        how, value = it["updated"]
                        if how == "x":
                            pe.wait_ge(x_ready, value)
                        else:
                            enter(value)
                    if it["src"] == "o":
                        pe.wait_ge(head_copied, it["heads"])
                    if it["src"][0] == "p":
                        pe.wait_ge(p_in[it["src"][1]], 16)
                    for t in range(T):
                        if it["src"] == "xhat":
                            pe.wait_ge(rows_ready, it["wait"] - T + t + 1)
                        for c in range(it["n"]):
                            b = it["banks"][c // 2][0]
                            o = (c % 2) * S + t * P
                            mm = nc.tensor.transpose(bank[b][:, o:o + P], source(it, t, it["a"] + c), ident)
                    mm.then_inc(job_done, 1)

                elif kind == "turn":
                    enter(it["banks"])
                    if it["wait"]:
                        pe.wait_ge(rows_ready, it["wait"])
                    for b in range(4):
                        pe.wait_ge(bank_free[b], it["before"][b])
                    for c, col in enumerate(it["cols"]):
                        b = it["banks"][c // 2][0]
                        for t in range(T):
                            o = (c % 2) * S + t * P
                            mm = nc.tensor.transpose(bank[b][:, o:o + P], tok[:, t, col:col + P], ident)
                    mm.then_inc(job_done, 1)

                elif kind == "tokens":
                    n = it["tile"]
                    if it["enter"]:
                        enter(it["banks"])
                    pe.wait_ge(split_done, it["cut"])
                    pe.wait_ge(low_done, n + 1)
                    hi, lo = views(n)
                    if it["lhs"] == "ht":
                        a_hi, a_lo = ht_hi[:, :, :], ht_lo[:, :, :]
                    elif it["lhs"] == "plt":
                        a_hi, a_lo = plt_hi[:, :, :], plt_lo[:, :, :]
                    else:
                        a_hi, a_lo = hid_hi[:, it["lhs"][1], :, :], hid_lo[:, it["lhs"][1], :, :]
                    for t, (b, _) in enumerate(it["banks"]):
                        dst = bank[b][:, 0:it["width"]]
                        for k in range(it["kc"]):
                            rows = slice(t * P, (t + 1) * P)
                            c = it["off"] + k
                            nc.tensor.matmul(dst, a_hi[:, c, rows], lo[:, k, :], start=it["first"] and k == 0, stop=False)
                            nc.tensor.matmul(dst, a_hi[:, c, rows], hi[:, k, :], start=False, stop=False)
                            mm = nc.tensor.matmul(dst, a_lo[:, c, rows], hi[:, k, :], start=False,
                                                  stop=it["last"] and k == it["kc"] - 1)
                        mm.then_inc(tile_done if t else half_done, 1)

                elif kind == "hidden":
                    n = it["tile"]
                    b, used = it["banks"][it["half"]]
                    enter([(b, used)])
                    pe.wait_ge(split_done, it["cut"][0])
                    pe.wait_ge(low_done, n + 1)
                    hi, lo = views(n)
                    for c in range(2):
                        dst = bank[b][:, c * S:(c + 1) * S]
                        for k in range(KD):
                            if c == 0 and k == 4:
                                pe.wait_ge(split_done, it["cut"][1])
                            cols = slice(c * P, (c + 1) * P)
                            nc.tensor.matmul(dst, lo[:, k, cols], ht_hi[:, k, :], start=k == 0, stop=False)
                            nc.tensor.matmul(dst, hi[:, k, cols], ht_lo[:, k, :], start=False, stop=False)
                            mm = nc.tensor.matmul(dst, hi[:, k, cols], ht_hi[:, k, :], start=False, stop=k == KD - 1)
                    mm.then_inc(tile_done, 1)

                elif kind == "heads":
                    mode, spec, s0, h0 = it["mode"], it["spec"], it["s0"], it["h0"]
                    for b in range(8):
                        if it["uses"][b]:
                            pe.wait_ge(bank_free[b], it["uses"][b])
                    if mode == "sparse":
                        pe.wait_ge(mask_ready, 1)
                    last_lag = 0 if mode == "index" else 3
                    for i in range(len(spec) + last_lag):
                        if i < len(spec):
                            s = s0 + i
                            qc, half, kc, _, _ = spec[i]
                            part = slice(half * HD, (half + 1) * HD)
                            if s >= 4:
                                pe.wait_ge(scores_used, s - 3)
                            for t in range(T):
                                m = head_cols(mode, t)
                                masks = {"causal": [(t * P, maskb[:, 2, :])],
                                         "window": [(0, maskb[:, 2 - t:3, :].rearrange("p a n -> p (a n)"))],
                                         "sparse": [(0, smask[:, t, 0:m])]}.get(mode, [])
                                mm = nc.tensor.matmul(bank[s % 4][:, t * S:t * S + m], qkt[part, qc, t * P:(t + 1) * P],
                                                      qkt[part, kc, 0:m], start=True, stop=not masks)
                                for o, mask in masks:
                                    mm = nc.tensor.matmul(bank[s % 4][:, t * S + o:t * S + m], maskb[:, 0, :], mask,
                                                          start=False, stop=True)
                            mm.then_inc(scores_ready, 1)
                        if mode == "index":
                            continue
                        if 2 <= i < len(spec) + 2:
                            h = h0 + i - 2
                            pe.wait_ge(scores_used, s0 + i - 1)
                            if h >= 2:
                                pe.wait_ge(turned_copied[h % 2], h // 2)
                            for t in range(T):
                                for k in range(head_cols(mode, t) // P):
                                    mm = nc.tensor.transpose(bank[4 + h % 2][:, k * S + t * P:k * S + (t + 1) * P],
                                                             probs[:, h % 3, t, k * P:(k + 1) * P], ident)
                            mm.then_inc(probs_turned, 1)
                        if i >= 3:
                            h = h0 + i - 3
                            v = spec[i - 3][3]
                            pe.wait_ge(turned_copied[h % 2], h // 2 + 1)
                            if h >= 2:
                                pe.wait_ge(head_copied, h - 1)
                            for t in range(T):
                                o = t * HD
                                nk = head_cols(mode, t) // P
                                for k in range(nk):
                                    mm = nc.tensor.matmul(bank[6 + h % 2][:, o:o + HD], probs_t[:, h % 2, k, t * P:(t + 1) * P],
                                                          tok[:, k, v:v + HD], start=k == 0, stop=k == nk - 1)
                            mm.then_inc(head_out, 1)

        @block.vector
        def _(dve):
            steps = [0]

            def link(ins):
                steps[0] += 1
                ins.then_inc(dve_step, 1)
                dve.wait_ge(dve_step, steps[0])

            def columns(it):
                s = it["s"]
                b, used = it["banks"][0]
                dve.wait_ge(job_done, it["job"])
                bias = vec[:, 3 * KD * s:3 * KD * s + 2 * KD]
                nc.vector.tensor_tensor(mod[:, :], bank[b][:, 0:2 * KD], bias, ALU.add).then_inc(bank_free[b], 1)
                dve.wait_ge(bank_free[b], used + 1)
                shift, scale = mod[:, 0:KD], mod[:, KD:2 * KD]
                if s == 0:
                    link(nc.vector.tensor_scalar(aff[:, 0, :], scale, 1.0, None, ALU.add))
                    nc.vector.tensor_copy(aff[:, 1, :], shift).then_inc(affine_ready, 1)
                else:
                    g = vec[:, N_VEC_A + KD * (s - 1):N_VEC_A + KD * s]
                    lb = vec[:, N_VEC_A + 32 + KD * (s - 1):N_VEC_A + 32 + KD * s]
                    link(nc.vector.scalar_tensor_tensor(aff[:, 0, :], scale, 1.0, g, ALU.add, ALU.mult))
                    link(nc.vector.scalar_tensor_tensor(aff[:, 1, :], scale, 1.0, lb, ALU.add, ALU.mult))
                    nc.vector.tensor_tensor(aff[:, 1, :], aff[:, 1, :], shift, ALU.add).then_inc(affine_ready, 1)
                dve.wait_ge(affine_ready, s + 1)

            lows = [0]

            def split_low(until):
                for n in range(lows[0], min(until + 1, len(split))):
                    weight_low(n)
                lows[0] = max(lows[0], until + 1)

            def weight_low(n):
                hi, lo = split_parts(n)
                dve.wait_ge(high_done, n + 1)
                nc.vector.tensor_tensor(lo, raw_tile(split[n]), hi.bitcast(F32), ALU.subtract).then_inc(low_done, 1)

            cuts = [0]

            def low_part(lo, v, hi):
                nc.vector.tensor_tensor(lo, v, hi.bitcast(F32), ALU.subtract).then_inc(split_done, 1)
                cuts[0] += 1

            def rsqrt(v, n):
                y, a, b = rstd[:, 0:n], small[:, 1, 0:n], small[:, 2, 0:n]
                link(nc.vector.tensor_scalar(bits[:, 0:n], v.bitcast(U32), 1, None, ALU.logical_shift_right))
                link(nc.vector.tensor_scalar(y.bitcast(U32), bits[:, 0:n], -1.0, RSQRT_MAGIC, ALU.mult, ALU.add))
                for _ in range(3):
                    link(nc.vector.tensor_tensor(a, y, y, ALU.mult))
                    link(nc.vector.scalar_tensor_tensor(b, a, -0.5, v, ALU.mult, ALU.mult))
                    link(nc.vector.scalar_tensor_tensor(y, b, 1.5, y, ALU.add, ALU.mult))

            def rope(it, cos, sin, groups, half):
                for n, (col, nh, dup) in enumerate(it["what"]):
                    for t in range(T):
                        w = nh * HD
                        q = tok[:, t, col:col + w]
                        ta, tb = tmp_a[:, 0:w], tmp_b[:, 0:w]
                        c = cos(t).unsqueeze(1).broadcast_to([P, nh, HD])
                        nc.vector.tensor_tensor(ta.rearrange("p (h d) -> p h d", h=nh), q.rearrange("p (h d) -> p h d", h=nh), c, ALU.mult)
                        for a in range(2):
                            qv = q.rearrange("p (h g a d) -> p h g a d", h=nh, g=groups, a=2)[:, :, :, 1 - a, :]
                            tv = tb.rearrange("p (h g a d) -> p h g a d", h=nh, g=groups, a=2)[:, :, :, a, :]
                            sv = sin(t).rearrange("p (g a d) -> p g a d", g=groups, a=2)[:, :, a, :]\
                                .unsqueeze(1).broadcast_to([P, nh, groups, half])
                            if groups == 1:
                                qv, tv, sv = qv[:, :, 0, :], tv[:, :, 0, :], sv[:, :, 0, :]
                            ins = nc.vector.tensor_tensor(tv, qv, sv, ALU.mult)
                        link(ins)
                        if dup is None:
                            ins = nc.vector.tensor_tensor(q, ta, tb, ALU.add)
                        else:
                            for r in range(2):
                                o = tok[:, t, dup:dup + 2 * w].rearrange("p (h r d) -> p h r d", h=nh, r=2)[:, :, r, :]
                                ins = nc.vector.tensor_tensor(o, ta.rearrange("p (h d) -> p h d", h=nh),
                                                              tb.rearrange("p (h d) -> p h d", h=nh), ALU.add)
                        if n == len(it["what"]) - 1 and t == T - 1:
                            ins.then_inc(rows_ready, 1)
                            dve.wait_ge(rows_ready, it["rows"])
                        else:
                            link(ins)

            def projected(it):
                for b in range(4):
                    dve.wait_ge(bank_free[b], it["uses"][b])

            turned = next(i for i in plan if i["kind"] == "turn_vectors")
            dve.wait_ge(job_done, turned["job"])
            nv = N_VEC_A + N_VEC_B
            b0 = turned["banks"][0][0]
            nc.vector.tensor_copy(vec[:, :], bank[b0][:, 0:nv]).then_inc(bank_free[b0], 1)
            dve.wait_ge(bank_free[b0], 1)
            cvec = vec[:, VEC_A["c"]:VEC_A["c"] + KD]
            link(nc.vector.tensor_scalar(cs[:, 2, :], cvec, 0.5, None, ALU.mult))
            dve.wait_ge(tanh_ready, 1)
            tanhs = 1
            nc.vector.scalar_tensor_tensor(cs[:, 0, :], cs[:, 1, :], 1.0, cs[:, 2, :], ALU.add, ALU.mult).then_inc(silu_ready, 1)
            for n in range(8):
                ada_products(dve, nc.vector, n)
            for m, name in enumerate(("ident", "window", "causal")):
                link(nc.vector.tensor_copy(maskb[:, m, :], const(name)))
            link(nc.vector.tensor_copy(pos_f[:, :], pos_i[:, :]))
            for t in range(T):
                link(nc.vector.tensor_scalar(angle[:, 0, t, :], const("invf"), pos_f[:, t:t + 1], None, ALU.mult))
            for j, turn in ((1, 0.0), (2, 0.25)):
                k = tmp_a[:, 0:T * HD]
                a0 = angle[:, 0, :, :].rearrange("p t d -> p (t d)")
                r = angle[:, j, :, :].rearrange("p t d -> p (t d)")
                link(nc.vector.tensor_scalar(k, a0, float(1 / TWO_PI), turn, ALU.mult, ALU.add))
                link(nc.vector.tensor_scalar(k, k, ROUND, -ROUND, ALU.add, ALU.add))
                link(nc.vector.scalar_tensor_tensor(r, k, -C1, a0, ALU.mult, ALU.add))
                link(nc.vector.scalar_tensor_tensor(r, k, -C2, r, ALU.mult, ALU.add))
                link(nc.vector.scalar_tensor_tensor(r, k, -C3, r, ALU.mult, ALU.add))
                link(nc.vector.tensor_scalar(r, r, float(turn * TWO_PI), 3.1415925, ALU.add, ALU.min))
                ins = nc.vector.tensor_scalar(r, r, -3.1415925, None, ALU.max)
                if j == 2:
                    ins.then_inc(angle_ready, 1)
                else:
                    link(ins)
            split_low(0)
            columns(next(i for i in plan if i["kind"] == "ada_columns"))

            for it in plan:
                kind = it["kind"]
                if kind == "ada_columns":
                    if it["s"]:
                        columns(it)

                elif kind == "rope_tables":
                    dve.wait_ge(sin_ready, 2)
                    for t in range(T):
                        link(nc.vector.tensor_tensor(sinr[:, t, :], sinr[:, t, :], const("sign"), ALU.mult))
                    dve.wait_ge(misc_in, 48)
                    link(nc.vector.tensor_scalar(sinks[:, 1, :], sinks[:, 0, :], -1.0, None, ALU.mult))

                elif kind == "gate_row":
                    dve.wait_ge(gate_in, 16 * (it["s"] + 1))
                    dve.wait_ge(job_done, it["job"])
                    for n, (b, used) in enumerate(it["banks"]):
                        row = gate_row[:, n * 512:(n + 1) * 512]
                        nc.vector.scalar_tensor_tensor(row, bank[b][:, :], 1.0, row, ALU.add, ALU.add).then_inc(bank_free[b], 1)
                        dve.wait_ge(bank_free[b], used + 1)

                elif kind == "turn_split":
                    dve.wait_ge(job_done, it["job"])
                    hi_all, lo_all = parts(it)
                    if len(it["banks"]) > 1:
                        b, used = it["banks"][1]
                        c0 = it["dst0"] + it["a"] + 2
                        hi, lo = hi_all[:, c0:c0 + 2, :], lo_all[:, c0:c0 + 2, :]
                        for c in range(2):
                            k = it["a"] + 2 + c
                            dst, ps = full[:, b, c * S:(c + 1) * S], bank[b][:, c * S:(c + 1) * S]
                            if it["affine"] is None:
                                ins = nc.vector.tensor_copy(dst, ps)
                            elif it["affine"][0] == "affine":
                                ins = nc.vector.tensor_scalar(dst, ps, aff[:, 0, k:k + 1], aff[:, 1, k:k + 1], ALU.mult, ALU.add)
                            else:
                                v = N_VEC_A + it["affine"][1] + k
                                ins = nc.vector.tensor_scalar(dst, ps, vec[:, v:v + 1], None, ALU.mult)
                        ins.then_inc(bank_free[b], 1)
                        dve.wait_ge(bank_free[b], used + 1)
                        v2 = full[:, b, :].rearrange("p (c s) -> p c s", c=2)
                        link(nc.vector.tensor_copy(hi, v2))
                        low_part(lo, v2, hi)
                    b, _ = it["banks"][0]
                    m = min(2, it["n"])
                    c0 = it["dst0"] + it["a"]
                    dve.wait_ge(high_copied, it["high"])
                    low_part(lo_all[:, c0:c0 + m, :], full[:, b, 0:m * S].rearrange("p (c s) -> p c s", c=m), hi_all[:, c0:c0 + m, :])

                elif kind == "turn":
                    b, _ = it["banks"][1]
                    dve.wait_ge(job_done, it["job"])
                    nc.vector.tensor_copy(qkt[:, it["dst"] + 2:it["dst"] + 4, :],
                                          bank[b][:, :].rearrange("p (c s) -> p c s", c=2)).then_inc(bank_free[b], 1)

                elif kind in ("tokens", "hidden"):
                    n = it["tile"]
                    split_low(it["ahead"])
                    end = it.get("end")
                    if end is None:
                        continue
                    if end == "hidden":
                        b, used = it["banks"][1]
                        dve.wait_ge(tile_done, n + 1)
                        v2 = full[:, b, :].rearrange("p (c s) -> p c s", c=2)
                        link(nc.vector.tensor_scalar(full[:, b, :], bank[b][:, :], 0.0, None, ALU.max))
                        nc.vector.tensor_tensor(full[:, b, :], full[:, b, :], full[:, b, :], ALU.mult).then_inc(bank_free[b], 1)
                        dve.wait_ge(bank_free[b], used + 1)
                        hi = hid_hi[:, it["buf"], it["c0"] + 2:it["c0"] + 4, :]
                        link(nc.vector.tensor_copy(hi, v2))
                        low_part(hid_lo[:, it["buf"], it["c0"] + 2:it["c0"] + 4, :], v2, hi)
                        b, _ = it["banks"][0]
                        dve.wait_ge(high_copied, it["high"])
                        low_part(hid_lo[:, it["buf"], it["c0"]:it["c0"] + 2, :],
                                 full[:, b, :].rearrange("p (c s) -> p c s", c=2),
                                 hid_hi[:, it["buf"], it["c0"]:it["c0"] + 2, :])
                    elif end[0] == "y_ln":
                        if end[2]:
                            dve.wait_ge(resid_done, T * end[2])
                        cols = slice(end[1] * 512, (end[1] + 1) * 512)
                        for t, (b, used) in enumerate(it["banks"]):
                            came(dve, it, t)
                            nc.vector.tensor_tensor(tmp_a[:, :], bank[b][:, :], gate_row[:, cols], ALU.mult).then_inc(bank_free[b], 1)
                            dve.wait_ge(bank_free[b], used + 1)
                            link(nc.vector.scalar_tensor_tensor(u[:, t, cols], x[:, t, cols], ALPHA, tmp_a[:, :], ALU.mult, ALU.add))
                            link(nc.vector.bn_stats(stats[:, t, end[1], :], u[:, t, cols]))
                    elif end[0] == "y_rms":
                        cols = slice(end[1] * 512, (end[1] + 1) * 512)
                        for t, (b, used) in enumerate(it["banks"]):
                            came(dve, it, t)
                            nc.vector.tensor_tensor(x[:, t, cols], bank[b][:, :], x[:, t, cols], ALU.add).then_inc(bank_free[b], 1)
                            dve.wait_ge(bank_free[b], used + 1)
                    elif end[0] == "ple":
                        cols = slice(end[1] * 512, (end[1] + 1) * 512)
                        for t, (b, used) in enumerate(it["banks"]):
                            dve.wait_ge(bank_free[b], used + 1)
                            link(nc.vector.scalar_tensor_tensor(tmp_a[:, :], full[:, 2 * end[1] + t, :], 1.0, tok[:, t, cols], ALU.add, ALU.mult))
                            nc.vector.tensor_tensor(x[:, t, cols], x[:, t, cols], tmp_a[:, :], ALU.add).then_inc(x_ready, 1)
                            dve.wait_ge(x_ready, it["x"] - T + t + 1)

                elif kind == "ln":
                    if it["s"] == N_SUB - 1:
                        ng = vec[:, N_VEC_A + VEC_B["norm_g"]:N_VEC_A + VEC_B["norm_g"] + KD]
                        for i, first in enumerate((KD * it["s"], 32 + KD * it["s"])):
                            ins = nc.vector.tensor_tensor(aff[:, i, :], vec[:, N_VEC_A + first:N_VEC_A + first + KD], ng, ALU.mult)
                            if i == 0:
                                link(ins)
                        ins.then_inc(affine_ready, 1)
                        dve.wait_ge(affine_ready, N_SUB + 1)
                    for t in range(T):
                        link(nc.vector.bn_aggr(meanvar[:, t, :], stats[:, t, :, :]))
                    link(nc.vector.tensor_scalar(small[:, 0, 0:T], meanvar[:, :, 1], LN_EPS, None, ALU.add))
                    rsqrt(small[:, 0, 0:T], T)
                    for t in range(T):
                        nc.vector.tensor_scalar(u[:, t, :], u[:, t, :], meanvar[:, t, 0:1], rstd[:, t:t + 1],
                                                ALU.subtract, ALU.mult).then_inc(rows_ready, 1)
                        dve.wait_ge(rows_ready, it["rows"] - T + t + 1)

                elif kind == "resid":
                    dve.wait_ge(row_in, 32 * (it["s"] + 1))
                    for t in range(T):
                        link(nc.vector.tensor_tensor(x[:, t, :], u[:, t, :], g_row[:, :], ALU.mult))
                        nc.vector.tensor_tensor(x[:, t, :], x[:, t, :], b_row[:, :], ALU.add).then_inc(resid_done, 1)
                        dve.wait_ge(resid_done, T * it["s"] + t + 1)

                elif kind in ("rms", "final"):
                    dve.wait_ge(ssq_ready, it["ssq"])
                    v = small[:, 0, 0:T]
                    link(nc.vector.tensor_tensor(v, ssq[:, :, 0], ssq[:, :, 1], ALU.add))
                    link(nc.vector.tensor_scalar(v, v, 1.0 / D, RMS_EPS, ALU.mult, ALU.add))
                    rsqrt(v, T)
                    if kind == "rms":
                        link(nc.vector.tensor_copy(rms[:, it["i"], 0, :], rstd[:, 0:T]))
                        nc.vector.tensor_scalar(rms[:, it["i"], 1, :], rstd[:, 0:T], 0.5, None, ALU.mult).then_inc(rms_ready, 1)
                        dve.wait_ge(rms_ready, it["i"] + 1)
                        continue
                    dve.wait_ge(final_in, 16)
                    for t in range(T):
                        nc.vector.scalar_tensor_tensor(u[:, t, :], x[:, t, :], rstd[:, t:t + 1], g_final[:, :], ALU.mult, ALU.mult)\
                            .then_inc(rows_ready, 1)
                        dve.wait_ge(rows_ready, it["rows"] - T + t + 1)

                elif kind == "low_rank":
                    projected(it)
                    for t in range(T):
                        cq = tok[:, t, 768:1024]
                        link(nc.vector.tensor_tensor(tmp_a[:, 0:256], cq, cq, ALU.mult))
                        link(nc.vector.tensor_reduce(small[:, 0, t:t + 1], tmp_a[:, 0:256], AX, ALU.add))
                    v = small[:, 0, 0:T]
                    link(nc.vector.tensor_scalar(v, v, 1.0 / 256, RMS_EPS, ALU.mult, ALU.add))
                    rsqrt(v, T)
                    for t in range(T):
                        ins = nc.vector.tensor_scalar(tok[:, t, 768:1024], tok[:, t, 768:1024], rstd[:, t:t + 1], None, ALU.mult)
                        if t == T - 1:
                            ins.then_inc(rows_ready, 1)
                            dve.wait_ge(rows_ready, it["rows"])

                elif kind == "rope":
                    projected(it)
                    rope(it, lambda t: cosr[:, t, :], lambda t: sinr[:, t, :], 1, HD // 2)

                elif kind == "qk_rope":
                    projected(it)
                    g = 0 if it["gain"] == "q" else 1
                    col, nh, _ = it["what"][0]
                    w = nh * HD
                    for t in range(T):
                        q = tok[:, t, col:col + w]
                        link(nc.vector.tensor_tensor(tmp_a[:, 0:w], q, q, ALU.mult))
                        link(nc.vector.tensor_reduce(small[:, 0, t * nh:(t + 1) * nh], tmp_a[:, 0:w].rearrange("p (h d) -> p h d", h=nh), AX, ALU.add))
                    v = small[:, 0, 0:T * nh]
                    link(nc.vector.tensor_scalar(v, v, 1.0 / HD, RMS_EPS, ALU.mult, ALU.add))
                    rsqrt(v, T * nh)
                    for t in range(T):
                        q = tok[:, t, col:col + w].rearrange("p (h d) -> p h d", h=nh)
                        link(nc.vector.tensor_tensor(q, q, rstd[:, t * nh:(t + 1) * nh].unsqueeze(2).broadcast_to([P, nh, HD]), ALU.mult))
                    rope(it, lambda t: ax[:, g, 0, t, :], lambda t: ax[:, g, 1, t, :], 2, HD // 4)

                elif kind == "axial_tables":
                    for g in range(2):
                        for t in range(T):
                            cs_t = const("axcos")[:, t * HD:(t + 1) * HD]
                            sn_t = const("axsin")[:, t * HD:(t + 1) * HD].rearrange("p (g a d) -> p g a d", g=2, a=2)
                            gv = gain[:, g, :].rearrange("p (g a d) -> p g a d", g=2, a=2)
                            dst = ax[:, g, 1, t, :].rearrange("p (g a d) -> p g a d", g=2, a=2)
                            link(nc.vector.tensor_tensor(ax[:, g, 0, t, :], cs_t, gain[:, g, :], ALU.mult))
                            for a in range(2):
                                link(nc.vector.tensor_tensor(dst[:, :, a, :], sn_t[:, :, a, :], gv[:, :, 1 - a, :], ALU.mult))

                elif kind == "bias_table":
                    part = it["part"]
                    dve.wait_ge(bias_in[part], 32)
                    dst = near_bias[:, 8 * part:8 * part + 8, :].rearrange("p h (r k) -> p (h r) k", k=GRID)
                    nc.vector.tensor_tensor(dst, near_rev[:, :, ::-1], const("near").unsqueeze(1).broadcast_to([P, 48, GRID]), ALU.add)\
                        .then_inc(rows_ready, 1)
                    dve.wait_ge(rows_ready, it["rows"])

                elif kind == "gates":
                    for t in range(T):
                        tanhs += 1
                        dve.wait_ge(tanh_ready, tanhs)
                        gv = tok[:, t, it["c0"]:it["c0"] + D].rearrange("p (a n) -> p a n", a=2)
                        link(nc.vector.scalar_tensor_tensor(gv, full[:, 2 * t:2 * t + 2, :], 1.0, gv, ALU.add, ALU.mult))

                elif kind == "heads":
                    mode, spec, s0, h0 = it["mode"], it["spec"], it["s0"], it["h0"]
                    if mode == "causal":
                        dve.wait_ge(resid_done, 2 * T)
                    if mode == "index":
                        link(nc.vector.tensor_scalar(iw[:, :, :], tok[:, :, 1216:1224], IW_SCALE, None, ALU.mult))
                        for i in range(len(spec)):
                            dve.wait_ge(scores_used, s0 + i + 1)
                            for t in range(T):
                                m = head_cols(mode, t)
                                src, w = biased[:, i % 2, t, 0:m], iw[:, t, i:i + 1]
                                if i == 0:
                                    ins = nc.vector.tensor_scalar(score[:, t, 0:m], src, w, None, ALU.mult)
                                else:
                                    ins = nc.vector.scalar_tensor_tensor(score[:, t, 0:m], src, w, score[:, t, 0:m], ALU.mult, ALU.add)
                            ins.then_inc(index_used, 1)
                            dve.wait_ge(index_used, i + 1)
                        for t in range(T):
                            own = score[:, t, t * P:(t + 1) * P]
                            link(nc.vector.tensor_tensor(own, own, const("causal"), ALU.add))
                        continue
                    for i in range(len(spec) + 3):
                        if i < len(spec):
                            s, h = s0 + i, h0 + i
                            dve.wait_ge(scores_ready, s + 1)
                            if mode == "near":
                                if i >= 2:
                                    dve.wait_ge(scores_used, s - 1)
                                for t in range(T):
                                    o = (2 - 2 * t) * GRID
                                    ins = nc.vector.scalar_tensor_tensor(biased[:, h % 2, t, :], bank[s % 4][:, t * S:(t + 1) * S], SCALE,
                                                                         near_bias[:, spec[i][4], o:o + S], ALU.mult, ALU.add)
                                link(ins)
                                link(nc.vector.tensor_reduce(mx[:, h % 4, :], biased[:, h % 2, :, :], AX, ALU.max))
                            elif mode == "full":
                                link(nc.vector.tensor_reduce(mx[:, h % 4, :], bank[s % 4][:, :].rearrange("p (t k) -> p t k", t=T), AX, ALU.max))
                            else:
                                for t in range(T):
                                    ins = nc.vector.tensor_reduce(mx[:, h % 4, t:t + 1], bank[s % 4][:, t * S:t * S + head_cols(mode, t)], AX, ALU.max)
                                link(ins)
                            if mode == "window":
                                hh = spec[i][4]
                                nc.vector.tensor_scalar(nmx[:, h % 4, :], mx[:, h % 4, :], -SCALE, sinks[:, 1, hh:hh + 1],
                                                        ALU.mult, ALU.min).then_inc(negmax_ready, 1)
                            else:
                                nc.vector.tensor_scalar(nmx[:, h % 4, :], mx[:, h % 4, :], -1.0 if mode == "near" else -SCALE, None,
                                                        ALU.mult).then_inc(negmax_ready, 1)
                        h = h0 + i - 2
                        if 2 <= i < len(spec) + 2 and h % 2:
                            dve.wait_ge(probs_turned, h + 1)
                            if h >= 2:
                                dve.wait_ge(head_out, h - 1)
                            for dst, src in turned_halves(mode, h):
                                ins = nc.vector.tensor_copy(dst, src)
                            ins.then_inc(turned_copied[1], 1)
                        if i >= 3:
                            h = h0 + i - 3
                            hh = spec[i - 3][4]
                            dve.wait_ge(scores_used, s0 + i - 2)
                            if mode == "window":
                                link(nc.vector.tensor_tensor(sums[:, h % 4, :], sums[:, h % 4, :], sink_exp[:, h % 4, :], ALU.add))
                            link(nc.vector.reciprocal(rs[:, h % 4, :], sums[:, h % 4, :]))
                            dve.wait_ge(head_out, h + 1)
                            ps = bank[6 + h % 2][:, 0:P].rearrange("p (t d) -> p t d", t=T)
                            if "gate" in it:
                                for t in range(T):
                                    gc = it["gate"] + hh * HD
                                    ins = nc.vector.scalar_tensor_tensor(u[:, t, hh * HD:(hh + 1) * HD], ps[:, t, :], rs[:, h % 4, t:t + 1],
                                                                         tok[:, t, gc:gc + HD], ALU.mult, ALU.mult)
                            else:
                                ins = nc.vector.tensor_tensor(u[:, :, hh * HD:(hh + 1) * HD], ps,
                                                              rs[:, h % 4, :].unsqueeze(2).broadcast_to([P, T, HD]), ALU.mult)
                            ins.then_inc(head_copied, 1)
                        if mode == "window" and i < 8:
                            for r in (2 * i, 2 * i + 1):
                                t = r // 8
                                sc = score[:, t, 0:P * (t + 1)]
                                link(nc.vector.max(top8[:, :], sc))
                                link(nc.vector.match_replace(sc, top8[:, :], sc, PICKED))
                            if i == 7:
                                for t in range(T):
                                    m = P * (t + 1)
                                    link(nc.vector.tensor_scalar(smask[:, t, 0:m], score[:, t, 0:m], PICKED / 2, MASKED, ALU.is_gt, ALU.mult))
                                    own = smask[:, t, t * P:m]
                                    ins = nc.vector.tensor_tensor(own, own, maskb[:, 2, :], ALU.min)
                                    if t == 0:
                                        link(ins)
                                ins.then_inc(mask_ready, 1)


_INS = ["x", "c", "positions", "ab_w_in", "ab_q_norm", "ab_w_uq", "ab_w_uiq", "ab_sinks", "ab_w_out", "c_w_in", "c_w_out",
        "ada_w", "ada_b", "ln_g", "ln_b", "mlp_w1", "mlp_w2", "p_2", "norm_g_2", "a_w_in_2", "a_rpb_2", "a_w_out_2",
        "b_w_in_2", "b_q_norm_2", "b_k_norm_2", "b_w_out_2", "ple_norm_g_2", "ple_w_gate_2", "ple_w_proj_2", "final_norm_g_2"]


def kernel(**inputs):
    import concourse.bacc as bacc
    from concourse.bass_utils import run_bass_kernel_spmd

    nc = bacc.Bacc("TRN2", target_bir_lowering=False, num_devices=1)
    arrays, rows = {}, {}
    for name in _INS:
        a = np.ascontiguousarray(inputs[name])
        arrays[f"in_{name}"] = a
        rows[name] = nc.dram_tensor(f"in_{name}", a.shape, mybir.dt.from_np(a.dtype), kind="ExternalInput").ap()
    arrays["in_consts"] = constants()
    rows["consts"] = nc.dram_tensor("in_consts", (P, N_CONST), F32, kind="ExternalInput").ap()
    out = nc.dram_tensor("out_0", (1, S, D), F32, kind="ExternalOutput").ap()
    toeplitz = nc.dram_tensor("toeplitz", (2, 16, 6, 128), F32, kind="Internal")
    block_kernel(nc, rows, out, toeplitz)
    r = run_bass_kernel_spmd(nc, [arrays], core_ids=[0])
    return r.results[0]["out_0"]
```

```python
from contextlib import ExitStack

import numpy as np

import concourse.bass as bass
from concourse import mybir

F32 = mybir.dt.float32
F32R = mybir.dt.float32r
BF16 = mybir.dt.bfloat16
I32 = mybir.dt.int32
U32 = mybir.dt.uint32
ALU = mybir.AluOpType
ACT = mybir.ActivationFunctionType
AX = mybir.AxisListType.X

P = 128
S = 256
T = S // P
D = 1024
KD = D // P
HD = 64
FF = 4 * D
N_SUB = 4
ALPHA = 4 ** 0.25
LN_EPS = 1e-5
RMS_EPS = 1e-6
SCALE = HD ** -0.5
MASKED = -1e30
PICKED = -3e38
GRID = 64
IW_SCALE = 8 ** -0.5 * HD ** -0.5
TWO_PI = 2 * np.pi
C1 = 6.28125
C2 = float(np.float32(np.round((TWO_PI - C1) * 2 ** 20) / 2 ** 20))
C3 = float(np.float32(TWO_PI - C1 - C2))
ROUND = 1.5 * 2 ** 23
RSQRT_MAGIC = float(0x5F3759DF)

TILE = 2048
RAW_SLOTS = 5
TURN_LAG = 3
OUT_LAG = 4
HEADS_HELD = 6
HIGH_SLOTS = 3

CONST = {}
_at = 0
for _name, _n in (("ident", P), ("ones", P), ("causal", P), ("window", P), ("invf", HD), ("sign", HD),
                  ("axcos", T * HD), ("axsin", T * HD), ("near", GRID)):
    CONST[_name] = (_at, _at + _n)
    _at += _n
N_CONST = _at

VEC_A = {"ada_b": 0, "c": 96}
N_VEC_A = 104
VEC_B = {"ln_g": 0, "ln_b": 32, "norm_g": 64, "ple_g": 80, "q_norm": 96}
N_VEC_B = 98


def constants():
    out = np.zeros((P, N_CONST), np.float32)

    def put(name, value):
        a, b = CONST[name]
        out[:, a:b] = value

    row = np.arange(P)[:, None]
    col = np.arange(P)[None, :]
    put("ident", np.eye(P))
    put("ones", 1.0)
    put("causal", np.where(col <= row, 0.0, MASKED))
    put("window", np.where(col > row, 0.0, MASKED))
    inv = 10000.0 ** (-np.arange(0, HD, 2) / HD)
    put("invf", np.concatenate([inv, inv])[None, :])
    put("sign", np.concatenate([-np.ones(HD // 2), np.ones(HD // 2)])[None, :])
    quarter = HD // 4
    inv = 10000.0 ** (-np.arange(quarter) * 2.0 / (HD // 2))
    token = np.arange(S).reshape(T, P).T
    ang = np.stack([(token // GRID)[:, :, None] * inv, (token % GRID)[:, :, None] * inv], 2)
    put("axcos", np.stack([np.cos(ang), np.cos(ang)], 3).reshape(P, T * HD))
    put("axsin", np.stack([-np.sin(ang), np.sin(ang)], 3).reshape(P, T * HD))
    c = np.arange(P)[:, None] % GRID
    start = np.clip(c - 8, 0, GRID - 16)
    key = np.arange(GRID)[None, :]
    put("near", np.where((key >= start) & (key < start + 16), 0.0, MASKED))
    return out


def make_plan(R):
    plan, tiles = [], []
    count = {"split": 0, "ada": 0, "job": 0, "rows": 0, "cut": 0, "head": 0, "score": 0, "ssq": 0, "high": 0, "x": 0, "half": 0}
    cuts = {}
    uses = [0] * 8
    cut_of = {}
    pair = [0]
    updated = {}
    gate_jobs = []

    def tick(name, n=1):
        count[name] += n
        return count[name]

    def rows():
        return tick("rows")

    def add(kind, **k):
        plan.append({"kind": kind, **k})
        return plan[-1]

    def banks(pairs=None):
        if pairs is None:
            b = 2 * (pair[0] % 2)
            pair[0] += 1
            pairs = (b, b + 1)
        got = [(b, uses[b]) for b in pairs]
        for b in pairs:
            uses[b] += 1
        return got

    ride = [0, 1, 0]

    def tile(view, kc, cols, kind):
        if kind == "split" and ride[0]:
            ride[2] += 1
            if ride[2] % ride[1] == 0:
                ride[0] -= 1
                ada_tiles(1)
                tiles[-1]["riding"] = True
        tiles.append({"view": view, "kc": kc, "cols": cols, "kind": kind, "n": tick(kind) - 1})
        return tiles[-1]["n"]

    def job(kind, pairs=None, **k):
        return add(kind, banks=banks(pairs), job=tick("job"), **k)

    def linear(w, c0, width, kc, lhs, end, between=None):
        return linears([(w, c0, width, kc, lhs, end)], between)

    def linears(ofs, between=None):
        known = dict(cuts)
        own = [banks() for _ in ofs]
        pair_after = pair[0]
        for h in range(2 if ofs[0][3] > 4 else 1):
            for bk, (w, c0, width, kc, lhs, end) in zip(own, ofs):
                step = min(4, kc)
                v = w.rearrange("(k p) n -> p k n", p=P)
                n = tile(v[:, h * step:(h + 1) * step, c0:c0 + width], step, width, "split")
                last = h == kc // step - 1
                it = add("tokens", tile=n, kc=step, width=width, lhs=lhs, off=h * step, banks=bk,
                         first=h == 0, last=last, cut=(cuts if len(ofs) > 1 else known)[lhs][h], enter=h == 0, half=tick("half"))
                if between:
                    between()
                    between = None
                    pair[0] = pair_after
                if last:
                    it["end"] = end
        return it

    def split_rows(src, chunks, dst, wait, affine=None, halves=(0, 1)):
        for half in halves:
            a = 4 * half
            n = min(4, chunks - a)
            nb = (n + 1) // 2
            it = job("turn_split", None if chunks <= 4 else (4 + 2 * half, 5 + 2 * half), src=src, a=a, n=n, dst=dst,
                     wait=wait, affine=affine)
            if src == "x" and updated:
                it["updated"] = updated[half]
            it["banks"] = it["banks"][:nb]
            if nb == 1:
                uses[it["banks"][0][0] + 1] -= 1
            it["heads"] = count["head"] - (8 if a == 0 else 0)
            it["high"] = tick("high")
            place = it["banks"][0][0] % 4
            it["emptied"] = cut_of.get(place, 0)
            tick("cut", nb)
            cut_of[place] = count["cut"]
            cuts[dst] = (count["cut"] if a == 0 else cuts[dst][0], count["cut"])

    def gate(s):
        gate_jobs.append(count["job"] + 1)
        return job("gate_row", s=s)

    def turn(src_cols, dst, wait, before=None, firsts=None, shared=0):
        before = before or list(uses)
        for i, a in enumerate(firsts or range(0, len(src_cols), 4)):
            own = {1: (4, 5), 2: (6, 7)} if len(firsts or ()) == 4 else {1: (4, 5)} if firsts else {}
            job("turn", own.get(i), shared=shared, cols=src_cols[a:a + 4], dst=dst + a, wait=wait,
                before=before)

    def heads(kind, spec):
        it = add("heads", mode=kind, spec=spec, s0=count["score"], h0=count["head"], uses=list(uses))
        tick("score", len(spec))
        if kind != "index":
            tick("head", len(spec))
        return it

    def ada_tiles(n):
        for i in range(count["ada"], count["ada"] + n):
            s, part, k = i // 12, i // 4 % 3, i % 4
            w = R["ada_w"][s // 2, s % 2].rearrange("(k p) n -> p k n", p=P)
            tile(w[:, 2 * k:2 * k + 2, part * D:(part + 1) * D], 2, D, "ada")
            tiles[-1].update(s=s, part=part, k=2 * k)

    def spread(n, every):
        ride[:] = [n, every, 0]

    def ada(s):
        it = add("ada_columns", s=s, banks=banks((4 if s else 0,)), job=tick("job"))
        it["ada"] = 12 * s + 8

    def mlp(layer, end):
        w1 = R["mlp_w1"][layer].rearrange("(k p) n -> p k n", p=P)
        w2 = R["mlp_w2"][layer].rearrange("(k p) n -> p k n", p=P)
        yb = {n: banks((4 + 2 * n, 5 + 2 * n)) for n in range(2)}
        hid_cut = {}
        enter = {0: True, 1: True}
        need = cuts["ht"]

        def up(g):
            for j in range(2):
                bk = banks()
                for h in range(2):
                    c0 = g * 1024 + j * 512 + h * 256
                    n = tile(w1[:, :, c0:c0 + 256], KD, 256, "split")
                    it = add("hidden", tile=n, half=h, banks=bk, cut=need, buf=g % 2, c0=4 * j)
                it["end"] = "hidden"
                it["high"] = tick("high")
                it["emptied"] = cut_of.get(bk[0][0], 0)
                tick("cut", 2)
                cut_of[bk[0][0]] = count["cut"]
            hid_cut[g] = count["cut"]

        def down(g):
            for n in range(2):
                for h in range(2):
                    k0 = g * 8 + h * 4
                    t = tile(w2[:, k0:k0 + 4, n * 512:(n + 1) * 512], 4, 512, "split")
                    it = add("tokens", tile=t, kc=4, width=512, lhs=("hid", g % 2), off=h * 4, banks=yb[n],
                             first=g == 0 and h == 0, last=g == 3 and h == 1, cut=hid_cut[g], enter=g == 0 and h == 0, half=tick("half"))
                if g == 3:
                    it["end"] = ("y_ln", n, 2 * layer + 1)

        up(0)
        gate(2 * layer + 1)
        if layer == 0:
            spread(12, 2)
        up(1), down(0), up(2), down(1), up(3), down(2), down(3)

    def norm_ln(s):
        it = add("ln", s=s)
        it["rows"] = tick("rows", 2)
        return it["rows"]

    def norm_rms(i):
        add("rms", ssq=count["ssq"], i=i)

    def x_rows(gain, half):
        split_rows("x", KD, "ht", 0, ("vec", gain), halves=(half,))

    job("turn_vectors")
    uses[1] -= 1
    ada_tiles(8)
    spread(4, 2)
    w = R["ab_w_in"][0]
    split_rows("x", KD, "ht", 0, ("affine", 0))
    ada(0)
    linear(w, 0, 512, KD, "ht", ("tok", 0, 1.0, 512))
    add("rope_tables")
    add("rope", what=[(0, 8, None)], rows=rows(), uses=list(uses))
    aq_rows = count["rows"]
    before = list(uses)
    linear(w, 512, 512, KD, "ht", ("tok", 512, 1.0, 512))
    add("low_rank", rows=rows(), uses=list(uses))
    cq_rows = count["rows"]
    linear(w, 1024, 200, KD, "ht", ("tok", 1024, 1.0, 200))
    split_rows("cq", 2, "plt", cq_rows, ("vec", VEC_B["q_norm"]), halves=(0,))
    turn([0, 128, 256, 384], 0, aq_rows, before)
    linear(R["ab_w_uiq"][0], 0, 512, 2, "plt", ("tok", 1792, 1.0, 512))
    add("rope", what=[(512, 2, 2304), (1024, 1, 2560), (1152, 1, 2688)], rows=rows(), uses=list(uses))
    key_rows = count["rows"]
    add("rope", what=[(1792, 8, None)], rows=rows(), uses=list(uses))
    biq_rows = count["rows"]
    before = list(uses)
    linear(R["ab_w_uq"][0], 0, 512, 2, "plt", ("tok", 1280, 1.0, 512))
    add("rope", what=[(1280, 8, None)], rows=rows(), uses=list(uses))
    ada_tiles(12)
    turn([2304, 2432, 2560, 2688], 4, key_rows, before)
    turn([1792, 1920, 2048, 2176], 12, biq_rows, before)
    turn([1280, 1408, 1536, 1664], 8, count["rows"])
    gate(0)
    heads("index", [(12 + h // 2, h % 2, 7, None, h) for h in range(8)])
    heads("window", [(h // 2, h % 2, 4 + h // 4, 640 + HD * (h // 4), h) for h in range(8)])
    heads("sparse", [(8 + h // 2, h % 2, 6, 1088, 8 + h) for h in range(8)])
    split_rows("o", KD, "ht", 0)
    for n in range(2):
        linear(R["ab_w_out"][0], n * 512, 512, KD, "ht", ("y_ln", n, 0))
    r = norm_ln(0)
    ada(1)
    split_rows("xhat", KD, "ht", r, ("affine", 1))
    mlp(0, None)
    r = norm_ln(1)
    ada(2)
    split_rows("xhat", KD, "ht", r, ("affine", 2))
    w = R["c_w_in"][0]
    for j in range(4):
        linear(w, j * 512, 512, KD, "ht", ("tok", j * 512, 1.0, 512))
        add("rope", what=[(j * 512, 8, None)], rows=rows(), uses=list(uses))
        if j == 0:
            gate(2)
            spread(8, 2)
    before = list(uses)
    for j in range(4, 6):
        linear(w, j * 512, 512, KD, "ht", ("tok", j * 512, 1.0, 512))
    ada_tiles(4)
    turn([P * i for i in range(16)], 0, count["rows"], before, firsts=(0, 4, 12, 8))
    heads("causal", [(h // 2, h % 2, 8 + h // 2, 2048 + HD * h, h) for h in range(16)])
    split_rows("o", KD, "ht", 0)
    for n in range(2):
        linear(R["c_w_out"][0], n * 512, 512, KD, "ht", ("y_ln", n, 2))
    r = norm_ln(2)
    ada(3)
    split_rows("xhat", KD, "ht", r, ("affine", 3))
    mlp(1, None)
    last_rows = norm_ln(3)
    def stream_rows():
        add("resid", s=3)
        tick("ssq", 4)

    for i in range(2):
        r = 2 * i
        if i == 0:
            split_rows("xhat", KD, "ht", last_rows, ("affine", 4))
            w = R["a_w_in_2"][0]
            for j in (0, 1, 2, 3, 6, 7, 4, 5):
                if j == 1:
                    norm_rms(r)
                end = ("tok", j * 512, (r, 0), 512) if j < 6 else ("silu", j * 512, (r, 1), 512, j - 6)
                linear(w, j * 512, 512, KD, "ht", end, between=stream_rows if j == 0 else None)
                if j in (2, 7):
                    add("bias_table", rows=rows(), part=int(j > 2))
                if j == 3:
                    before = list(uses)
            turn([P * j for j in range(16)], 0, count["rows"], before, firsts=(0, 4, 12, 8))
            heads("near", [(h // 2, h % 2, 8 + h // 2, 2048 + HD * h, h) for h in range(16)])["gate"] = 3072
        else:
            w = R["b_w_in_2"][0]

            def second_half():
                x_rows(VEC_B["norm_g"] + KD, 1)
                norm_rms(r)

            linears([(w, c0, 512, KD, "ht", ("tok", c0, (r, 0), 512)) for c0 in (1024, 0)], second_half)
            add("qk_rope", what=[(1024, 4, 2560)], gain="k", shared=0, rows=rows(), uses=list(uses))
            for j in range(2):
                if j:
                    linear(w, j * 512, 512, KD, "ht", ("tok", j * 512, (r, 0), 512))
                    before = list(uses)
                    add("qk_rope", what=[(j * 512, 8, None)], gain="q", shared=j + 1, rows=rows(), uses=list(uses))
                linear(w, (3 + j) * 512, 512, KD, "ht", ("silu", (3 + j) * 512, (r, 1), 512, j))
                if j == 0:
                    add("qk_rope", what=[(j * 512, 8, None)], gain="q", shared=j + 1, rows=rows(), uses=list(uses))
            turn([P * j for j in range(8)] + [2560 + P * j for j in range(4)], 0, count["rows"], before, firsts=(8, 4, 0), shared=2)
            heads("full", [(h // 2, h % 2, 8 + h // 4, 1280 + HD * (h // 4), h) for h in range(16)])["gate"] = 1536
        split_rows("o", KD, "ht", 0)
        w = R[("a" if i == 0 else "b") + "_w_out_2"][0]

        def embedding_rows():
            split_rows(("p", i), 2, "plt", 0, halves=(0,))
            x_rows(VEC_B["ple_g"] + KD * i, 0)

        for n in range(2):
            it = linear(w, n * 512, 512, KD, "ht", ("y_rms", n), between=embedding_rows if n else None)
            updated[n] = ("bank", [(b, used + 1) for b, used in it["banks"]])
            if n == i == 0:
                add("axial_tables")
            tick("ssq", 2)
        for n in range(2):
            linear(R["ple_w_proj_2"][i], n * 512, 512, 2, "plt", ("tok", n * 512, 0.5, 512))
        x_rows(VEC_B["ple_g"] + KD * i, 1)
        norm_rms(r + 1)
        for n in range(2):
            between = (lambda: x_rows(VEC_B["norm_g"] + KD, 0)) if n and i == 0 else None
            it = linear(R["ple_w_gate_2"][i], n * 512, 512, KD, "ht", ("ple", n, r + 1), between=between)
            it["x"] = tick("x", 2)
            updated[n] = ("x", it["x"])
            tick("ssq", 2)
    add("final", ssq=count["ssq"], rows=tick("rows", 2))
    for it, after in zip(plan, plan[1:]):
        if "tile" in it:
            late = after["kind"] in ("turn_split", "ln", "turn", "ada_columns", "heads")
            it["ahead"] = it["tile"] + (1 if late else 2)
    assert ride[0] == 0 and count["ada"] == 12 * N_SUB
    split = [t for t in tiles if t["kind"] == "split"]
    order = tiles[:8] + split[:2]
    for t in tiles[8:]:
        if t["kind"] == "ada":
            order.append(t)
        elif t["n"] + 2 < len(split):
            order.append(split[t["n"] + 2])
    for i, t in enumerate(tiles):
        t["turn"] = i + (2.5 if t.get("riding") else 0)
    held, filled = [None] * RAW_SLOTS, [0] * RAW_SLOTS
    for t in order:
        slot = min(range(RAW_SLOTS), key=lambda i: (held[i]["turn"] if held[i] else -1, i))
        filled[slot] += 1
        t["slot"], t["full"], t["old"] = slot, 16 * filled[slot], held[slot]
        held[slot] = t
    adas = [t for t in tiles if t["kind"] == "ada"]
    for t in adas:
        if t["s"]:
            t["gate_job"] = gate_jobs[t["s"] - 1]
            t["columns_job"] = next(i["job"] for i in plan if i["kind"] == "ada_columns" and i["s"] == t["s"] - 1)
    return plan, order, split, adas


def block_kernel(nc, R, out, toeplitz):
    plan, order, split, adas = make_plan(R)
    p_after = [i["h0"] + len(i["spec"]) for i in plan if i["kind"] == "heads" and i["mode"] in ("near", "full")]

    with ExitStack() as ctx:
        def sb(name, shape, dt=F32):
            return ctx.enter_context(nc.sbuf_tensor(name, shape, dt))

        def sem(name):
            return ctx.enter_context(nc.semaphore(name))

        x = sb("x", [P, T, D])
        u = sb("u", [P, T, D])
        ht_hi = sb("ht_hi", [P, KD, S], F32R)
        ht_lo = sb("ht_lo", [P, KD, S], F32R)
        plt_hi = sb("plt_hi", [P, 2, S], F32R)
        plt_lo = sb("plt_lo", [P, 2, S], F32R)
        tok = sb("tok", [P, T, 4 * D])
        qkt = sb("qkt", [P, 16, S])
        near_bias = sb("near_bias", [P, 16, 6 * GRID])
        raw = sb("raw", [P, RAW_SLOTS, TILE])
        w_hi = sb("w_hi", [P, HIGH_SLOTS, TILE], F32R)
        full = sb("full", [P, 4, 512])
        probs = sb("probs", [P, 3, T, S])
        probs_t = sb("probs_t", [P, 2, T, S])
        biased = sb("biased", [P, 2, T, S])
        tmp_a = sb("tmp_a", [P, 512])
        tmp_b = sb("tmp_b", [P, 512])
        consts = sb("consts", [P, N_CONST])
        vec = sb("vec", [P, N_VEC_A + N_VEC_B])
        cs = sb("cs", [P, 3, KD])
        mod = sb("mod", [P, 2 * KD])
        aff = sb("aff", [P, 2, KD])
        pos_i = sb("pos_i", [P, T], I32)
        pos_f = sb("pos_f", [P, T])
        cosr = sb("cosr", [P, T, HD])
        sinr = sb("sinr", [P, T, HD])
        gain = sb("gain", [P, 2, HD])
        stats = sb("stats", [P, T, 2, 6])
        meanvar = sb("meanvar", [P, T, 2])
        ssq = sb("ssq", [P, T, 2])
        rms = sb("rms", [P, 4, 2, T])
        small = sb("small", [P, 3, 16])
        bits = sb("bits", [P, 16], U32)
        rstd = sb("rstd", [P, 16])
        sinks = sb("sinks", [P, 2, 8])
        mx = sb("mx", [P, HEADS_HELD, T])
        nmx = sb("nmx", [P, HEADS_HELD, T])
        sums = sb("sums", [P, HEADS_HELD, T])
        rs = sb("rs", [P, HEADS_HELD, T])
        sink_exp = sb("sink_exp", [P, HEADS_HELD, T])
        iw = sb("iw", [P, T, 8])
        top8 = sb("top8", [P, 8])
        maskb = sb("maskb", [P, 3, P], BF16)
        smask = sb("smask", [P, T, S], BF16)

        def over(owner, offset, name, shape, dt=F32):
            return nc.alloc_sbuf_tensor_at(name, shape, dt, offset=nc.lookup_mloc(owner).addr + offset)

        w_lo = over(raw, 0, "w_lo", [P, RAW_SLOTS, TILE], F32R)
        hid_hi = over(tok, 0, "hid_hi", [P, 2, KD, S], F32R)
        hid_lo = over(tok, 2 * KD * S * 4, "hid_lo", [P, 2, KD, S], F32R)
        g_row = over(near_bias, 0, "g_row", [P, D])
        b_row = over(near_bias, 4 * D, "b_row", [P, D])
        gate_row = over(near_bias, 8 * D, "gate_row", [P, D])
        ada_sum = over(near_bias, 12 * D, "ada_sum", [P, 3, D])
        score = over(plt_hi, 0, "score", [P, T, S])
        near_rev = over(qkt, 0, "near_rev", [P, 48, GRID])
        rpb_rows = over(qkt, 12 * D, "rpb_rows", [16, 7, 128])
        rpb_in_rows = over(probs_t, 0, "rpb_in_rows", [16, 7, 31])
        vec_rows = over(qkt, 4 * D, "vec_rows", [P, 2, P])
        ax = over(near_bias, 8 * D, "ax", [P, 2, 2, T, HD])
        angle = over(biased, 0, "angle", [P, 3, T, HD])
        junk = over(probs, 4 * D, "junk", [P, 512])
        g_final = over(near_bias, 0, "g_final", [P, D])
        p_rows = over(probs, 0, "p_rows", [P, T, S])
        pool_a = over(probs, 0, "pool_a", [P, 512])
        pool_b = over(probs, 2 * D, "pool_b", [P, 512])
        assert nc.lookup_mloc(near_bias).dims[1] >= 24 * D

        bank = [ctx.enter_context(nc.psum_tensor(f"bank{b}", [P, 512], F32)) for b in range(8)]

        raw_in = [sem(f"raw_in{i}") for i in range(RAW_SLOTS)]
        const_in = sem("const_in")
        vec_in = sem("vec_in")
        x_in = sem("x_in")
        gate_in = sem("gate_in")
        row_in = sem("row_in")
        p_in = [sem(f"p_in{i}") for i in range(2)]
        misc_in = sem("misc_in")
        rpb_in = sem("rpb_in")
        pad_out = sem("pad_out")
        bias_in = [sem(f"bias_in{i}") for i in range(2)]
        final_in = sem("final_in")
        out_done = sem("out_done")
        high_done = sem("high_done")
        low_done = sem("low_done")
        tile_done = sem("tile_done")
        half_done = sem("half_done")
        ada_done = sem("ada_done")
        job_done = sem("job_done")
        bank_free = [sem(f"bank_free{b}") for b in range(8)]
        high_copied = sem("high_copied")
        split_done = sem("split_done")
        scaled = sem("scaled")
        pool_rows = sem("pool_rows")
        rows_ready = sem("rows_ready")
        silu_ready = sem("silu_ready")
        affine_ready = sem("affine_ready")
        resid_done = sem("resid_done")
        first_rows = sem("first_rows")
        x_ready = sem("x_ready")
        rms_ready = sem("rms_ready")
        ssq_ready = sem("ssq_ready")
        tanh_ready = sem("tanh_ready")
        angle_ready = sem("angle_ready")
        sin_ready = sem("sin_ready")
        scores_ready = sem("scores_ready")
        negmax_ready = sem("negmax_ready")
        scores_used = sem("scores_used")
        probs_turned = sem("probs_turned")
        turned_copied = [sem("turned_copied_act"), sem("turned_copied_dve")]
        head_out = sem("head_out")
        head_copied = sem("head_copied")
        index_used = sem("index_used")
        mask_ready = sem("mask_ready")
        act_step = sem("act_step")
        dve_step = sem("dve_step")
        pool_step = sem("pool_step")

        def const(name):
            a, b = CONST[name]
            return consts[:, a:b]

        ident = const("ident")
        sources = {"x": x, "xhat": u, "o": u}

        def raw_tile(t):
            return raw[:, t["slot"], 0:t["kc"] * t["cols"]]

        def split_parts(n):
            t = split[n]
            size = t["kc"] * t["cols"]
            return w_hi[:, n % HIGH_SLOTS, 0:size], w_lo[:, t["slot"], 0:size]

        def views(n):
            return [v.rearrange("p (k n) -> p k n", k=split[n]["kc"]) for v in split_parts(n)]

        def source(it, t, c):
            if it["src"] == "cq":
                return tok[:, t, 768 + c * P:768 + (c + 1) * P]
            if it["src"][0] == "p":
                return p_rows[:, t, c * P:(c + 1) * P]
            return sources[it["src"]][:, t, c * P:(c + 1) * P]

        def came(engine, it, t):
            if t == 0:
                engine.wait_ge(half_done, it["half"])
            else:
                engine.wait_ge(tile_done, it["tile"] + 1)

        def rope_products(ops, q, ta, tb, nh, cos, sin, groups, half):
            heads_of = "p (h d) -> p h d"
            ops.tensor_tensor(ta.rearrange(heads_of, h=nh), q.rearrange(heads_of, h=nh), cos.unsqueeze(1).broadcast_to([P, nh, HD]),
                              ALU.mult)
            for a in range(2):
                qv = q.rearrange("p (h g a d) -> p h g a d", h=nh, g=groups, a=2)[:, :, :, 1 - a, :]
                tv = tb.rearrange("p (h g a d) -> p h g a d", h=nh, g=groups, a=2)[:, :, :, a, :]
                sv = sin.rearrange("p (g a d) -> p g a d", g=groups, a=2)[:, :, a, :].unsqueeze(1).broadcast_to([P, nh, groups, half])
                if groups == 1:
                    qv, tv, sv = qv[:, :, 0, :], tv[:, :, 0, :], sv[:, :, 0, :]
                ins = ops.tensor_tensor(tv, qv, sv, ALU.mult)
            return ins

        pool_steps = [0]

        def ada_products(engine, ops, n):
            t = adas[n]
            if n in (0, 8):
                engine.wait_ge(silu_ready, 1)
            if n == 8:
                engine.wait_ge(ada_done, 16)
            if t["s"] and t["k"] == 0 and t["part"] in (0, 2):
                engine.wait_ge(job_done, t["gate_job"] if t["part"] else t["columns_job"])
            engine.wait_ge(raw_in[t["slot"]], t["full"])
            w = raw_tile(t).rearrange("p (k n) -> p k n", k=2)
            dst = ada_sum[:, t["part"], :]
            for i in range(2):
                c = cs[:, 0, t["k"] + i:t["k"] + i + 1]
                if t["k"] + i == 0:
                    ins = ops.tensor_tensor(dst, w[:, i, :], c.broadcast_to([P, D]), ALU.mult)
                elif n < 8:
                    ins = ops.scalar_tensor_tensor(dst, w[:, i, :], c, dst, ALU.mult, ALU.add)
                else:
                    ops.tensor_tensor(w[:, i, :], w[:, i, :], c.broadcast_to([P, D]), ALU.mult).then_inc(pool_step, 1)
                    pool_steps[0] += 1
                    engine.wait_ge(pool_step, pool_steps[0])
                    ins = ops.tensor_tensor(dst, w[:, i, :], dst, ALU.add)
                ins.then_inc(ada_done, 1)
                engine.wait_ge(ada_done, 2 * n + i + 1)

        def parts(it):
            return (plt_hi, plt_lo) if it["dst"] == "plt" else (ht_hi, ht_lo)

        def head_cols(mode, t):
            return P * (t + 1) if mode in ("causal", "window", "sparse", "index") else S

        def turned_halves(mode, h):
            dst, src = probs_t[:, h % 2, :, :], bank[4 + h % 2][:, :].rearrange("p (k q) -> p k q", k=T)
            if mode in ("near", "full"):
                return [(dst, src)]
            return [(dst[:, 0, :], src[:, 0, :]), (dst[:, 1, P:S], src[:, 1, P:S])]

        block = ctx.enter_context(nc.Block())

        @block.sync
        def _(sp):
            sp.dma_start(consts[:, :], R["consts"]).then_inc(const_in, 16)
            ada_rows = R["ada_b"].rearrange("l s (j p) -> (l s j) p", p=P)
            ln_rows = [R[n].rearrange("l s (j p) -> (l s j) p", p=P) for n in ("ln_g", "ln_b")]
            sp.dma_start(vec_rows[0:96, 0, :], ada_rows).then_inc(vec_in, 16)
            sp.dma_start(vec_rows[96:104, 0, :], R["c"].rearrange("b (j p) -> (b j) p", p=P)).then_inc(vec_in, 16)
            sp.dma_start(vec_rows[0:32, 1, :], ln_rows[0]).then_inc(vec_in, 16)
            sp.dma_start(vec_rows[32:64, 1, :], ln_rows[1]).then_inc(vec_in, 16)
            for name, a, n in (("norm_g_2", 64, 16), ("ple_norm_g_2", 80, 16), ("ab_q_norm", 96, 2)):
                sp.dma_start(vec_rows[a:a + n, 1, :], R[name].rearrange("l (j p) -> (l j) p", p=P)).then_inc(vec_in, 16)
            with nc.allow_non_contiguous_dma("256 positions"):
                sp.dma_start(pos_i[:, :], R["positions"][0].rearrange("(t p) -> p t", p=P)).then_inc(const_in, 16)
            for r, t in enumerate(order):
                if r == 4:
                    sp.dma_start(x[:, :, :], R["x"][0].rearrange("(t p) d -> p t d", p=P)).then_inc(x_in, 16)
                old = t["old"]
                if old:
                    if old["kind"] == "split":
                        sp.wait_ge(tile_done, old["n"] + 1)
                    else:
                        sp.wait_ge(ada_done, 2 * (old["n"] + 1))
                dst = raw_tile(t).rearrange("p (k n) -> p k n", k=t["kc"])
                sp.dma_start(dst, t["view"]).then_inc(raw_in[t["slot"]], 16)
            for t in range(T):
                sp.wait_ge(rows_ready, plan[-1]["rows"] - T + t + 1)
                sp.dma_start(out[0, t * P:(t + 1) * P, :], u[:, t, :]).then_inc(out_done, 16)
            sp.wait_ge(out_done, 16 * T)

        @block.gpsimd
        def _(pool):
            norm_rows = [i["rows"] for i in plan if i["kind"] == "ln"]
            pool.dma_start(sinks[:, 0, :], R["ab_sinks"][0].partition_broadcast(P)).then_inc(misc_in, 16)
            pool.dma_start(gain[:, 0, :], R["b_q_norm_2"][0].partition_broadcast(P)).then_inc(misc_in, 16)
            pool.dma_start(gain[:, 1, :], R["b_k_norm_2"][0].partition_broadcast(P)).then_inc(misc_in, 16)
            for s in range(N_SUB):
                if s:
                    pool.wait_ge(resid_done, T * s)
                else:
                    pool.wait_ge(ada_done, 16)
                gate_bias = R["ada_b"][s // 2, s % 2, 2 * D:3 * D]
                pool.dma_start(gate_row[:, :], gate_bias.partition_broadcast(P)).then_inc(gate_in, 16)
                pool.dma_start(g_row[:, :], R["ln_g"][s // 2, s % 2].partition_broadcast(P)).then_inc(row_in, 16)
                pool.dma_start(b_row[:, :], R["ln_b"][s // 2, s % 2].partition_broadcast(P)).then_inc(row_in, 16)
                for n, t in enumerate(adas):
                    if n >= 8 and (t["s"] == s + 1 or n < 12 and s == 0):
                        ada_products(pool, nc.gpsimd, n)
                pool.wait_ge(row_in, 32 * (s + 1))
                for t in range(0 if s < 3 else 1, T):
                    pool.wait_ge(rows_ready, norm_rows[s] - T + t + 1)
                    nc.gpsimd.tensor_tensor(x[:, t, :], u[:, t, :], g_row[:, :], ALU.mult).then_inc(pool_step, 1)
                    pool_steps[0] += 1
                    pool.wait_ge(pool_step, pool_steps[0])
                    nc.gpsimd.tensor_tensor(x[:, t, :], x[:, t, :], b_row[:, :], ALU.add).then_inc(resid_done, 1)
            nc.gpsimd.memset(rpb_rows[:, :, :], 0.0).then_inc(pool_step, 1)
            pool.dma_start(rpb_in_rows[:, :, :], R["a_rpb_2"][0, :, 4:11, :]).then_inc(rpb_in, 16)
            pool.wait_ge(rpb_in, 16)
            pool.wait_ge(pool_step, pool_steps[0] + 1)
            nc.gpsimd.tensor_copy(rpb_rows[:, :, 49:80], rpb_in_rows[:, :, ::-1]).then_inc(pool_step, 1)
            pool.wait_ge(pool_step, pool_steps[0] + 2)
            for half in range(2):
                pool.dma_start(toeplitz[half, :, :, :], rpb_rows[:, 1 - half:7 - half, :]).then_inc(pad_out, 16)
            pool.wait_ge(pad_out, 32)
            for part in range(2):
                if part:
                    pool.wait_ge(rows_ready, next(i["rows"] for i in plan if i["kind"] == "bias_table"))
                for half in range(2):
                    pool.dma_start(
                        near_rev[half * GRID:(half + 1) * GRID, :, :],
                        bass.AP(toeplitz, ((half * 2 + part) * 48) * 128 + 1, [[1, GRID], [128, 48], [1, GRID]]),
                    ).then_inc(bias_in[part], 16)
            for i in range(2):
                pool.wait_ge(probs_turned, p_after[i])
                pool.dma_start(p_rows[:, :, :], R["p_2"][i, 0].rearrange("(t p) d -> p t d", p=P)).then_inc(p_in[i], 16)
                if i == 0:
                    for it in plan:
                        if it["kind"] == "qk_rope" and it["shared"]:
                            pool.wait_ge(scaled, it["shared"])
                            q = tok[:, 1, it["what"][0][0]:it["what"][0][0] + 512]
                            rope_products(nc.gpsimd, q, pool_a[:, :], pool_b[:, :], 8, ax[:, 0, 0, 1, :], ax[:, 0, 1, 1, :], 2, HD // 4)\
                                .then_inc(pool_step, 1)
                            pool_steps[0] += 1
                            pool.wait_ge(pool_step, pool_steps[0] + 2)
                            nc.gpsimd.tensor_tensor(q, pool_a[:, :], pool_b[:, :], ALU.add).then_inc(pool_rows, 1)
                            pool.wait_ge(pool_rows, it["shared"])
                    pool.dma_start(g_final[:, :], R["final_norm_g_2"].partition_broadcast(P)).then_inc(final_in, 16)

        @block.scalar
        def _(act):
            steps = [0]

            def link(ins):
                steps[0] += 1
                ins.then_inc(act_step, 1)
                act.wait_ge(act_step, steps[0])

            highs = [0]

            def split_high(until):
                for n in range(highs[0], min(until + 1, len(split))):
                    high_part(n)
                highs[0] = max(highs[0], until + 1)

            def high_part(n):
                t = split[n]
                act.wait_ge(raw_in[t["slot"]], t["full"])
                if n >= HIGH_SLOTS:
                    act.wait_ge(tile_done, n - HIGH_SLOTS + 1)
                nc.scalar.activation(split_parts(n)[0], raw_tile(t), ACT.Copy).then_inc(high_done, 1)

            def squares(t, n):
                nc.scalar.activation(junk[:, :], x[:, t, n * 512:(n + 1) * 512], ACT.Square,
                                     accum_out=ssq[:, t, n:n + 1]).then_inc(ssq_ready, 1)
                squared[0] += 1
                act.wait_ge(ssq_ready, squared[0])

            squared = [0]
            act.wait_ge(bank_free[0], 1)
            nc.scalar.activation(cs[:, 1, :], vec[:, VEC_A["c"]:VEC_A["c"] + KD], ACT.Tanh, scale=0.5).then_inc(tanh_ready, 1)
            split_high(1)
            act.wait_ge(angle_ready, 1)
            nc.scalar.activation(sinr[:, :, :], angle[:, 1, :, :], ACT.Sin).then_inc(sin_ready, 1)
            nc.scalar.activation(cosr[:, :, :], angle[:, 2, :, :], ACT.Sin).then_inc(sin_ready, 1)

            for it in plan:
                kind = it["kind"]
                if kind == "turn_split":
                    b, used = it["banks"][0]
                    act.wait_ge(job_done, it["job"])
                    if it["emptied"]:
                        act.wait_ge(split_done, it["emptied"])
                    m = min(2, it["n"])
                    hi = parts(it)[0][:, it["a"]:it["a"] + m, :]
                    if it["affine"] and it["affine"][0] == "affine":
                        act.wait_ge(affine_ready, it["affine"][1] + 1)
                    for c in range(m):
                        dst, ps = full[:, b % 4, c * S:(c + 1) * S], bank[b][:, c * S:(c + 1) * S]
                        k = it["a"] + c
                        if it["affine"] is None:
                            ins = nc.scalar.activation(dst, ps, ACT.Copy)
                        elif it["affine"][0] == "affine":
                            ins = nc.scalar.activation(dst, ps, ACT.Identity, scale=aff[:, 0, k:k + 1], bias=aff[:, 1, k:k + 1])
                        else:
                            v = N_VEC_A + it["affine"][1] + k
                            ins = nc.scalar.activation(dst, ps, ACT.Copy, scale=vec[:, v:v + 1])
                    ins.then_inc(bank_free[b], 1)
                    act.wait_ge(bank_free[b], used + 1)
                    nc.scalar.activation(hi, full[:, b % 4, 0:m * S].rearrange("p (c s) -> p c s", c=m), ACT.Copy)\
                        .then_inc(high_copied, 1)

                elif kind == "turn":
                    b, used = it["banks"][0]
                    act.wait_ge(job_done, it["job"])
                    nc.scalar.activation(qkt[:, it["dst"]:it["dst"] + 2, :],
                                         bank[b][:, :].rearrange("p (c s) -> p c s", c=2), ACT.Copy).then_inc(bank_free[b], 1)

                elif kind in ("tokens", "hidden"):
                    n = it["tile"]
                    split_high(it["ahead"])
                    end = it.get("end")
                    if end is None:
                        continue
                    if end == "hidden":
                        b, used = it["banks"][0]
                        act.wait_ge(tile_done, n + 1)
                        if it["emptied"]:
                            act.wait_ge(split_done, it["emptied"])
                        link(nc.scalar.activation(full[:, b, :], bank[b][:, :], ACT.Relu))
                        nc.scalar.activation(full[:, b, :], full[:, b, :], ACT.Square).then_inc(bank_free[b], 1)
                        act.wait_ge(bank_free[b], used + 1)
                        nc.scalar.activation(hid_hi[:, it["buf"], it["c0"]:it["c0"] + 2, :],
                                             full[:, b, :].rearrange("p (c s) -> p c s", c=2), ACT.Copy).then_inc(high_copied, 1)
                    elif end[0] in ("tok", "silu"):
                        c0, scale, width = end[1:4]
                        if isinstance(scale, tuple):
                            act.wait_ge(rms_ready, scale[0] + 1)
                        for t, (b, used) in enumerate(it["banks"]):
                            came(act, it, t)
                            value = rms[:, scale[0], scale[1], t:t + 1] if isinstance(scale, tuple) else scale
                            ins = nc.scalar.activation(tok[:, t, c0:c0 + width], bank[b][:, 0:width], ACT.Copy, scale=value)
                            if end[0] == "silu":
                                ins = nc.scalar.activation(full[:, 2 * end[4] + t, :], bank[b][:, :], ACT.Tanh, scale=value)
                            ins.then_inc(bank_free[b], 1)
                    elif end[0] == "y_rms":
                        for t, (b, used) in enumerate(it["banks"]):
                            act.wait_ge(bank_free[b], used + 1)
                            squares(t, end[1])
                    elif end[0] == "ple":
                        act.wait_ge(rms_ready, end[2] + 1)
                        for t, (b, used) in enumerate(it["banks"]):
                            came(act, it, t)
                            nc.scalar.activation(full[:, 2 * end[1] + t, :], bank[b][:, :], ACT.Tanh, scale=rms[:, end[2], 1, t:t + 1])\
                                .then_inc(bank_free[b], 1)
                        for t in range(T):
                            act.wait_ge(x_ready, it["x"] - T + t + 1)
                            squares(t, end[1])

                elif kind == "resid" and it["s"] == 3:
                    for t in range(T):
                        act.wait_ge(*((resid_done, T * 3 + 1) if t else (first_rows, 1)))
                        for n in range(2):
                            squares(t, n)

                elif kind == "heads":
                    mode, spec, s0, h0 = it["mode"], it["spec"], it["s0"], it["h0"]
                    if mode == "index":
                        for i in range(len(spec)):
                            s = s0 + i
                            act.wait_ge(scores_ready, s + 1)
                            if i >= 2:
                                act.wait_ge(index_used, i - 1)
                            for t in range(T):
                                m = head_cols(mode, t)
                                ins = nc.scalar.activation(biased[:, i % 2, t, 0:m], bank[s % 4][:, t * S:t * S + m], ACT.Relu)
                            ins.then_inc(scores_used, 1)
                        continue
                    for i in range(len(spec) + TURN_LAG):
                        h = h0 + i - TURN_LAG
                        if i >= TURN_LAG and h % 2 == 0:
                            act.wait_ge(probs_turned, h + 1)
                            if h >= 2:
                                act.wait_ge(head_out, h - 1)
                            for dst, src in turned_halves(mode, h):
                                ins = nc.scalar.activation(dst, src, ACT.Copy)
                            ins.then_inc(turned_copied[0], 1)
                        if i < len(spec):
                            s, h = s0 + i, h0 + i
                            act.wait_ge(negmax_ready, h + 1)
                            if h >= 3:
                                act.wait_ge(probs_turned, h - 2)
                            if mode == "window":
                                hh = spec[i][4]
                                nc.scalar.activation(sink_exp[:, h % HEADS_HELD, :], nmx[:, h % HEADS_HELD, :], ACT.Exp, bias=sinks[:, 0, hh:hh + 1])
                            for t in range(T):
                                m = head_cols(mode, t)
                                src = biased[:, h % 2, t, :] if mode == "near" else bank[s % 4][:, t * S:t * S + m]
                                ins = nc.scalar.activation(probs[:, h % 3, t, 0:m], src, ACT.Exp, bias=nmx[:, h % HEADS_HELD, t:t + 1],
                                                           scale=1.0 if mode == "near" else SCALE,
                                                           accum_out=sums[:, h % HEADS_HELD, t:t + 1])
                            ins.then_inc(scores_used, 1)

        @block.tensor
        def _(pe):
            def enter(banks):
                for b, used in banks:
                    if used:
                        pe.wait_ge(bank_free[b], used)

            for it in plan:
                kind = it["kind"]
                if kind == "turn_vectors":
                    pe.wait_ge(const_in, 32)
                    pe.wait_ge(vec_in, 16 * 7)
                    b, _ = it["banks"][0]
                    nc.tensor.transpose(bank[b][:, 0:N_VEC_A], vec_rows[0:N_VEC_A, 0, :], ident[0:N_VEC_A, 0:N_VEC_A])
                    nc.tensor.transpose(bank[b][:, N_VEC_A:N_VEC_A + N_VEC_B], vec_rows[0:N_VEC_B, 1, :],
                                        ident[0:N_VEC_B, 0:N_VEC_B]).then_inc(job_done, 1)

                elif kind == "ada_columns":
                    enter(it["banks"])
                    pe.wait_ge(ada_done, 2 * it["ada"])
                    b = it["banks"][0][0]
                    for i in range(2 * KD):
                        mm = nc.tensor.matmul(bank[b][:, i:i + 1], ada_sum[:, i // KD, (i % KD) * P:(i % KD + 1) * P],
                                              const("ones")[:, 0:1], start=True, stop=True)
                    mm.then_inc(job_done, 1)

                elif kind == "gate_row":
                    enter(it["banks"])
                    pe.wait_ge(ada_done, 24 * (it["s"] + 1))
                    for n, (b, _) in enumerate(it["banks"]):
                        mm = nc.tensor.matmul(bank[b][:, :], const("ones"), ada_sum[:, 2, n * 512:(n + 1) * 512], start=True, stop=True)
                    mm.then_inc(job_done, 1)

                elif kind == "turn_split":
                    enter(it["banks"])
                    if it["src"] == "x":
                        pe.wait_ge(x_in, 16)
                    if it["wait"] and it["src"] != "xhat":
                        pe.wait_ge(rows_ready, it["wait"])
                    if "updated" in it:
                        how, value = it["updated"]
                        if how == "x":
                            pe.wait_ge(x_ready, value)
                        else:
                            enter(value)
                    if it["src"] == "o":
                        pe.wait_ge(head_copied, it["heads"])
                    if it["src"][0] == "p":
                        pe.wait_ge(p_in[it["src"][1]], 16)
                    for t in range(T):
                        if it["src"] == "xhat":
                            pe.wait_ge(rows_ready, it["wait"] - T + t + 1)
                        for c in range(it["n"]):
                            b = it["banks"][c // 2][0]
                            o = (c % 2) * S + t * P
                            mm = nc.tensor.transpose(bank[b][:, o:o + P], source(it, t, it["a"] + c), ident)
                    mm.then_inc(job_done, 1)

                elif kind == "turn":
                    enter(it["banks"])
                    if it["shared"]:
                        pe.wait_ge(pool_rows, it["shared"])
                    if it["wait"]:
                        pe.wait_ge(rows_ready, it["wait"])
                    for b in range(4):
                        pe.wait_ge(bank_free[b], it["before"][b])
                    for c, col in enumerate(it["cols"]):
                        b = it["banks"][c // 2][0]
                        for t in range(T):
                            o = (c % 2) * S + t * P
                            mm = nc.tensor.transpose(bank[b][:, o:o + P], tok[:, t, col:col + P], ident)
                    mm.then_inc(job_done, 1)

                elif kind == "tokens":
                    n = it["tile"]
                    if it["enter"]:
                        enter(it["banks"])
                    pe.wait_ge(split_done, it["cut"])
                    pe.wait_ge(low_done, n + 1)
                    hi, lo = views(n)
                    if it["lhs"] == "ht":
                        a_hi, a_lo = ht_hi[:, :, :], ht_lo[:, :, :]
                    elif it["lhs"] == "plt":
                        a_hi, a_lo = plt_hi[:, :, :], plt_lo[:, :, :]
                    else:
                        a_hi, a_lo = hid_hi[:, it["lhs"][1], :, :], hid_lo[:, it["lhs"][1], :, :]
                    for t, (b, _) in enumerate(it["banks"]):
                        dst = bank[b][:, 0:it["width"]]
                        for k in range(it["kc"]):
                            rows = slice(t * P, (t + 1) * P)
                            c = it["off"] + k
                            nc.tensor.matmul(dst, a_hi[:, c, rows], lo[:, k, :], start=it["first"] and k == 0, stop=False)
                            nc.tensor.matmul(dst, a_hi[:, c, rows], hi[:, k, :], start=False, stop=False)
                            mm = nc.tensor.matmul(dst, a_lo[:, c, rows], hi[:, k, :], start=False,
                                                  stop=it["last"] and k == it["kc"] - 1)
                        mm.then_inc(tile_done if t else half_done, 1)

                elif kind == "hidden":
                    n = it["tile"]
                    b, used = it["banks"][it["half"]]
                    enter([(b, used)])
                    pe.wait_ge(split_done, it["cut"][0])
                    pe.wait_ge(low_done, n + 1)
                    hi, lo = views(n)
                    for c in range(2):
                        dst = bank[b][:, c * S:(c + 1) * S]
                        for k in range(KD):
                            if c == 0 and k == 4:
                                pe.wait_ge(split_done, it["cut"][1])
                            cols = slice(c * P, (c + 1) * P)
                            nc.tensor.matmul(dst, lo[:, k, cols], ht_hi[:, k, :], start=k == 0, stop=False)
                            nc.tensor.matmul(dst, hi[:, k, cols], ht_lo[:, k, :], start=False, stop=False)
                            mm = nc.tensor.matmul(dst, hi[:, k, cols], ht_hi[:, k, :], start=False, stop=k == KD - 1)
                    mm.then_inc(tile_done, 1)

                elif kind == "heads":
                    mode, spec, s0, h0 = it["mode"], it["spec"], it["s0"], it["h0"]
                    enter([(b, it["uses"][b]) for b in range(4)])
                    if mode == "sparse":
                        pe.wait_ge(mask_ready, 1)
                    last_lag = 0 if mode == "index" else OUT_LAG
                    for i in range(len(spec) + last_lag):
                        if i < len(spec):
                            s = s0 + i
                            qc, half, kc, _, _ = spec[i]
                            part = slice(half * HD, (half + 1) * HD)
                            if s >= 4:
                                pe.wait_ge(scores_used, s - 3)
                            for t in range(T):
                                m = head_cols(mode, t)
                                masks = {"causal": [(t * P, maskb[:, 2, :])],
                                         "window": [(0, maskb[:, 2 - t:3, :].rearrange("p a n -> p (a n)"))],
                                         "sparse": [(0, smask[:, t, 0:m])]}.get(mode, [])
                                mm = nc.tensor.matmul(bank[s % 4][:, t * S:t * S + m], qkt[part, qc, t * P:(t + 1) * P],
                                                      qkt[part, kc, 0:m], start=True, stop=not masks)
                                for o, mask in masks:
                                    mm = nc.tensor.matmul(bank[s % 4][:, t * S + o:t * S + m], maskb[:, 0, :], mask,
                                                          start=False, stop=True)
                            mm.then_inc(scores_ready, 1)
                        if mode == "index":
                            continue
                        if i == TURN_LAG:
                            enter([(b, it["uses"][b]) for b in range(4, 8)])
                        if TURN_LAG <= i < len(spec) + TURN_LAG:
                            h = h0 + i - TURN_LAG
                            pe.wait_ge(scores_used, s0 + i - TURN_LAG + 1)
                            if h >= 2:
                                pe.wait_ge(turned_copied[h % 2], h // 2)
                            for t in range(T):
                                for k in range(head_cols(mode, t) // P):
                                    mm = nc.tensor.transpose(bank[4 + h % 2][:, k * S + t * P:k * S + (t + 1) * P],
                                                             probs[:, h % 3, t, k * P:(k + 1) * P], ident)
                            mm.then_inc(probs_turned, 1)
                        if i >= OUT_LAG:
                            h = h0 + i - OUT_LAG
                            v = spec[i - OUT_LAG][3]
                            pe.wait_ge(turned_copied[h % 2], h // 2 + 1)
                            if h >= 2:
                                pe.wait_ge(head_copied, h - 1)
                            for t in range(T):
                                o = t * HD
                                nk = head_cols(mode, t) // P
                                for k in range(nk):
                                    mm = nc.tensor.matmul(bank[6 + h % 2][:, o:o + HD], probs_t[:, h % 2, k, t * P:(t + 1) * P],
                                                          tok[:, k, v:v + HD], start=k == 0, stop=k == nk - 1)
                            mm.then_inc(head_out, 1)

        @block.vector
        def _(dve):
            steps = [0]

            def link(ins):
                steps[0] += 1
                ins.then_inc(dve_step, 1)
                dve.wait_ge(dve_step, steps[0])

            def columns(it):
                s = it["s"]
                b, used = it["banks"][0]
                dve.wait_ge(job_done, it["job"])
                bias = vec[:, 3 * KD * s:3 * KD * s + 2 * KD]
                nc.vector.tensor_tensor(mod[:, :], bank[b][:, 0:2 * KD], bias, ALU.add).then_inc(bank_free[b], 1)
                dve.wait_ge(bank_free[b], used + 1)
                shift, scale = mod[:, 0:KD], mod[:, KD:2 * KD]
                if s == 0:
                    link(nc.vector.tensor_scalar(aff[:, 0, :], scale, 1.0, None, ALU.add))
                    nc.vector.tensor_copy(aff[:, 1, :], shift).then_inc(affine_ready, 1)
                else:
                    g = vec[:, N_VEC_A + KD * (s - 1):N_VEC_A + KD * s]
                    lb = vec[:, N_VEC_A + 32 + KD * (s - 1):N_VEC_A + 32 + KD * s]
                    link(nc.vector.scalar_tensor_tensor(aff[:, 0, :], scale, 1.0, g, ALU.add, ALU.mult))
                    link(nc.vector.scalar_tensor_tensor(aff[:, 1, :], scale, 1.0, lb, ALU.add, ALU.mult))
                    nc.vector.tensor_tensor(aff[:, 1, :], aff[:, 1, :], shift, ALU.add).then_inc(affine_ready, 1)
                dve.wait_ge(affine_ready, s + 1)

            lows = [0]

            def split_low(until):
                for n in range(lows[0], min(until + 1, len(split))):
                    weight_low(n)
                lows[0] = max(lows[0], until + 1)

            def weight_low(n):
                hi, lo = split_parts(n)
                dve.wait_ge(high_done, n + 1)
                nc.vector.tensor_tensor(lo, raw_tile(split[n]), hi.bitcast(F32), ALU.subtract).then_inc(low_done, 1)

            cuts = [0]

            def low_part(lo, v, hi):
                nc.vector.tensor_tensor(lo, v, hi.bitcast(F32), ALU.subtract).then_inc(split_done, 1)
                cuts[0] += 1

            def rsqrt(v, n):
                y, a, b = rstd[:, 0:n], small[:, 1, 0:n], small[:, 2, 0:n]
                link(nc.vector.tensor_scalar(bits[:, 0:n], v.bitcast(U32), 1, None, ALU.logical_shift_right))
                link(nc.vector.tensor_scalar(y.bitcast(U32), bits[:, 0:n], -1.0, RSQRT_MAGIC, ALU.mult, ALU.add))
                for _ in range(3):
                    link(nc.vector.tensor_tensor(a, y, y, ALU.mult))
                    link(nc.vector.scalar_tensor_tensor(b, a, -0.5, v, ALU.mult, ALU.mult))
                    link(nc.vector.scalar_tensor_tensor(y, b, 1.5, y, ALU.add, ALU.mult))

            def rope(it, cos, sin, groups, half, tiles=range(T)):
                for n, (col, nh, dup) in enumerate(it["what"]):
                    for t in tiles:
                        w = nh * HD
                        q = tok[:, t, col:col + w]
                        ta, tb = tmp_a[:, 0:w], tmp_b[:, 0:w]
                        ins = rope_products(nc.vector, q, ta, tb, nh, cos(t), sin(t), groups, half)
                        link(ins)
                        if dup is None:
                            ins = nc.vector.tensor_tensor(q, ta, tb, ALU.add)
                        else:
                            for r in range(2):
                                o = tok[:, t, dup:dup + 2 * w].rearrange("p (h r d) -> p h r d", h=nh, r=2)[:, :, r, :]
                                ins = nc.vector.tensor_tensor(o, ta.rearrange("p (h d) -> p h d", h=nh),
                                                              tb.rearrange("p (h d) -> p h d", h=nh), ALU.add)
                        if n == len(it["what"]) - 1 and t == tiles[-1]:
                            ins.then_inc(rows_ready, 1)
                            dve.wait_ge(rows_ready, it["rows"])
                        else:
                            link(ins)

            def projected(it):
                for b in range(4):
                    dve.wait_ge(bank_free[b], it["uses"][b])

            turned = next(i for i in plan if i["kind"] == "turn_vectors")
            dve.wait_ge(job_done, turned["job"])
            nv = N_VEC_A + N_VEC_B
            b0 = turned["banks"][0][0]
            nc.vector.tensor_copy(vec[:, :], bank[b0][:, 0:nv]).then_inc(bank_free[b0], 1)
            dve.wait_ge(bank_free[b0], 1)
            cvec = vec[:, VEC_A["c"]:VEC_A["c"] + KD]
            link(nc.vector.tensor_scalar(cs[:, 2, :], cvec, 0.5, None, ALU.mult))
            dve.wait_ge(tanh_ready, 1)
            nc.vector.scalar_tensor_tensor(cs[:, 0, :], cs[:, 1, :], 1.0, cs[:, 2, :], ALU.add, ALU.mult).then_inc(silu_ready, 1)
            for n in range(8):
                ada_products(dve, nc.vector, n)
            for m, name in enumerate(("ident", "window", "causal")):
                link(nc.vector.tensor_copy(maskb[:, m, :], const(name)))
            link(nc.vector.tensor_copy(pos_f[:, :], pos_i[:, :]))
            for t in range(T):
                link(nc.vector.tensor_scalar(angle[:, 0, t, :], const("invf"), pos_f[:, t:t + 1], None, ALU.mult))
            for j, turn in ((1, 0.0), (2, 0.25)):
                k = tmp_a[:, 0:T * HD]
                a0 = angle[:, 0, :, :].rearrange("p t d -> p (t d)")
                r = angle[:, j, :, :].rearrange("p t d -> p (t d)")
                link(nc.vector.tensor_scalar(k, a0, float(1 / TWO_PI), turn, ALU.mult, ALU.add))
                link(nc.vector.tensor_scalar(k, k, ROUND, -ROUND, ALU.add, ALU.add))
                link(nc.vector.scalar_tensor_tensor(r, k, -C1, a0, ALU.mult, ALU.add))
                link(nc.vector.scalar_tensor_tensor(r, k, -C2, r, ALU.mult, ALU.add))
                link(nc.vector.scalar_tensor_tensor(r, k, -C3, r, ALU.mult, ALU.add))
                link(nc.vector.tensor_scalar(r, r, float(turn * TWO_PI), 3.1415925, ALU.add, ALU.min))
                ins = nc.vector.tensor_scalar(r, r, -3.1415925, None, ALU.max)
                if j == 2:
                    ins.then_inc(angle_ready, 1)
                else:
                    link(ins)
            split_low(0)
            columns(next(i for i in plan if i["kind"] == "ada_columns"))

            for it in plan:
                kind = it["kind"]
                if kind == "ada_columns":
                    if it["s"]:
                        columns(it)

                elif kind == "rope_tables":
                    dve.wait_ge(sin_ready, 2)
                    for t in range(T):
                        link(nc.vector.tensor_tensor(sinr[:, t, :], sinr[:, t, :], const("sign"), ALU.mult))
                    dve.wait_ge(misc_in, 48)
                    link(nc.vector.tensor_scalar(sinks[:, 1, :], sinks[:, 0, :], -1.0, None, ALU.mult))

                elif kind == "gate_row":
                    dve.wait_ge(gate_in, 16 * (it["s"] + 1))
                    dve.wait_ge(job_done, it["job"])
                    for n, (b, used) in enumerate(it["banks"]):
                        row = gate_row[:, n * 512:(n + 1) * 512]
                        nc.vector.scalar_tensor_tensor(row, bank[b][:, :], 1.0, row, ALU.add, ALU.add).then_inc(bank_free[b], 1)
                        dve.wait_ge(bank_free[b], used + 1)

                    if it["s"] == N_SUB - 1:
                        ng = vec[:, N_VEC_A + VEC_B["norm_g"]:N_VEC_A + VEC_B["norm_g"] + KD]
                        for i, first in enumerate((KD * it["s"], 32 + KD * it["s"])):
                            ins = nc.vector.tensor_tensor(aff[:, i, :], vec[:, N_VEC_A + first:N_VEC_A + first + KD], ng, ALU.mult)
                            if i == 0:
                                link(ins)
                        ins.then_inc(affine_ready, 1)
                        dve.wait_ge(affine_ready, N_SUB + 1)

                elif kind == "turn_split":
                    dve.wait_ge(job_done, it["job"])
                    hi_all, lo_all = parts(it)
                    if len(it["banks"]) > 1:
                        b, used = it["banks"][1]
                        c0 = it["a"] + 2
                        hi, lo = hi_all[:, c0:c0 + 2, :], lo_all[:, c0:c0 + 2, :]
                        for c in range(2):
                            k = it["a"] + 2 + c
                            dst, ps = full[:, b % 4, c * S:(c + 1) * S], bank[b][:, c * S:(c + 1) * S]
                            if it["affine"] is None:
                                ins = nc.vector.tensor_copy(dst, ps)
                            elif it["affine"][0] == "affine":
                                ins = nc.vector.tensor_scalar(dst, ps, aff[:, 0, k:k + 1], aff[:, 1, k:k + 1], ALU.mult, ALU.add)
                            else:
                                v = N_VEC_A + it["affine"][1] + k
                                ins = nc.vector.tensor_scalar(dst, ps, vec[:, v:v + 1], None, ALU.mult)
                        ins.then_inc(bank_free[b], 1)
                        dve.wait_ge(bank_free[b], used + 1)
                        v2 = full[:, b % 4, :].rearrange("p (c s) -> p c s", c=2)
                        link(nc.vector.tensor_copy(hi, v2))
                        low_part(lo, v2, hi)
                    b, _ = it["banks"][0]
                    m = min(2, it["n"])
                    c0 = it["a"]
                    dve.wait_ge(high_copied, it["high"])
                    low_part(lo_all[:, c0:c0 + m, :], full[:, b % 4, 0:m * S].rearrange("p (c s) -> p c s", c=m), hi_all[:, c0:c0 + m, :])

                elif kind == "turn":
                    b, _ = it["banks"][1]
                    dve.wait_ge(job_done, it["job"])
                    nc.vector.tensor_copy(qkt[:, it["dst"] + 2:it["dst"] + 4, :],
                                          bank[b][:, :].rearrange("p (c s) -> p c s", c=2)).then_inc(bank_free[b], 1)

                elif kind in ("tokens", "hidden"):
                    n = it["tile"]
                    split_low(it["ahead"])
                    end = it.get("end")
                    if end is None:
                        continue
                    if end == "hidden":
                        b, used = it["banks"][1]
                        dve.wait_ge(tile_done, n + 1)
                        v2 = full[:, b, :].rearrange("p (c s) -> p c s", c=2)
                        link(nc.vector.tensor_scalar(full[:, b, :], bank[b][:, :], 0.0, None, ALU.max))
                        nc.vector.tensor_tensor(full[:, b, :], full[:, b, :], full[:, b, :], ALU.mult).then_inc(bank_free[b], 1)
                        dve.wait_ge(bank_free[b], used + 1)
                        hi = hid_hi[:, it["buf"], it["c0"] + 2:it["c0"] + 4, :]
                        link(nc.vector.tensor_copy(hi, v2))
                        low_part(hid_lo[:, it["buf"], it["c0"] + 2:it["c0"] + 4, :], v2, hi)
                        b, _ = it["banks"][0]
                        dve.wait_ge(high_copied, it["high"])
                        low_part(hid_lo[:, it["buf"], it["c0"]:it["c0"] + 2, :],
                                 full[:, b, :].rearrange("p (c s) -> p c s", c=2),
                                 hid_hi[:, it["buf"], it["c0"]:it["c0"] + 2, :])
                    elif end[0] == "y_ln":
                        if end[2]:
                            dve.wait_ge(resid_done, T * end[2])
                        cols = slice(end[1] * 512, (end[1] + 1) * 512)
                        for t, (b, used) in enumerate(it["banks"]):
                            came(dve, it, t)
                            nc.vector.tensor_tensor(tmp_a[:, :], bank[b][:, :], gate_row[:, cols], ALU.mult).then_inc(bank_free[b], 1)
                            dve.wait_ge(bank_free[b], used + 1)
                            link(nc.vector.scalar_tensor_tensor(u[:, t, cols], x[:, t, cols], ALPHA, tmp_a[:, :], ALU.mult, ALU.add))
                            link(nc.vector.bn_stats(stats[:, t, end[1], :], u[:, t, cols]))
                    elif end[0] == "silu":
                        for t, (b, used) in enumerate(it["banks"]):
                            dve.wait_ge(bank_free[b], used + 1)
                            g = tok[:, t, end[1]:end[1] + 512]
                            link(nc.vector.scalar_tensor_tensor(g, full[:, 2 * end[4] + t, :], 1.0, g, ALU.add, ALU.mult))
                    elif end[0] == "y_rms":
                        cols = slice(end[1] * 512, (end[1] + 1) * 512)
                        for t, (b, used) in enumerate(it["banks"]):
                            came(dve, it, t)
                            nc.vector.tensor_tensor(x[:, t, cols], bank[b][:, :], x[:, t, cols], ALU.add).then_inc(bank_free[b], 1)
                            dve.wait_ge(bank_free[b], used + 1)
                    elif end[0] == "ple":
                        cols = slice(end[1] * 512, (end[1] + 1) * 512)
                        for t, (b, used) in enumerate(it["banks"]):
                            dve.wait_ge(bank_free[b], used + 1)
                            link(nc.vector.scalar_tensor_tensor(tmp_a[:, :], full[:, 2 * end[1] + t, :], 1.0, tok[:, t, cols], ALU.add, ALU.mult))
                            nc.vector.tensor_tensor(x[:, t, cols], x[:, t, cols], tmp_a[:, :], ALU.add).then_inc(x_ready, 1)
                            dve.wait_ge(x_ready, it["x"] - T + t + 1)

                elif kind == "ln":
                    for t in range(T):
                        link(nc.vector.bn_aggr(meanvar[:, t, :], stats[:, t, :, :]))
                    link(nc.vector.tensor_scalar(small[:, 0, 0:T], meanvar[:, :, 1], LN_EPS, None, ALU.add))
                    rsqrt(small[:, 0, 0:T], T)
                    for t in range(T):
                        nc.vector.tensor_scalar(u[:, t, :], u[:, t, :], meanvar[:, t, 0:1], rstd[:, t:t + 1],
                                                ALU.subtract, ALU.mult).then_inc(rows_ready, 1)
                        dve.wait_ge(rows_ready, it["rows"] - T + t + 1)

                elif kind == "resid":
                    dve.wait_ge(row_in, 32 * (it["s"] + 1))
                    link(nc.vector.tensor_tensor(x[:, 0, :], u[:, 0, :], g_row[:, :], ALU.mult))
                    nc.vector.tensor_tensor(x[:, 0, :], x[:, 0, :], b_row[:, :], ALU.add).then_inc(first_rows, 1)
                    dve.wait_ge(first_rows, 1)

                elif kind in ("rms", "final"):
                    dve.wait_ge(ssq_ready, it["ssq"])
                    v = small[:, 0, 0:T]
                    link(nc.vector.tensor_tensor(v, ssq[:, :, 0], ssq[:, :, 1], ALU.add))
                    link(nc.vector.tensor_scalar(v, v, 1.0 / D, RMS_EPS, ALU.mult, ALU.add))
                    rsqrt(v, T)
                    if kind == "rms":
                        link(nc.vector.tensor_copy(rms[:, it["i"], 0, :], rstd[:, 0:T]))
                        nc.vector.tensor_scalar(rms[:, it["i"], 1, :], rstd[:, 0:T], 0.5, None, ALU.mult).then_inc(rms_ready, 1)
                        dve.wait_ge(rms_ready, it["i"] + 1)
                        continue
                    dve.wait_ge(final_in, 16)
                    for t in range(T):
                        nc.vector.scalar_tensor_tensor(u[:, t, :], x[:, t, :], rstd[:, t:t + 1], g_final[:, :], ALU.mult, ALU.mult)\
                            .then_inc(rows_ready, 1)
                        dve.wait_ge(rows_ready, it["rows"] - T + t + 1)

                elif kind == "low_rank":
                    projected(it)
                    for t in range(T):
                        cq = tok[:, t, 768:1024]
                        link(nc.vector.tensor_tensor(tmp_a[:, 0:256], cq, cq, ALU.mult))
                        link(nc.vector.tensor_reduce(small[:, 0, t:t + 1], tmp_a[:, 0:256], AX, ALU.add))
                    v = small[:, 0, 0:T]
                    link(nc.vector.tensor_scalar(v, v, 1.0 / 256, RMS_EPS, ALU.mult, ALU.add))
                    rsqrt(v, T)
                    for t in range(T):
                        ins = nc.vector.tensor_scalar(tok[:, t, 768:1024], tok[:, t, 768:1024], rstd[:, t:t + 1], None, ALU.mult)
                        if t == T - 1:
                            ins.then_inc(rows_ready, 1)
                            dve.wait_ge(rows_ready, it["rows"])

                elif kind == "rope":
                    projected(it)
                    rope(it, lambda t: cosr[:, t, :], lambda t: sinr[:, t, :], 1, HD // 2)

                elif kind == "qk_rope":
                    projected(it)
                    g = 0 if it["gain"] == "q" else 1
                    col, nh, _ = it["what"][0]
                    w = nh * HD
                    for t in range(T):
                        q = tok[:, t, col:col + w]
                        link(nc.vector.tensor_tensor(tmp_a[:, 0:w], q, q, ALU.mult))
                        link(nc.vector.tensor_reduce(small[:, 0, t * nh:(t + 1) * nh], tmp_a[:, 0:w].rearrange("p (h d) -> p h d", h=nh), AX, ALU.add))
                    v = small[:, 0, 0:T * nh]
                    link(nc.vector.tensor_scalar(v, v, 1.0 / HD, RMS_EPS, ALU.mult, ALU.add))
                    rsqrt(v, T * nh)
                    for t in range(T):
                        q = tok[:, t, col:col + w].rearrange("p (h d) -> p h d", h=nh)
                        ins = nc.vector.tensor_tensor(q, q, rstd[:, t * nh:(t + 1) * nh].unsqueeze(2).broadcast_to([P, nh, HD]), ALU.mult)
                        if t == 0 or not it["shared"]:
                            link(ins)
                    if it["shared"]:
                        ins.then_inc(scaled, 1)
                        dve.wait_ge(scaled, it["shared"])
                    rope(it, lambda t: ax[:, g, 0, t, :], lambda t: ax[:, g, 1, t, :], 2, HD // 4,
                         range(1) if it["shared"] else range(T))

                elif kind == "axial_tables":
                    for g in range(2):
                        for t in range(T):
                            cs_t = const("axcos")[:, t * HD:(t + 1) * HD]
                            sn_t = const("axsin")[:, t * HD:(t + 1) * HD].rearrange("p (g a d) -> p g a d", g=2, a=2)
                            gv = gain[:, g, :].rearrange("p (g a d) -> p g a d", g=2, a=2)
                            dst = ax[:, g, 1, t, :].rearrange("p (g a d) -> p g a d", g=2, a=2)
                            link(nc.vector.tensor_tensor(ax[:, g, 0, t, :], cs_t, gain[:, g, :], ALU.mult))
                            for a in range(2):
                                link(nc.vector.tensor_tensor(dst[:, :, a, :], sn_t[:, :, a, :], gv[:, :, 1 - a, :], ALU.mult))

                elif kind == "bias_table":
                    part = it["part"]
                    dve.wait_ge(resid_done, T * 3 + 1)
                    dve.wait_ge(bias_in[part], 32)
                    dst = near_bias[:, 8 * part:8 * part + 8, :].rearrange("p h (r k) -> p (h r) k", k=GRID)
                    nc.vector.tensor_tensor(dst, near_rev[:, :, ::-1], const("near").unsqueeze(1).broadcast_to([P, 48, GRID]), ALU.add)\
                        .then_inc(rows_ready, 1)
                    dve.wait_ge(rows_ready, it["rows"])

                elif kind == "heads":
                    mode, spec, s0, h0 = it["mode"], it["spec"], it["s0"], it["h0"]
                    if mode == "causal":
                        dve.wait_ge(resid_done, 2 * T)
                    if mode == "index":
                        link(nc.vector.tensor_scalar(iw[:, :, :], tok[:, :, 1216:1224], IW_SCALE, None, ALU.mult))
                        for i in range(len(spec)):
                            dve.wait_ge(scores_used, s0 + i + 1)
                            for t in range(T):
                                m = head_cols(mode, t)
                                src, w = biased[:, i % 2, t, 0:m], iw[:, t, i:i + 1]
                                if i == 0:
                                    ins = nc.vector.tensor_scalar(score[:, t, 0:m], src, w, None, ALU.mult)
                                else:
                                    ins = nc.vector.scalar_tensor_tensor(score[:, t, 0:m], src, w, score[:, t, 0:m], ALU.mult, ALU.add)
                            ins.then_inc(index_used, 1)
                            dve.wait_ge(index_used, i + 1)
                        for t in range(T):
                            own = score[:, t, t * P:(t + 1) * P]
                            link(nc.vector.tensor_tensor(own, own, const("causal"), ALU.add))
                        continue
                    for i in range(len(spec) + OUT_LAG):
                        h = h0 + i - TURN_LAG
                        if TURN_LAG <= i < len(spec) + TURN_LAG and h % 2:
                            dve.wait_ge(probs_turned, h + 1)
                            if h >= 2:
                                dve.wait_ge(head_out, h - 1)
                            for dst, src in turned_halves(mode, h):
                                ins = nc.vector.tensor_copy(dst, src)
                            ins.then_inc(turned_copied[1], 1)
                        if i < len(spec):
                            s, h = s0 + i, h0 + i
                            dve.wait_ge(scores_ready, s + 1)
                            if mode == "near":
                                if i >= 2:
                                    dve.wait_ge(scores_used, s - 1)
                                for t in range(T):
                                    o = (2 - 2 * t) * GRID
                                    ins = nc.vector.scalar_tensor_tensor(biased[:, h % 2, t, :], bank[s % 4][:, t * S:(t + 1) * S], SCALE,
                                                                         near_bias[:, spec[i][4], o:o + S], ALU.mult, ALU.add)
                                link(ins)
                                link(nc.vector.tensor_reduce(mx[:, h % HEADS_HELD, :], biased[:, h % 2, :, :], AX, ALU.max))
                            elif mode == "full":
                                link(nc.vector.tensor_reduce(mx[:, h % HEADS_HELD, :], bank[s % 4][:, :].rearrange("p (t k) -> p t k", t=T), AX, ALU.max))
                            else:
                                for t in range(T):
                                    ins = nc.vector.tensor_reduce(mx[:, h % HEADS_HELD, t:t + 1], bank[s % 4][:, t * S:t * S + head_cols(mode, t)], AX, ALU.max)
                                link(ins)
                            if mode == "window":
                                hh = spec[i][4]
                                nc.vector.tensor_scalar(nmx[:, h % HEADS_HELD, :], mx[:, h % HEADS_HELD, :], -SCALE, sinks[:, 1, hh:hh + 1],
                                                        ALU.mult, ALU.min).then_inc(negmax_ready, 1)
                            else:
                                nc.vector.tensor_scalar(nmx[:, h % HEADS_HELD, :], mx[:, h % HEADS_HELD, :], -1.0 if mode == "near" else -SCALE, None,
                                                        ALU.mult).then_inc(negmax_ready, 1)
                        if i >= OUT_LAG:
                            h = h0 + i - OUT_LAG
                            hh = spec[i - OUT_LAG][4]
                            dve.wait_ge(scores_used, s0 + i - OUT_LAG + 1)
                            if mode == "window":
                                link(nc.vector.tensor_tensor(sums[:, h % HEADS_HELD, :], sums[:, h % HEADS_HELD, :], sink_exp[:, h % HEADS_HELD, :], ALU.add))
                            link(nc.vector.reciprocal(rs[:, h % HEADS_HELD, :], sums[:, h % HEADS_HELD, :]))
                            dve.wait_ge(head_out, h + 1)
                            ps = bank[6 + h % 2][:, 0:P].rearrange("p (t d) -> p t d", t=T)
                            if "gate" in it:
                                for t in range(T):
                                    gc = it["gate"] + hh * HD
                                    ins = nc.vector.scalar_tensor_tensor(u[:, t, hh * HD:(hh + 1) * HD], ps[:, t, :], rs[:, h % HEADS_HELD, t:t + 1],
                                                                         tok[:, t, gc:gc + HD], ALU.mult, ALU.mult)
                            else:
                                ins = nc.vector.tensor_tensor(u[:, :, hh * HD:(hh + 1) * HD], ps,
                                                              rs[:, h % HEADS_HELD, :].unsqueeze(2).broadcast_to([P, T, HD]), ALU.mult)
                            ins.then_inc(head_copied, 1)
                        if mode == "window" and i < 8:
                            for r in (2 * i, 2 * i + 1):
                                t = r // 8
                                sc = score[:, t, 0:P * (t + 1)]
                                link(nc.vector.max(top8[:, :], sc))
                                link(nc.vector.match_replace(sc, top8[:, :], sc, PICKED))
                            if i == 7:
                                for t in range(T):
                                    m = P * (t + 1)
                                    link(nc.vector.tensor_scalar(smask[:, t, 0:m], score[:, t, 0:m], PICKED / 2, MASKED, ALU.is_gt, ALU.mult))
                                    own = smask[:, t, t * P:m]
                                    ins = nc.vector.tensor_tensor(own, own, maskb[:, 2, :], ALU.min)
                                    if t == 0:
                                        link(ins)
                                ins.then_inc(mask_ready, 1)


_INS = ["x", "c", "positions", "ab_w_in", "ab_q_norm", "ab_w_uq", "ab_w_uiq", "ab_sinks", "ab_w_out", "c_w_in", "c_w_out",
        "ada_w", "ada_b", "ln_g", "ln_b", "mlp_w1", "mlp_w2", "p_2", "norm_g_2", "a_w_in_2", "a_rpb_2", "a_w_out_2",
        "b_w_in_2", "b_q_norm_2", "b_k_norm_2", "b_w_out_2", "ple_norm_g_2", "ple_w_gate_2", "ple_w_proj_2", "final_norm_g_2"]


def kernel(**inputs):
    import concourse.bacc as bacc
    from concourse.bass_utils import run_bass_kernel_spmd

    nc = bacc.Bacc("TRN2", target_bir_lowering=False, num_devices=1)
    arrays, rows = {}, {}
    for name in _INS:
        a = np.ascontiguousarray(inputs[name])
        arrays[f"in_{name}"] = a
        rows[name] = nc.dram_tensor(f"in_{name}", a.shape, mybir.dt.from_np(a.dtype), kind="ExternalInput").ap()
    arrays["in_consts"] = constants()
    rows["consts"] = nc.dram_tensor("in_consts", (P, N_CONST), F32, kind="ExternalInput").ap()
    out = nc.dram_tensor("out_0", (1, S, D), F32, kind="ExternalOutput").ap()
    toeplitz = nc.dram_tensor("toeplitz", (2, 16, 6, 128), F32, kind="Internal")
    block_kernel(nc, rows, out, toeplitz)
    r = run_bass_kernel_spmd(nc, [arrays], core_ids=[0])
    return r.results[0]["out_0"]
```
